# Optimizing a Trainium2 kernel written in Bass

```python
import functools
import jax, jax.numpy as jnp
from jax import lax
import numpy as np
import math

D_MODEL = 1024
BATCH = 1
SEQ = 256
DEPTH = 2

CHUNK = 64
Q_BLOCK = 128
MLA_HEADS = 8
MLA_NOPE = 64
MLA_ROPE = 32
MLA_V = 64
Q_LORA = 384
KV_LORA = 256
ROPE_THETA = 10000.0
SB_HEADS = 8
SB_DIM = 64
C_HEADS = 16
C_DIM = 64
LEFT_CHUNKS = 8
BAND = (LEFT_CHUNKS + 1) * CHUNK
REL_CLIP = 256
D_FF = -(-8 * D_MODEL // (3 * 256)) * 256
EVEN_IN = Q_LORA + KV_LORA + MLA_ROPE + 3 * SB_HEADS * SB_DIM
MIX_EVEN = MLA_HEADS * MLA_V + SB_HEADS * SB_DIM
MIX_ODD = C_HEADS * C_DIM
N_EVEN = (DEPTH + 1) // 2
N_ODD = DEPTH // 2
RMS_EPS = 1e-6


def rms_norm(x, g):
    x32 = x.astype(jnp.float32)
    y = x32 * lax.rsqrt(jnp.mean(x32 * x32, axis=-1, keepdims=True) + RMS_EPS)
    return (y * g.astype(jnp.float32)).astype(x.dtype)

def rope_tables(seq, dim):
    pos = jnp.arange(seq, dtype=jnp.float32)
    inv_freq = ROPE_THETA ** (-jnp.arange(0, dim, 2, dtype=jnp.float32) / dim)
    ang = pos[:, None] * inv_freq[None, :]
    return jnp.cos(ang), jnp.sin(ang)

def apply_rope(x, cos, sin):
    half = x.shape[-1] // 2
    c, s = cos.astype(x.dtype), sin.astype(x.dtype)
    x1, x2 = x[..., :half], x[..., half:]
    return jnp.concatenate([x1 * c - x2 * s, x2 * c + x1 * s], axis=-1)

def swiglu(u, w_gate, w_up, w_down):
    return (jax.nn.silu(u @ w_gate) * (u @ w_up)) @ w_down

def mla_stick_breaking_mixer(u, w_in, g_cq, w_uq, g_ckv, w_ukv, w_out):
    bsz, seq, _ = u.shape
    proj = u @ w_in
    o1 = Q_LORA
    o2 = o1 + KV_LORA
    o3 = o2 + MLA_ROPE
    nb = SB_HEADS * SB_DIM
    c_q, c_kv, k_r = proj[..., :o1], proj[..., o1:o2], proj[..., o2:o3]
    q_b = proj[..., o3:o3 + nb].reshape(bsz, seq, SB_HEADS, SB_DIM)
    k_b = proj[..., o3 + nb:o3 + 2 * nb].reshape(bsz, seq, SB_HEADS, SB_DIM)
    v_b = proj[..., o3 + 2 * nb:].reshape(bsz, seq, SB_HEADS, SB_DIM)

    cos, sin = rope_tables(seq, MLA_ROPE)
    q_a = (rms_norm(c_q, g_cq) @ w_uq).reshape(bsz, seq, MLA_HEADS, MLA_NOPE + MLA_ROPE)
    q_a = jnp.concatenate([q_a[..., :MLA_NOPE],
                           apply_rope(q_a[..., MLA_NOPE:], cos[:, None, :], sin[:, None, :])], axis=-1)
    kv = (rms_norm(c_kv, g_ckv) @ w_ukv).reshape(bsz, seq, MLA_HEADS, MLA_NOPE + MLA_V)
    k_rope = apply_rope(k_r, cos, sin)
    k_a = jnp.concatenate([kv[..., :MLA_NOPE],
                           jnp.broadcast_to(k_rope[:, :, None, :], (bsz, seq, MLA_HEADS, MLA_ROPE))], axis=-1)
    v_a = kv[..., MLA_NOPE:]
    scale_a = (MLA_NOPE + MLA_ROPE) ** -0.5
    scale_b = SB_DIM ** -0.5

    outs_a, outs_b = [], []
    for blk in range(seq // Q_BLOCK):
        t0 = blk * Q_BLOCK
        kend = t0 + Q_BLOCK
        t_pos = t0 + jnp.arange(Q_BLOCK)[:, None]
        s_pos = jnp.arange(kend)[None, :]
        s_a = jnp.einsum('bqhd,bkhd->bhqk', q_a[:, t0:kend], k_a[:, :kend]).astype(jnp.float32) * scale_a
        chunk_ok = (s_pos // CHUNK) <= (t_pos // CHUNK)
        p_a = jax.nn.softmax(jnp.where(chunk_ok, s_a, -jnp.inf), axis=-1)
        outs_a.append(jnp.einsum('bhqk,bkhd->bqhd', p_a.astype(v_a.dtype), v_a[:, :kend]))
        z = jnp.einsum('bqhd,bkhd->bhqk', q_b[:, t0:kend], k_b[:, :kend]).astype(jnp.float32) * scale_b
        before = s_pos < t_pos
        log_keep = jnp.where(before, jax.nn.log_sigmoid(-z), 0.0)
        log_between = lax.cumsum(log_keep, axis=3, reverse=True) - log_keep
        w_b = jnp.where(before, jnp.exp(jax.nn.log_sigmoid(z) + log_between), 0.0)
        outs_b.append(jnp.einsum('bhqk,bkhd->bqhd', w_b.astype(v_b.dtype), v_b[:, :kend]))

    o_a = jnp.concatenate(outs_a, axis=1).reshape(bsz, seq, MLA_HEADS * MLA_V)
    o_b = jnp.concatenate(outs_b, axis=1).reshape(bsz, seq, SB_HEADS * SB_DIM)
    return jnp.concatenate([o_a, o_b], axis=-1) @ w_out

def chunk_band_mixer(u, w_qkv, rel_bias, w_out):
    bsz, seq, _ = u.shape
    n_chunks = seq // CHUNK
    qkv = (u @ w_qkv).reshape(bsz, n_chunks, CHUNK, 3, C_HEADS, C_DIM)
    q, k, v = qkv[:, :, :, 0], qkv[:, :, :, 1], qkv[:, :, :, 2]
    pad = ((0, 0), (LEFT_CHUNKS, 0), (0, 0), (0, 0), (0, 0))
    k_p = jnp.pad(k, pad)
    v_p = jnp.pad(v, pad)
    scores = jnp.concatenate(
        [jnp.einsum('bnqhd,bnkhd->bnhqk', q, k_p[:, i:i + n_chunks]) for i in range(LEFT_CHUNKS + 1)],
        axis=-1).astype(jnp.float32) * (C_DIM ** -0.5)
    q_in = jnp.arange(CHUNK)[:, None]
    j = jnp.arange(BAND)[None, :]
    rel = (LEFT_CHUNKS - j // CHUNK) * CHUNK + q_in - j % CHUNK
    bias = rel_bias[:, jnp.clip(rel, -REL_CLIP, REL_CLIP) + REL_CLIP]
    valid = (jnp.arange(n_chunks)[:, None] - LEFT_CHUNKS + j // CHUNK) >= 0
    scores = scores + bias.astype(jnp.float32)[None, None]
    p = jax.nn.softmax(jnp.where(valid[None, :, None, None, :], scores, -jnp.inf), axis=-1).astype(v.dtype)
    parts = [jnp.einsum('bnhqk,bnkhd->bnqhd', p[..., i * CHUNK:(i + 1) * CHUNK], v_p[:, i:i + n_chunks])
             for i in range(LEFT_CHUNKS + 1)]
    o = functools.reduce(jnp.add, parts)
    return o.reshape(bsz, seq, MIX_ODD) @ w_out

def first_inputs(seed: int = 0) -> dict:
    key = jax.random.key(seed)
    ks = jax.random.split(key, 17)
    f32 = jnp.float32

    def nrm(k, shape, fan_in):
        return jax.random.normal(k, shape, f32) * (fan_in ** -0.5)

    def gain(k, shape):
        return 1.0 + 0.05 * jax.random.normal(k, shape, f32)

    return {
        "x": jax.random.normal(ks[0], (BATCH, SEQ, D_MODEL), f32),
        "ev_w_in": nrm(ks[1], (N_EVEN, D_MODEL, EVEN_IN), D_MODEL),
        "ev_g_cq": gain(ks[2], (N_EVEN, Q_LORA)),
        "ev_w_uq": nrm(ks[3], (N_EVEN, Q_LORA, MLA_HEADS * (MLA_NOPE + MLA_ROPE)), Q_LORA),
        "ev_g_ckv": gain(ks[4], (N_EVEN, KV_LORA)),
        "ev_w_ukv": nrm(ks[5], (N_EVEN, KV_LORA, MLA_HEADS * (MLA_NOPE + MLA_V)), KV_LORA),
        "ev_w_out": nrm(ks[6], (N_EVEN, MIX_EVEN, D_MODEL), MIX_EVEN),
        "od_w_qkv": nrm(ks[7], (N_ODD, D_MODEL, 3 * MIX_ODD), D_MODEL),
        "od_rel_bias": 0.1 * jax.random.normal(ks[8], (N_ODD, C_HEADS, 2 * REL_CLIP + 1), f32),
        "od_w_out": nrm(ks[9], (N_ODD, MIX_ODD, D_MODEL), MIX_ODD),
        "g_mix": gain(ks[10], (DEPTH, D_MODEL)),
        "g_ffn": gain(ks[11], (DEPTH, D_MODEL)),
        "w_gate": nrm(ks[12], (DEPTH, D_MODEL, D_FF), D_MODEL),
        "w_up": nrm(ks[13], (DEPTH, D_MODEL, D_FF), D_MODEL),
        "w_down": nrm(ks[14], (DEPTH, D_FF, D_MODEL), D_FF),
        "g_final": gain(ks[15], (D_MODEL,)),
    }

def first_block(x, ev_w_in, ev_g_cq, ev_w_uq, ev_g_ckv, ev_w_ukv, ev_w_out,
              od_w_qkv, od_rel_bias, od_w_out, g_mix, g_ffn, w_gate, w_up, w_down, g_final):
    h = x
    for layer in range(DEPTH):
        u = rms_norm(h, g_mix[layer])
        if layer % 2 == 0:
            i = layer // 2
            h = h + mla_stick_breaking_mixer(u, ev_w_in[i], ev_g_cq[i], ev_w_uq[i],
                                             ev_g_ckv[i], ev_w_ukv[i], ev_w_out[i])
        else:
            i = layer // 2
            h = h + chunk_band_mixer(u, od_w_qkv[i], od_rel_bias[i], od_w_out[i])
        u = rms_norm(h, g_ffn[layer])
        h = h + swiglu(u, w_gate[layer], w_up[layer], w_down[layer])
    return rms_norm(h, g_final)


DEPTH_2 = 1

N_META = 16
D_CONV = D_MODEL
CONV_WIDTH = 31
N_HEADS = 8
HEAD_DIM = 128
N_KV_HEADS = 2
N_IDX_HEADS = 8
IDX_DIM = 64
TOPK_MAX = 256
D_FF_2 = 2816
FFN_CONV_WIDTH = 3
EPS = 1e-6
META_BONUS = 1e30

COLS = (
    2 * D_CONV,
    N_HEADS * HEAD_DIM,
    N_KV_HEADS * HEAD_DIM,
    N_KV_HEADS * HEAD_DIM,
    N_IDX_HEADS * IDX_DIM,
    IDX_DIM,
    N_IDX_HEADS,
    2 * D_MODEL,
)
D_IN_PROJ = sum(COLS)


def rms_norm_2(x, g):
    xf = x.astype(jnp.float32)
    y = xf * lax.rsqrt(jnp.mean(xf * xf, axis=-1, keepdims=True) + EPS)
    return (y * g.astype(jnp.float32)).astype(x.dtype)

def layer_norm(x, g, b):
    xf = x.astype(jnp.float32)
    mu = jnp.mean(xf, axis=-1, keepdims=True)
    var = jnp.mean(jnp.square(xf - mu), axis=-1, keepdims=True)
    y = (xf - mu) * lax.rsqrt(var + EPS)
    return (y * g.astype(jnp.float32) + b.astype(jnp.float32)).astype(x.dtype)

def rope(x, pos):
    half = x.shape[-1] // 2
    inv = ROPE_THETA ** (-jnp.arange(half, dtype=jnp.float32) / half)
    ang = pos.astype(jnp.float32)[:, None] * inv[None, :]
    cos = jnp.cos(ang)[None, :, None, :]
    sin = jnp.sin(ang)[None, :, None, :]
    xf = x.astype(jnp.float32)
    x1, x2 = xf[..., :half], xf[..., half:]
    return jnp.concatenate([x1 * cos - x2 * sin, x2 * cos + x1 * sin], axis=-1).astype(x.dtype)

def causal_depthwise_conv(x, w, b):
    width, c = w.shape
    y = lax.conv_general_dilated(
        x, w[:, None, :].astype(x.dtype), window_strides=(1,),
        padding=[(width - 1, 0)], dimension_numbers=("NWC", "WIO", "NWC"),
        feature_group_count=c)
    return y + b.astype(x.dtype)

def conformer_conv_branch(u, ln_g, ln_b, dw_w, dw_b, pw_out):
    a, gate = jnp.split(u, 2, axis=-1)
    h = a * jax.nn.sigmoid(gate)
    h = causal_depthwise_conv(h, dw_w, dw_b)
    h = layer_norm(h, ln_g, ln_b)
    h = jax.nn.silu(h)
    return h @ pw_out

def dsa_sparse_attention(q, k, v, q_idx, k_idx, w_idx, w_o):
    bsz, seq_len = q.shape[0], q.shape[1]
    top_k = min(TOPK_MAX, seq_len // 4)
    n_blk = -(-seq_len // Q_BLOCK)
    pad = n_blk * Q_BLOCK - seq_len
    rep = N_HEADS // N_KV_HEADS

    def to_blocks(t):
        t = jnp.pad(t, [(0, 0), (0, pad)] + [(0, 0)] * (t.ndim - 2))
        t = t.reshape((bsz, n_blk, Q_BLOCK) + t.shape[2:])
        return jnp.moveaxis(t, 1, 0)

    key_pos = jnp.arange(seq_len, dtype=jnp.int32)
    q_pos_blocks = jnp.arange(n_blk * Q_BLOCK, dtype=jnp.int32).reshape(n_blk, Q_BLOCK)
    k_idx_f = k_idx.astype(jnp.float32)
    gather = jax.vmap(lambda kb, ib: kb[ib])

    def one_block(args):
        qb, qib, wb, qpos = args
        dots = jnp.einsum("bqhd,bsd->bqhs", qib.astype(jnp.float32), k_idx_f) * (IDX_DIM ** -0.5)
        score = jnp.einsum("bqh,bqhs->bqs", wb.astype(jnp.float32) * (N_IDX_HEADS ** -0.5),
                           jax.nn.relu(dots))
        visible = key_pos[None, :] <= qpos[:, None]
        is_meta = visible & (key_pos[None, :] < N_META)
        score = jnp.where(visible[None], score, -jnp.inf)
        score = jnp.where(is_meta[None], jnp.float32(METAB_PLACEHOLDER) if False else jnp.float32(METAB), score) if False else jnp.where(is_meta[None], jnp.float32(META_BONUS), score)
        vals, idx = lax.top_k(score, top_k)
        valid = jnp.isfinite(vals)
        ks = gather(k, idx)
        vs = gather(v, idx)
        qg = qb.reshape(bsz, Q_BLOCK, N_KV_HEADS, rep, HEAD_DIM)
        logits = jnp.einsum("bqgrd,bqkgd->bqgrk", qg, ks).astype(jnp.float32) * (HEAD_DIM ** -0.5)
        logits = jnp.where(valid[:, :, None, None, :], logits, -jnp.inf)
        p = jax.nn.softmax(logits, axis=-1).astype(v.dtype)
        o = jnp.einsum("bqgrk,bqkgd->bqgrd", p, vs)
        return o.reshape(bsz, Q_BLOCK, N_HEADS * HEAD_DIM)

    outs = lax.map(one_block, (to_blocks(q), to_blocks(q_idx), to_blocks(w_idx), q_pos_blocks))
    outs = jnp.moveaxis(outs, 0, 1).reshape(bsz, n_blk * Q_BLOCK, N_HEADS * HEAD_DIM)[:, :seq_len]
    return outs @ w_o

def second_inputs(seed: int = 0) -> dict:
    key = jax.random.key(seed)
    ks = jax.random.split(key, 20)
    f32 = jnp.float32

    def nrm(k, shape, scale):
        return jax.random.normal(k, shape, f32) * scale

    def gain(k, shape):
        return 1.0 + 0.05 * jax.random.normal(k, shape, f32)

    return {
        "x": jax.random.normal(ks[0], (BATCH, SEQ, D_MODEL), f32),
        "meta_tokens": nrm(ks[1], (N_META, D_MODEL), 1.0),
        "mix_norm_g": gain(ks[2], (DEPTH_2, D_MODEL)),
        "w_in": nrm(ks[3], (DEPTH_2, D_MODEL, D_IN_PROJ), D_MODEL ** -0.5),
        "conv_ln_g": gain(ks[4], (DEPTH_2, D_CONV)),
        "conv_ln_b": nrm(ks[5], (DEPTH_2, D_CONV), 0.01),
        "conv_dw_w": nrm(ks[6], (DEPTH_2, CONV_WIDTH, D_CONV), CONV_WIDTH ** -0.5),
        "conv_dw_b": nrm(ks[7], (DEPTH_2, D_CONV), 0.01),
        "conv_pw_out": nrm(ks[8], (DEPTH_2, D_CONV, D_MODEL), D_CONV ** -0.5),
        "attn_w_o": nrm(ks[9], (DEPTH_2, N_HEADS * HEAD_DIM, D_MODEL), (N_HEADS * HEAD_DIM) ** -0.5),
        "w_merge_out": nrm(ks[10], (DEPTH_2, D_MODEL, D_MODEL), D_MODEL ** -0.5),
        "ffn_norm_g": gain(ks[11], (DEPTH_2, D_MODEL)),
        "ffn_up": nrm(ks[12], (DEPTH_2, D_MODEL, 2 * D_FF_2), D_MODEL ** -0.5),
        "ffn_dw_w": nrm(ks[13], (DEPTH_2, FFN_CONV_WIDTH, 2 * D_FF_2), FFN_CONV_WIDTH ** -0.5),
        "ffn_dw_b": nrm(ks[14], (DEPTH_2, 2 * D_FF_2), 0.01),
        "ffn_down": nrm(ks[15], (DEPTH_2, D_FF_2, D_MODEL), D_FF_2 ** -0.5),
        "final_norm_g": gain(ks[16], (D_MODEL,)),
    }

def second_block(x, meta_tokens, mix_norm_g, w_in, conv_ln_g, conv_ln_b, conv_dw_w, conv_dw_b,
              conv_pw_out, attn_w_o, w_merge_out, ffn_norm_g, ffn_up, ffn_dw_w, ffn_dw_b,
              ffn_down, final_norm_g):
    bsz = x.shape[0]
    meta = jnp.broadcast_to(meta_tokens.astype(x.dtype)[None], (bsz, N_META, x.shape[-1]))
    stream = jnp.concatenate([meta, x], axis=1)
    seq_len = stream.shape[1]
    pos = jnp.arange(seq_len, dtype=jnp.int32)
    split_at = np.cumsum(COLS)[:-1].tolist()

    for l in range(DEPTH_2):
        h = rms_norm_2(stream, mix_norm_g[l])
        proj = h @ w_in[l]
        u_conv, q, k, v, q_idx, k_idx, w_idx, gates = jnp.split(proj, split_at, axis=-1)
        q = rope(q.reshape(bsz, seq_len, N_HEADS, HEAD_DIM), pos)
        k = rope(k.reshape(bsz, seq_len, N_KV_HEADS, HEAD_DIM), pos)
        v = v.reshape(bsz, seq_len, N_KV_HEADS, HEAD_DIM)
        q_idx = rope(q_idx.reshape(bsz, seq_len, N_IDX_HEADS, IDX_DIM), pos)
        k_idx = rope(k_idx[:, :, None, :], pos)[:, :, 0, :]

        y_a = conformer_conv_branch(u_conv, conv_ln_g[l], conv_ln_b[l], conv_dw_w[l],
                                    conv_dw_b[l], conv_pw_out[l])
        y_b = dsa_sparse_attention(q, k, v, q_idx, k_idx, w_idx, attn_w_o[l])
        g_a, g_b = jnp.split(jax.nn.sigmoid(gates), 2, axis=-1)
        stream = stream + (g_a * y_a + g_b * y_b) @ w_merge_out[l]

        h = rms_norm_2(stream, ffn_norm_g[l])
        up = causal_depthwise_conv(h @ ffn_up[l], ffn_dw_w[l], ffn_dw_b[l])
        a, b_ = jnp.split(up, 2, axis=-1)
        stream = stream + (jax.nn.silu(a) * b_) @ ffn_down[l]

    out = rms_norm_2(stream, final_norm_g)
    return out[:, N_META:]


def setup_inputs(seed=0):
    out = dict(first_inputs(seed))
    for name, value in second_inputs(seed + 1).items():
        if name != "x":
            out[name + "_2"] = value
    return out


def reference(
    x, ev_w_in, ev_g_cq, ev_w_uq, ev_g_ckv, ev_w_ukv, ev_w_out, od_w_qkv, od_rel_bias, od_w_out,
    g_mix, g_ffn, w_gate, w_up, w_down, g_final, meta_tokens_2, mix_norm_g_2, w_in_2,
    conv_ln_g_2, conv_ln_b_2, conv_dw_w_2, conv_dw_b_2, conv_pw_out_2, attn_w_o_2,
    w_merge_out_2, ffn_norm_g_2, ffn_up_2, ffn_dw_w_2, ffn_dw_b_2, ffn_down_2, final_norm_g_2,
):
    x = first_block(
        x, ev_w_in, ev_g_cq, ev_w_uq, ev_g_ckv, ev_w_ukv, ev_w_out, od_w_qkv, od_rel_bias,
        od_w_out, g_mix, g_ffn, w_gate, w_up, w_down, g_final,
    )
    return second_block(
        x, meta_tokens_2, mix_norm_g_2, w_in_2, conv_ln_g_2, conv_ln_b_2, conv_dw_w_2,
        conv_dw_b_2, conv_pw_out_2, attn_w_o_2, w_merge_out_2, ffn_norm_g_2, ffn_up_2,
        ffn_dw_w_2, ffn_dw_b_2, ffn_down_2, final_norm_g_2,
    )


_drawn_inputs = setup_inputs


def setup_inputs(seed=0):
    import zlib

    import numpy as np

    out = dict(_drawn_inputs(seed))
    spreads = {}
    factors = {'ev_g_cq': 5.797,
     'ev_g_ckv': 4.306,
     'od_rel_bias': 9.857,
     'conv_ln_g_2': 2.795,
     'conv_ln_b_2': 8.0,
     'conv_dw_b_2': 8.0,
     'ffn_dw_b_2': 8.0}
    for name, (base, spread) in spreads.items():
        noise = np.random.default_rng([zlib.crc32(name.encode()), seed]).standard_normal(out[name].shape)
        drawn = base * np.exp(spread * noise) if base else spread * noise
        out[name] = __import__('jax').numpy.asarray(drawn.astype(out[name].dtype))
    for name, factor in factors.items():
        out[name] = (out[name] * factor).astype(out[name].dtype)
    return out
```

```python
from contextlib import ExitStack

import numpy as np

import concourse.bass as bass
from concourse import mybir

F32 = mybir.dt.float32
F32R = mybir.dt.float32r
BF16 = mybir.dt.bfloat16
ACT = mybir.ActivationFunctionType
ALU = mybir.AluOpType
AX = mybir.AxisListType.X

P = 128
SEQ, D, META = 256, 1024, 16
T1, T2 = SEQ, SEQ + META
KT = D // P
DFF = 2816
FT = DFF // P
UC = 256
UNIT = KT * UC
AHEAD = 3
EPS = 1e-6

MLA_H, NOPE, ROPE_D, VD = 8, 64, 32, 64
QL, KVL = 384, 256
SB_H, C_H, HD = 8, 16, 64
DH, KVH, IH, ID = 128, 2, 8, 64
TOPK = min(256, T2 // 4)
CONV_W, CHUNK = 31, 64
NEG, LOWEST, BONUS = -1e30, -3e38, 1e30

DOWN_KT = [(0, 6), (6, 6), (12, 5), (17, 5)]

BLOCKS1 = [(0, P, [(0, P)]), (P, P, [(0, P), (P, P)])]
BLOCKS2 = [
    (0, META, [(0, META)]),
    (META, P, [(0, META), (META, P)]),
    (META + P, P, [(0, META), (META, P), (META + P, P)]),
]

GAINS = {}
for _name, _rows in (("mix", 16), ("ffn", 16), ("final", 8), ("cq", 3), ("ckv", 2), ("mix2", 8),
                     ("ln_g", 8), ("ln_b", 8), ("dw_b", 8), ("ffn2", 8), ("final2", 8)):
    GAINS[_name] = (sum(r for _, r in GAINS.values()), _rows)
GAIN_ROWS = sum(r for _, r in GAINS.values())


def shape_constants():
    def half_rotation(dim):
        r = np.zeros((P, P), np.float32)
        for base in range(0, P, dim):
            for i in range(dim // 2):
                r[base + i, base + dim // 2 + i] = -1.0
                r[base + dim // 2 + i, base + i] = 1.0
        return r.T

    def tables(dim, n):
        half = dim // 2
        inv = np.float32(10000.0) ** (-np.arange(0, dim, 2, dtype=np.float32) / np.float32(dim))
        ang = np.arange(n, dtype=np.float32)[:, None] * inv[None, :].astype(np.float32)
        rows = (np.arange(P) % dim) % half
        return np.cos(ang).T[rows], np.sin(ang).T[rows]

    q, k = np.arange(P)[:, None], np.arange(P)[None, :]
    parts = {
        "ident": np.eye(P), "ones": np.ones((P, T2)),
        "rot32": half_rotation(32), "rot128": half_rotation(128), "rot64": half_rotation(64),
        "chunk_mask": np.where(k // CHUNK <= q // CHUNK, 0.0, NEG),
        "before_mask": np.where(k < q, 0.0, NEG),
        "seen_mask": np.where(k <= q, 0.0, LOWEST),
    }
    for name, dim, n in (("32", 32, T1), ("128", 128, T2), ("64", 64, T2)):
        parts["cos" + name], parts["sin" + name] = tables(dim, n)
    where, at = {}, 0
    for name, a in parts.items():
        where[name] = (at, a.shape[1])
        at += a.shape[1]
    return np.concatenate([a.astype(np.float32) for a in parts.values()], axis=1), where


def wait(eng, sem, value):
    if isinstance(value, int) and value <= 0:
        return
    eng.wait_ge(sem, value)


class Phase:

    def __init__(self, plan, units, body, group=1, dmas=None, peel=0):
        self.u0, self.units, self.body, self.group = plan["units"], units, body, group
        self.turns, self.rest = divmod(units, body)
        self.peel = peel
        self.loads0 = list(plan["loads"])
        self.groups = body // group
        self.used = list(plan["used"])
        self.dmas = dmas or [1] * units
        plan["units"] += units
        for n, d in enumerate(self.dmas):
            plan["loads"][(self.u0 + n) % 2] += 16 * d
        for n in range(units // group):
            plan["used"][n % self.groups % 4] += 1
        self.used_after = list(plan["used"])
        plan["phases"].append(self)

    def steps(self, eng):
        looped = self.turns - self.peel if self.turns - self.peel > 1 else 0
        if looped:
            with eng.Fori(0, looped) as i:
                for k in range(self.body):
                    yield i, k
        for i in range(looped, self.turns):
            for k in range(self.body):
                yield i, k
        for k in range(self.rest):
            yield self.turns, k

    def unit(self, i, k):
        return i * self.body + (self.u0 + k)

    def loaded(self, i, k):
        if isinstance(i, int):
            n = i * self.body + k
            return self.loads0[(self.u0 + k) % 2] + 16 * sum(
                self.dmas[m] for m in range(n + 1) if (m - n) % 2 == 0)
        return self.loads0[(self.u0 + k) % 2] + i * (16 * self.body // 2) + 16 * (k // 2 + 1)

    def pair(self, k):
        return k // self.group % self.groups % 4

    def used_before(self, i, k):
        per_turn = max(1, self.groups // 4)
        return i * per_turn + (self.used[self.pair(k)] + k // self.group % self.groups // 4)


def build(nc, x, ev_w_in, ev_g_cq, ev_w_uq, ev_g_ckv, ev_w_ukv, ev_w_out, od_w_qkv, od_rel_bias,
          od_w_out, g_mix, g_ffn, w_gate, w_up, w_down, g_final, meta_tokens_2, mix_norm_g_2,
          w_in_2, conv_ln_g_2, conv_ln_b_2, conv_dw_w_2, conv_dw_b_2, conv_pw_out_2, attn_w_o_2,
          w_merge_out_2, ffn_norm_g_2, ffn_up_2, ffn_dw_w_2, ffn_dw_b_2, ffn_down_2,
          final_norm_g_2, constants, where, out, debug=None):
    ctx = ExitStack()
    sems = {}

    def sem(name):
        if name not in sems:
            sems[name] = ctx.enter_context(nc.semaphore(name))
        return sems[name]

    def sb(name, shape, dt=F32, scope=None):
        return (scope or ctx).enter_context(nc.sbuf_tensor(name, shape, dt))

    raw = [sb(f"raw{s}", [P, UNIT]) for s in range(2)]
    w_hi = [sb(f"w_hi{s}", [P, UNIT], F32R) for s in range(4)]
    w_lo = [sb(f"w_lo{s}", [P, UNIT], F32R) for s in range(4)]
    h = sb("h", [P, KT, T2])
    u_hi = sb("u_hi", [P, KT, T2], F32R)
    u_lo = sb("u_lo", [P, KT, T2], F32R)
    work = sb("work", [P, KT, T2])
    const = sb("const", [P, constants.shape[1]])
    masks = sb("masks", [P, 4, P], BF16)
    gains = sb("gains", [P, GAIN_ROWS])
    ffn_dw = sb("ffn_dw", [P, 2, 2 * FT * 2])
    conv_w = sb("conv_w", [P, KT, CONV_W])
    eps = sb("eps", [P, 1])
    log_ms = sb("log_ms", [P, T2])
    rstd = sb("rstd", [P, T2])

    def c(name):
        at, n = where[name]
        return const[:, at:at + n]

    ident, wide_ones = c("ident"), c("ones")
    ones = wide_ones[:, 0:P]
    ident_b, chunk_b, before_b, seen_b = (masks[:, n, :] for n in range(4))

    with ExitStack() as s:
        x_rows = sb("x_rows", [P, 2, D], scope=s)
        meta_rows = sb("meta_rows", [META, D], scope=s)
        gain_rows = sb("gain_rows", [GAIN_ROWS, P], scope=s)
        dw_rows = sb("dw_rows", [2 * 2 * FT, 2, P], scope=s)
        conv_rows = sb("conv_rows", [CONV_W, D], scope=s)
    with ExitStack() as s:
        o1 = sb("o1", [P, 2, D], scope=s)
        p1 = sb("p1", [P, 2, 512], scope=s)
        pt1 = sb("pt1", [P, 2, 1024], scope=s)
        stat1 = sb("stat1", [P, 2, 4, 3], scope=s)
        k_rope = sb("k_rope", [P, T1], scope=s)
        q_nope = sb("q_nope", [P, 4, T1], scope=s)
        q_rope = sb("q_rope", [P, 2, T1], scope=s)
        k_nope = sb("k_nope", [P, 4, T1], scope=s)
        v_a = sb("v_a", [P, 2, MLA_H * VD], scope=s)
        q_b = sb("q_b", [P, 4, T1], scope=s)
        k_b = sb("k_b", [P, 4, T1], scope=s)
        v_b = sb("v_b", [P, 2, SB_H * HD], scope=s)
        q_pad = sb("q_pad", [P, 4, T1], scope=s)
        q_pad_r = sb("q_pad_r", [P, 4, T1], scope=s)
        rope_t = sb("rope_t", [P, 2, T2], scope=s)
        with ExitStack() as t:
            lat = sb("lat", [P, 5, T1], scope=t)
            lat_hi = sb("lat_hi", [P, 5, T1], F32R, scope=t)
            lat_lo = sb("lat_lo", [P, 5, T1], F32R, scope=t)
        stick = sb("stick", [P, 2, 5, 384], scope=s)
    with ExitStack() as s:
        a_hi = sb("a_hi", [P, FT, T1], F32R, scope=s)
        a_lo = sb("a_lo", [P, FT, T1], F32R, scope=s)
        act_g = sb("act_g", [P, 2, 2, T1], scope=s)
        act_a = sb("act_a", [P, 2, 2, T1], scope=s)
        cva = sb("cva", [P, 2, 2, T1], scope=s)
        cvb = sb("cvb", [P, 2, 2, T1], scope=s)
    with ExitStack() as s:
        o3 = sb("o3", [P, 2, D], scope=s)
        p3 = sb("p3", [P, 2, 512], scope=s)
        pt3 = sb("pt3", [P, 2, 1024], scope=s)
        stat3 = sb("stat3", [P, 2, 4, 3], scope=s)
        qk_c = sb("qk_c", [P, 16, T1], scope=s)
        q_c, k_c = qk_c[:, 0:8, :], qk_c[:, 8:16, :]
        v_c = sb("v_c", [P, 2, D], scope=s)
        q_pad_c = sb("q_pad_c", [P, 4, T1], scope=s)
        biased = sb("biased", [P, 2, 512], scope=s)
        bias_h = sb("bias_h", [P, C_H, 2 * P], scope=s)
    with ExitStack() as s:
        p4 = sb("p4", [P, 2, 512], scope=s)
        pt4 = sb("pt4", [P, 2, 1024], scope=s)
        stat4 = sb("stat4", [P, 2, 4, 3], scope=s)
        gates = sb("gates", [P, 2 * KT, T2], scope=s)
        q_d = sb("q_d", [P, 8, T2], scope=s)
        k_d = sb("k_d", [P, KVH, T2], scope=s)
        v_d = sb("v_d", [P, 3, KVH * DH], scope=s)
        qi = sb("qi", [P, IH * ID // P, T2], scope=s)
        ki = sb("ki", [P, T2], scope=s)
        wi = sb("wi", [P, 3, IH], scope=s)
        q_cur = sb("q_cur", [P, 2, T2], scope=s)
        rope4 = sb("rope4", [P, 2, T2], scope=s)
        sg4 = sb("sg4", [P, 2, 2, T2], scope=s)
        pick = sb("pick", [P, 416], BF16, scope=s)
        top8 = sb("top8", [P, 2, 8], scope=s)
        need = sb("need", [P, 2], scope=s)
        with ExitStack() as t:
            cin = sb("cin", [P, KT, CONV_W - 1 + T2], scope=t)
        o4 = sb("o4", [P, 3, D], scope=s)
    with ExitStack() as s:
        out_rows = sb("out_rows", [P, 2, D], scope=s)
    picks = cin[:].rearrange("p a b -> p (a b)")
    acc, left, above, equal = (picks[:, n * 416:(n + 1) * 416] for n in range(4))
    sg_flat = sg4[:].rearrange("p a b c -> p (a b c)")

    def dots(n):
        return sg_flat[:, n * 416:(n + 1) * 416]

    def biased_ap(e, b):
        return biased[:, e % 2, chk.cols[b]:chk.cols[b] + (b + 1) * P]

    ps = ctx.enter_context(nc.psum_tensor("ps", [P, 8, 512], F32))

    def pw(s, nk, n):
        return s[:, 0:nk * n].rearrange("p (k n) -> p k n", k=nk)

    plan = {"units": 0, "loads": [0, 0], "used": [0, 0, 0, 0], "phases": []}
    ph_in = Phase(plan, 9, 9, dmas=[1, 1, 5, 1, 1, 1, 1, 1, 1])
    ph_lat = Phase(plan, 4, 4, dmas=[6, 6, 2, 2])
    ph_out0 = Phase(plan, 4, 4)
    ph_ffn0 = Phase(plan, 2 * DFF // UC, 4)
    ph_down0 = Phase(plan, 16, 8, group=4)
    ph_qk = Phase(plan, 8, 4)
    ph_v = Phase(plan, 4, 4)
    ph_out1 = Phase(plan, 4, 4)
    ph_ffn1 = Phase(plan, 2 * DFF // UC, 4)
    ph_down1 = Phase(plan, 16, 8, group=4)
    ph_conv = Phase(plan, 8, 4)
    ph_proj = Phase(plan, 8, 8)
    ph_idx = Phase(plan, 1, 1, dmas=[3])
    ph_gate = Phase(plan, 8, 4)
    ph_pw = Phase(plan, 4, 4)
    ph_wo = Phase(plan, 4, 4)
    ph_merge = Phase(plan, 4, 4)
    ph_ffn2 = Phase(plan, 2 * DFF // UC, 4)
    ph_down2 = Phase(plan, 16, 8, group=4, peel=1)
    units = plan["units"]
    landed, count = [], [0, 0]
    for ph in plan["phases"]:
        for n, d in enumerate(ph.dmas):
            count[(ph.u0 + n) % 2] += 16 * d
            landed.append(count[(ph.u0 + n) % 2])

    raw_landed = [sem("raw_landed0"), sem("raw_landed1")]
    hi_done, lo_done, unit_done = sem("hi_done"), sem("lo_done"), sem("unit_done")
    pair_read = [sem(f"pair_read{n}") for n in range(4)]

    def pairs_read(eng, ph):
        for n in range(4):
            wait(eng, pair_read[n], ph.used_after[n])

    def split_hi(ph, i, k):
        t = ph.u0 + (i * ph.body if isinstance(i, int) else 0) + k + AHEAD
        if isinstance(i, int) and t >= units:
            return
        turn = 0 if isinstance(i, int) else i
        nc.scalar.wait_ge(raw_landed[t % 2], turn * (8 * ph.body) + landed[t])
        wait(nc.scalar, unit_done, turn * ph.body + (t - 3))
        nc.scalar.activation(w_hi[t % 4][:], raw[t % 2][:], ACT.Copy).then_inc(hi_done, 1)

    def split_lo(ph, i, k):
        t = ph.u0 + (i * ph.body if isinstance(i, int) else 0) + k + AHEAD
        if isinstance(i, int) and t >= units:
            return
        turn = 0 if isinstance(i, int) else i
        nc.vector.wait_ge(hi_done, turn * ph.body + (t + 1))
        nc.vector.tensor_tensor(w_lo[t % 4][:], raw[t % 2][:], w_hi[t % 4][:].bitcast(F32),
                                ALU.subtract).then_inc(lo_done, 1)

    prologue = Phase({"units": -AHEAD, "loads": [0, 0], "used": [0] * 4, "phases": []}, AHEAD, AHEAD)

    norm_at, norm_n = {}, [0, 0]
    for name, nk in (("mix0", KT), ("cq", 3), ("ckv", 2), ("ffn0", KT), ("mix1", KT), ("ffn1", KT),
                     ("final", KT), ("mix2", KT), ("ffn2", KT), ("final2", KT)):
        norm_at[name] = tuple(norm_n)
        norm_n[0] += 1
        norm_n[1] += nk

    def norm_act(name, src, nk, cols, dim, split=None):
        one, at = norm_at[name]
        n = cols.stop - cols.start
        for kt in range(nk):
            nc.scalar.activation(work[:, kt, 0:n], src(kt), ACT.Square).then_inc(sem("sq_done"), 1)
        nc.scalar.wait_ge(sem("ss_done"), one + 1)
        nc.scalar.activation(log_ms[:, 0:n], ps[:, 7, 0:n], ACT.Ln, scale=1.0 / dim,
                             bias=eps[:]).then_inc(sem("ln_done"), 1)
        nc.scalar.wait_ge(sem("ln_done"), one + 1)
        nc.scalar.activation(rstd[:, 0:n], log_ms[:, 0:n], ACT.Exp, scale=-0.5)\
            .then_inc(sem("rstd_done"), 1)
        if split is not None:
            for kt in range(nk):
                nc.scalar.wait_ge(sem("un_done"), at + kt + 1)
                nc.scalar.activation(split[0](kt), work[:, kt, 0:n], ACT.Copy)\
                    .then_inc(sem("xh_done"), 1)

    def norm_pe(name, nk, n):
        one, at = norm_at[name]
        for kt in range(nk):
            nc.tensor.wait_ge(sem("sq_done"), at + kt + 1)
            mm = nc.tensor.matmul(ps[:, 7, 0:n], ones, work[:, kt, 0:n], start=kt == 0,
                                  stop=kt == nk - 1)
        mm.then_inc(sem("ss_done"), 1)

    xh_total, xl_total = [0], [0]
    split_at = {}
    for name, nk in (("mix0", KT), ("cq", 3), ("ckv", 2), ("o0", KT), ("ffn0", KT), ("mix1", KT),
                     ("o1", KT), ("ffn1", KT), ("mix2", KT), ("ln", KT), ("o2", KT),
                     ("merge", KT), ("ffn2", KT)):
        split_at[name] = xl_total[0]
        xl_total[0] += nk

    def norm_dve(name, src, gain, nk, n, split=None, into=None):
        one, at = norm_at[name]
        g0 = GAINS[gain[0]][0] + gain[1]

        def lo(kt):
            nc.vector.wait_ge(sem("xh_done"), split_at[name] + kt + 1)
            nc.vector.tensor_tensor(split[1](kt), work[:, kt, 0:n], split[0](kt).bitcast(F32),
                                    ALU.subtract).then_inc(sem("xl_done"), 1)

        nc.vector.wait_ge(sem("rstd_done"), one + 1)
        for kt in range(nk):
            dst = work[:, kt, 0:n] if into is None else into(kt)
            nc.vector.scalar_tensor_tensor(out=dst, in0=src(kt), scalar=gains[:, g0 + kt:g0 + kt + 1],
                                           in1=rstd[:, 0:n], op0=ALU.mult, op1=ALU.mult)\
                .then_inc(sem("un_done"), 1)
            if split is not None and kt >= 1:
                lo(kt - 1)
        if split is not None:
            lo(nk - 1)

    def norm_split_act(name, src, nk, cols, dim, hi):
        norm_act(name, src, nk, cols, dim, split=(hi,))

    def u_h(n):
        return lambda kt: u_hi[:, kt, 0:n]

    def u_l(n):
        return lambda kt: u_lo[:, kt, 0:n]

    C1, C2, CF = slice(META, T2), slice(0, T2), slice(META - 2, T2)
    NF = T2 - META + 2

    def h_at(cols):
        return lambda kt: h[:, kt, cols]

    def product(out_ap, pairs, start=True, stop=True):
        for n, (a_h, a_l, b_h, b_l) in enumerate(pairs):
            nc.tensor.matmul(out_ap, a_h, b_h, start=start and n == 0, stop=False)
            nc.tensor.matmul(out_ap, a_h, b_l, start=False, stop=False)
            mm = nc.tensor.matmul(out_ap, a_l, b_h, start=False, stop=stop and n == len(pairs) - 1)
        return mm

    def feature_tile(out_ap, s, nk, n, col, xh, xl, x0=0, start=True, stop=True):
        hi, lo = pw(w_hi[s], nk, n), pw(w_lo[s], nk, n)
        return product(out_ap, [(hi[:, kt, col:col + P], lo[:, kt, col:col + P], xh(x0 + kt), xl(x0 + kt))
                                for kt in range(nk)], start, stop)

    def token_tile(out_ap, s, nk, n, cols, xh, xl, x0=0):
        hi, lo = pw(w_hi[s], nk, n), pw(w_lo[s], nk, n)
        return product(out_ap, [(xh(x0 + kt), xl(x0 + kt), hi[:, kt, cols], lo[:, kt, cols])
                                for kt in range(nk)])

    def begin_unit(ph, i, k):
        s = (ph.u0 + k) % 4
        nc.tensor.wait_ge(lo_done, ph.unit(i, k) + 1)
        if k % ph.group == 0:
            wait(nc.tensor, pair_read[ph.pair(k)], ph.used_before(i, k))
        return s, ph.pair(k)

    def by_tokens(ph, i, k):
        s, p = begin_unit(ph, i, k)
        for b in range(2):
            mm = token_tile(ps[:, 2 * p + b, 0:UC], s, KT, UC, slice(0, UC),
                            lambda kt: u_hi[:, kt, b * P:(b + 1) * P], lambda kt: u_lo[:, kt, b * P:(b + 1) * P])
        mm.then_inc(unit_done, 1)

    def two_tiles(ph, i, k, n, xh, xl):
        s, p = begin_unit(ph, i, k)
        for t in range(2):
            mm = feature_tile(ps[:, 2 * p + t, 0:n], s, KT, UC, t * P, xh, xl)
        mm.then_inc(unit_done, 1)

    def down_unit(ph, i, k):
        s, p = begin_unit(ph, i, k)
        k0, nk = DOWN_KT[k % 4]
        for t in range(2):
            mm = feature_tile(ps[:, 2 * p + t, 0:T1], s, nk, UC, t * P, lambda kt: a_hi[:, kt, :],
                              lambda kt: a_lo[:, kt, :], x0=k0, start=k % 4 == 0, stop=k % 4 == 3)
        mm.then_inc(unit_done, 1)

    def pair_ap(p, n):
        return ps[:, 2 * p:2 * p + 2, 0:n]

    ATT = {"mla": 0, "stick": MLA_H, "chunk": MLA_H + SB_H, "dsa": MLA_H + SB_H + C_H}

    class Attention:
        def __init__(self, name, heads, blocks, dv, banks, bufs, o, lag=1):
            self.soft = {"mla": 0, "chunk": MLA_H, "dsa": MLA_H + C_H}.get(name)
            self.base, self.turns, self.blocks, self.dv, self.lag = ATT[name], heads // 4, blocks, dv, lag
            self.heads = heads
            self.s_banks, self.pt_banks, self.o_banks = banks
            self.p, self.pt, self.stat = bufs
            self.o = o
            self.cols, at = [], 0
            for _, _, keys in blocks:
                self.cols.append(at)
                at += sum(n for _, n in keys)
            self.width = at
            self.tcols, small, large = [], 0, 0
            few = any(n < P for _, _, keys in blocks for _, n in keys)
            for _, nq, keys in blocks:
                row = []
                for _, n in keys:
                    if n < P:
                        row.append((0, small))
                        small += nq
                    else:
                        row.append((1 if few else 0, large))
                        large += nq
                self.tcols.append(row)
            self.parts = ([(META, 0, small)] if few else []) + [(P, 1 if few else 0, large)]

        def steps(self, eng):
            looped = self.turns > 2
            for i in range(1 if looped else self.turns):
                for e in range(4):
                    yield i, e
            if looped:
                with eng.Fori(1, self.turns) as i:
                    for e in range(4):
                        yield i, e

        def head(self, i, e, back=0):
            n = i * 4 + (e - back)
            return None if isinstance(n, int) and n < 0 else n

        def S(self, e, b):
            _, nq, keys = self.blocks[b]
            return ps[0:nq, self.s_banks[e % len(self.s_banks)],
                      self.cols[b]:self.cols[b] + sum(n for _, n in keys)]

        def P(self, e, b, key=None):
            _, nq, keys = self.blocks[b]
            at = self.cols[b] + (0 if key is None else sum(n for _, n in keys[:key]))
            n = sum(n for _, n in keys) if key is None else keys[key][1]
            return self.p[0:nq, e % 2, at:at + n]

        def pt_ps(self, e, b, key):
            _, nq, keys = self.blocks[b]
            bank, at = self.tcols[b][key]
            return ps[0:keys[key][1], self.pt_banks[e % 2][bank], at:at + nq]

        def PT(self, e, b, key):
            _, nq, keys = self.blocks[b]
            bank, at = self.tcols[b][key]
            return self.pt[0:keys[key][1], e % 2, 512 * bank + at:512 * bank + at + nq]

        def O(self, e, b):
            return ps[0:self.blocks[b][1], self.o_banks[e % 2], b * self.dv:(b + 1) * self.dv]

        def transposes(self, n, e):
            nc.tensor.wait_ge(sem("at_p"), n + (self.base + 1))
            wait(nc.tensor, sem("at_ptc"), n + (self.base - 1))
            for b, (_, nq, keys) in enumerate(self.blocks):
                for key in range(len(keys)):
                    mm = nc.tensor.transpose(self.pt_ps(e, b, key), self.P(e, b, key), ident[0:nq, 0:nq])
            mm.then_inc(sem("at_pt"), 1)

        def values(self, n, e, v):
            nc.tensor.wait_ge(sem("at_ptc"), n + (self.base + 1))
            wait(nc.tensor, sem("at_oev"), n + (self.base - 1))
            for b, (_, nq, keys) in enumerate(self.blocks):
                for key in range(len(keys)):
                    mm = nc.tensor.matmul(self.O(e, b), self.PT(e, b, key), v(n, e, b, key),
                                          start=key == 0, stop=key == len(keys) - 1)
            mm.then_inc(sem("at_o"), 1)

        def pe(self, scores, v):
            for i, e in self.steps(nc.tensor):
                n = self.head(i, e)
                wait(nc.tensor, sem("at_p"), n + (self.base + 1 - len(self.s_banks)))
                scores(self, i, e, n).then_inc(sem("at_scores"), 1)
                if (m := self.head(i, e, self.lag)) is not None:
                    self.transposes(m, (e - self.lag) % 4)
                if (m := self.head(i, e, self.lag + 1)) is not None:
                    self.values(m, (e - self.lag - 1) % 4, v)
            for m in range(self.heads - self.lag, self.heads):
                self.transposes(m, m % 4)
                self.values(m - 1, (m - 1) % 4, v)
            self.values(self.heads - 1, (self.heads - 1) % 4, v)

        def exps(self, n, e, scale, src):
            nc.scalar.wait_ge(sem("at_neg"), n + (self.soft + 1))
            wait(nc.scalar, sem("at_pt"), n + (self.base - 1))
            wait(nc.scalar, sem("at_oev"), n + (self.base - 1))
            for b, (_, nq, _) in enumerate(self.blocks):
                st = self.stat[0:nq, e % 2]
                a = nc.scalar.activation(self.P(e, b), src(e, b), ACT.Exp, scale=scale,
                                         bias=st[:, 1, b:b + 1], accum_out=st[:, 2, b:b + 1])
            a.then_inc(sem("at_p"), 1)

        def copies(self, n, e):
            nc.scalar.wait_ge(sem("at_pt"), n + (self.base + 1))
            wait(nc.scalar, sem("at_o"), n + (self.base - 1))
            for rows, bank, width in self.parts:
                a = nc.scalar.activation(self.pt[0:rows, e % 2, 512 * bank:512 * bank + width],
                                         ps[0:rows, self.pt_banks[e % 2][bank], 0:width], ACT.Copy)
            a.then_inc(sem("at_ptc"), 1)

        def act(self, scale, src):
            for i, e in self.steps(nc.scalar):
                self.exps(self.head(i, e), e, scale, src)
                if (m := self.head(i, e, 1)) is not None:
                    self.copies(m, (e - 1) % 4)
            self.copies(self.heads - 1, (self.heads - 1) % 4)

        def maxima(self, n, e, scale, src):
            wait(nc.vector, sem("at_p"), n + (self.base - 1))
            for b, (_, nq, _) in enumerate(self.blocks):
                a = nc.vector.reduce_max(self.stat[0:nq, e % 2, 0, b:b + 1], src(e, b), AX)
            a.then_inc(sem("at_max"), 1)
            nc.vector.wait_ge(sem("at_max"), n + (self.soft + 1))
            nb = len(self.blocks)
            nc.vector.tensor_scalar(self.stat[:, e % 2, 1, 0:nb], self.stat[:, e % 2, 0, 0:nb], -scale,
                                    None, ALU.mult).then_inc(sem("at_neg"), 1)

        def normalise(self, n, e):
            nc.vector.wait_ge(sem("at_p"), n + (self.base + 1))
            nb = len(self.blocks)
            nc.vector.reciprocal(self.stat[:, e % 2, 3, 0:nb], self.stat[:, e % 2, 2, 0:nb])\
                .then_inc(sem("at_rsum"), 1)
            nc.vector.wait_ge(sem("at_o"), n + (self.base + 1))
            nc.vector.wait_ge(sem("at_rsum"), n + (self.soft + 1))
            for b, (_, nq, _) in enumerate(self.blocks):
                a = nc.vector.tensor_scalar(self.o(n, b), self.O(e, b), self.stat[0:nq, e % 2, 3, b:b + 1],
                                            None, ALU.mult)
            a.then_inc(sem("at_oev"), 1)

        def dve(self, scale, src, before=None):
            for i, e in self.steps(nc.vector):
                n = self.head(i, e)
                nc.vector.wait_ge(sem("at_scores"), n + (self.base + 1))
                if before is not None:
                    before(self, n, e)
                self.maxima(n, e, scale, src)
                if (m := self.head(i, e, 2)) is not None:
                    self.normalise(m, (e - 2) % 4)
            for m in range(self.heads - 2, self.heads):
                self.normalise(m, m % 4)

    def by_head(t, n, d):
        return t.rearrange("p b (n d) -> p b n d", d=d)

    o1v, o3v, o4v = by_head(o1, 0, VD), by_head(o3, 0, HD), by_head(o4, 0, DH)
    wide = ([0, 1, 2, 3], [[4], [5]], [6, 7])
    mla = Attention("mla", MLA_H, BLOCKS1, VD, wide, (p1, pt1, stat1),
                    lambda n, b: o1v[:, b, n, :])
    stk = Attention("stick", SB_H, BLOCKS1, HD, wide, (p1, pt1, stat1),
                    lambda n, b: o1v[:, b, n + MLA_H, :], lag=2)
    chk = Attention("chunk", C_H, BLOCKS1, HD, wide, (p3, pt3, stat3),
                    lambda n, b: o3v[:, b, n, :])
    dsa = Attention("dsa", 8, BLOCKS2, DH, ([0, 1], [[2, 3], [4, 5]], [6, 7]), (p4, pt4, stat4),
                    lambda n, b: o4v[0:BLOCKS2[b][1], b, n, :])

    def pad_heads(att, q, q_dst, extra=None):
        for i, e in att.steps(nc.gpsimd):
            n = att.head(i, e)
            wait(nc.gpsimd, sem("at_scores"), n + (att.base - 3))
            wait(nc.gpsimd, sem("pad_done"), n + att.base)
            rows = slice(64 * (e % 2), 64 * (e % 2) + 64)
            a = nc.gpsimd.tensor_copy(q_dst[rows, e, :], q[rows, i * 2 + e // 2, :])
            if extra is not None:
                a.then_inc(sem("pad_part"), 1)
                nc.gpsimd.wait_ge(sem("pad_part"), n + 1)
                a = extra(i, e)
            a.then_inc(sem("pad_done"), 1)

    def masked_scores(att, e, b, terms, mask):
        out_ap = att.S(e, b)
        for t, (lhs, rhs) in enumerate(terms):
            nc.tensor.matmul(out_ap, lhs, rhs, start=t == 0, stop=False)
        _, nq, keys = att.blocks[b]
        own = sum(n for _, n in keys[:-1])
        return nc.tensor.matmul(out_ap[:, own:own + nq], ident_b[0:nq, 0:nq], mask[0:nq, 0:nq],
                                start=False, stop=True)

    def mla_scores(att, i, e, n):
        nc.tensor.wait_ge(sem("pad_done"), n + (att.base + 1))
        for b, (q0, nq, keys) in enumerate(att.blocks):
            end = keys[-1][0] + keys[-1][1]
            mm = masked_scores(att, e, b, [
                (q_pad[:, e, q0:q0 + nq], k_nope[:, i * 2 + e // 2, 0:end]),
                (q_pad_r[:, e, q0:q0 + nq], k_rope[:, 0:end])], chunk_b)
        return mm

    def pair_scores(q, kk, mask):
        def scores(att, i, e, n):
            nc.tensor.wait_ge(sem("pad_done"), n + (att.base + 1))
            for b, (q0, nq, keys) in enumerate(att.blocks):
                end = keys[-1][0] + keys[-1][1]
                mm = masked_scores(att, e, b, [(q[:, e, q0:q0 + nq], kk[:, i * 2 + e // 2, 0:end])], mask)
            return mm
        return scores

    def head_values(v, d):
        vv = v.rearrange("p b (n d) -> p b n d", d=d)
        return lambda n, e, b, key: vv[:, key, n, :]

    def rope_pe(rot, tiles, n, first):
        for t, x_ap in enumerate(tiles):
            wait(nc.tensor, sem("rope_done"), first + t - 1)
            nc.tensor.matmul(ps[:, (first + t) % 2, 0:n], rot, x_ap, start=True, stop=True)\
                .then_inc(sem("rot_done"), 1)

    def rope_dve(tiles, cos, sin, n, first, tmp):
        for t, x_ap in enumerate(tiles):
            at = first + t
            nc.vector.wait_ge(sem("rot_done"), at + 1)
            nc.vector.tensor_tensor(tmp[:, at % 2, 0:n], x_ap, cos, ALU.mult).then_inc(sem("rope_cos"), 1)
            nc.vector.wait_ge(sem("rope_cos"), at + 1)
            nc.vector.tensor_tensor(x_ap, ps[:, at % 2, 0:n], sin, ALU.mult).then_inc(sem("rope_sin"), 1)
            nc.vector.wait_ge(sem("rope_sin"), at + 1)
            nc.vector.tensor_tensor(x_ap, x_ap, tmp[:, at % 2, 0:n], ALU.add).then_inc(sem("rope_done"), 1)

    def turn_pe(o, blocks, n):
        for j in range(KT):
            for b, (q0, nq, _) in enumerate(blocks):
                mm = nc.tensor.transpose(ps[:, j, q0:q0 + nq], o[0:nq, b, j * P:(j + 1) * P], ident[0:nq, 0:nq])
            mm.then_inc(sem("turned"), 1)

    def turn_act(first, n):
        for j in range(KT):
            nc.scalar.wait_ge(sem("turned"), first + j + 1)
            nc.scalar.activation(u_hi[:, j, 0:n], ps[:, j, 0:n], ACT.Copy).then_inc(sem("xh_done"), 1)

    def turn_dve(name, n):
        for j in range(KT):
            nc.vector.wait_ge(sem("xh_done"), split_at[name] + j + 1)
            nc.vector.tensor_tensor(u_lo[:, j, 0:n], ps[:, j, 0:n], u_hi[:, j, 0:n].bitcast(F32), ALU.subtract)\
                .then_inc(sem("xl_done"), 1)

    def operands_ready(name, nk=KT):
        nc.tensor.wait_ge(sem("xl_done"), split_at[name] + nk)

    def residual_dve(ph, cols, group=1):
        n = cols.stop - cols.start
        for i, k in ph.steps(nc.vector):
            split_lo(ph, i, k)
            if k % group == group - 1:
                p = ph.pair(k)
                j = i * ph.groups + k // group
                nc.vector.wait_ge(unit_done, ph.unit(i, k) + 1)
                hv = h.rearrange("p (j t) n -> p j t n", t=2)[:, j, :, cols]
                nc.vector.tensor_tensor(hv, hv, pair_ap(p, n), ALU.add).then_inc(pair_read[p], 1)

    def splits_act(ph):
        for i, k in ph.steps(nc.scalar):
            split_hi(ph, i, k)

    FFN = {"ffn0": 0, "ffn1": FT // 2, "ffn2": FT}

    def paired(t):
        return t.rearrange("p (j t) n -> p j t n", t=2)

    def ffn_act(name, ph):
        for i, k in ph.steps(nc.scalar):
            split_hi(ph, i, k)
            j, s, p = i * 2 + k // 2, (k // 2) % 2, ph.pair(k)
            if k % 2 == 0:
                nc.scalar.wait_ge(unit_done, ph.unit(i, k) + 1)
                wait(nc.scalar, pair_read[ph.pair(k + 1)], ph.used_before(i, k + 1))
                nc.scalar.activation(act_g[:, s], pair_ap(p, T1), ACT.Silu).then_inc(pair_read[p], 1)
            else:
                nc.scalar.wait_ge(pair_read[p], ph.used_before(i, k) + 1)
                nc.scalar.activation(paired(a_hi)[:, j], act_a[:, s], ACT.Copy).then_inc(sem("ffn_hi"), 1)

    def ffn_lo(name, j, s):
        nc.vector.wait_ge(sem("ffn_hi"), j + (FFN[name] + 1))
        nc.vector.tensor_tensor(paired(a_lo)[:, j], act_a[:, s], paired(a_hi)[:, j].bitcast(F32), ALU.subtract)\
            .then_inc(sem("ffn_lo"), 1)

    def ffn_dve(name, ph):
        for i, k in ph.steps(nc.vector):
            split_lo(ph, i, k)
            if k % 2 == 0:
                continue
            j, s, p = i * 2 + k // 2, (k // 2) % 2, ph.pair(k)
            nc.vector.wait_ge(unit_done, ph.unit(i, k) + 1)
            gate = ph.pair(k - 1)
            nc.vector.wait_ge(pair_read[gate], ph.used_before(i, k - 1) + 1)
            nc.vector.wait_ge(sem("ffn_lo"), j + (FFN[name] + 1))
            nc.vector.tensor_tensor(act_a[:, s], pair_ap(p, T1), act_g[:, s], ALU.mult)\
                .then_inc(pair_read[p], 1)
            ffn_lo(name, j, s)

    def ffn_pe(ph, n, name):
        operands_ready(name)
        for i, k in ph.steps(nc.tensor):
            two_tiles(ph, i, k, n, u_h(n), u_l(n))

    def down_pe(name, ph):
        nc.tensor.wait_ge(sem("ffn_lo"), 2 + FFN[name] + FT // 2)
        for i, k in ph.steps(nc.tensor):
            down_unit(ph, i, k)
    def column_units(w, per):
        def unit(i, k):
            if isinstance(i, int):
                return w[:, (i * per + k) * UC:(i * per + k + 1) * UC].rearrange("(k p) n -> p k n", p=P)
            whole = w.shape[1] // (per * UC)
            return w[:, 0:whole * per * UC].rearrange("(k p) (i m n) -> p k i m n", p=P, m=per, n=UC)[:, :, i, k, :]
        return unit

    def down_units(w):
        v = w.rearrange("(k p) (i g n) -> p k i g n", p=P, g=2, n=UC)
        return lambda i, g, r: v[:, DOWN_KT[r][0]:DOWN_KT[r][0] + DOWN_KT[r][1], i, g, :]

    def begin_load(ph, i, k):
        wait(nc.sync, lo_done, ph.unit(i, k) - 1)
        nc.sync.sem_inc(sem("slot_taken"), 1)
        s = (ph.u0 + k) % 2
        return raw[s], raw_landed[s]

    def load(ph, i, k, src, nk=KT, n=UC):
        slot, landed_sem = begin_load(ph, i, k)
        nc.sync.dma_start(pw(slot, nk, n), src).then_inc(landed_sem, 16)

    def load_columns(ph, w):
        src = column_units(w, ph.body)
        for i, k in ph.steps(nc.sync):
            load(ph, i, k, src(i, k))

    def load_turns(ph, first, second):
        a, b = column_units(first, ph.body // 2), column_units(second, ph.body // 2)
        for i, k in ph.steps(nc.sync):
            load(ph, i, k, (a if k % 2 == 0 else b)(i, k // 2))

    def load_down(ph, w):
        src = down_units(w)
        for i, k in ph.steps(nc.sync):
            load(ph, i, k, src(i, k // 4, k % 4), nk=DOWN_KT[k % 4][1])

    block = ctx.enter_context(nc.Block())

    @block.sync
    def _(sp):
        nc.sync.dma_start(const[:], constants).then_inc(sem("x_landed"), 16)
        nc.sync.dma_start(x_rows[:], x[0].rearrange("(b p) d -> p b d", p=P)).then_inc(sem("x_landed"), 16)
        nc.sync.dma_start(meta_rows[:], meta_tokens_2).then_inc(sem("x_landed"), 16)
        w = ev_w_in[0]
        rope_col, b_col = QL + KVL, QL + KVL + ROPE_D
        for k in range(9):
            if k < 2:
                load(ph_in, 0, k, column_units(w[:, 0:2 * UC], 9)(0, k))
            elif k == 2:
                slot, landed_sem = begin_load(ph_in, 0, k)
                v, u = pw(slot, KT, UC), w.rearrange("(k p) n -> p k n", p=P)
                nc.sync.dma_start(v[:, :, 0:P], u[:, :, 2 * UC:rope_col]).then_inc(landed_sem, 16)
                for r in range(4):
                    at = P + r * ROPE_D
                    nc.sync.dma_start(v[:, :, at:at + ROPE_D], u[:, :, rope_col:b_col]).then_inc(landed_sem, 16)
            else:
                load(ph_in, 0, k, column_units(w[:, b_col:], 9)(0, k - 3))
        for k in range(2):
            slot, landed_sem = begin_load(ph_lat, 0, k)
            v = pw(slot, 3, 384)
            u = ev_w_uq[0].rearrange("(k p) (g a n) -> p k g a n", p=P, g=2, a=4)
            for kt in range(3):
                nc.sync.dma_start(v[:, kt, 0:256].rearrange("p (a n) -> p a n", a=4),
                                  u[:, kt, k, :, 0:NOPE]).then_inc(landed_sem, 16)
                nc.sync.dma_start(v[:, kt, 256:384].rearrange("p (a n) -> p a n", a=4),
                                  u[:, kt, k, :, NOPE:]).then_inc(landed_sem, 16)
        for k in range(2):
            slot, landed_sem = begin_load(ph_lat, 0, 2 + k)
            v = pw(slot, 2, 512)
            u = ev_w_ukv[0].rearrange("(k p) (a n) -> p k a n", p=P, a=MLA_H)
            for kt in range(2):
                nc.sync.dma_start(v[:, kt, :].rearrange("p (a n) -> p a n", a=MLA_H),
                                  u[:, kt, :, k * NOPE:(k + 1) * NOPE]).then_inc(landed_sem, 16)
        load_columns(ph_out0, ev_w_out[0])
        load_turns(ph_ffn0, w_gate[0], w_up[0])
        load_down(ph_down0, w_down[0])
        load_columns(ph_qk, od_w_qkv[0][:, 0:2 * D])
        load_columns(ph_v, od_w_qkv[0][:, 2 * D:])
        load_columns(ph_out1, od_w_out[0])
        load_turns(ph_ffn1, w_gate[1], w_up[1])
        load_down(ph_down1, w_down[1])
        w = w_in_2[0]
        load_turns(ph_conv, w[:, D:2 * D], w[:, 0:D])
        load_columns(ph_proj, w[:, 2 * D:2 * D + 8 * UC])
        slot, landed_sem = begin_load(ph_idx, 0, 0)
        v, u, at = pw(slot, KT, 2 * ID + IH), w.rearrange("(k p) n -> p k n", p=P), 2 * D + 8 * UC
        for r in range(2):
            nc.sync.dma_start(v[:, :, r * ID:(r + 1) * ID], u[:, :, at:at + ID]).then_inc(landed_sem, 16)
        nc.sync.dma_start(v[:, :, 2 * ID:], u[:, :, at + ID:at + ID + IH]).then_inc(landed_sem, 16)
        load_columns(ph_gate, w[:, at + ID + IH:])
        load_columns(ph_pw, conv_pw_out_2[0])
        load_columns(ph_wo, attn_w_o_2[0])
        load_columns(ph_merge, w_merge_out_2[0])
        load_turns(ph_ffn2, ffn_up_2[0][:, 0:DFF], ffn_up_2[0][:, DFF:])
        load_down(ph_down2, ffn_down_2[0])
        for t in range(2):
            sp.wait_ge(sem(f"out_copied{t}"), 1)
            nc.sync.dma_start(out[0, t * P:(t + 1) * P, :], out_rows[:, t, :]).then_inc(sem("out_stored"), 16)
        sp.wait_ge(sem("out_stored"), 32)

    @block.gpsimd
    def _(pool):
        pool.wait_ge(sem("gains_ready"), 1)
        nc.gpsimd.memset(q_pad[:], 0.0).then_inc(sem("zeroed"), 1)
        pool.wait_ge(sem("zeroed"), 1)
        nc.gpsimd.memset(q_pad_r[:], 0.0).then_inc(sem("zeroed"), 1)
        pool.wait_ge(sem("zeroed"), 2)
        pairs_read(pool, ph_lat)
        pool.wait_ge(sem("rope_done"), 3)

        def rope_part(i, e):
            rows = slice(32 * e, 32 * e + 32)
            return nc.gpsimd.tensor_copy(q_pad_r[rows, e, :], q_rope[rows, i, :])

        pad_heads(mla, q_nope, q_pad, rope_part)
        pad_heads(stk, q_b, q_pad)

        pairs_read(pool, ph_down0)
        rel = bass.AP(tensor=od_rel_bias.tensor, offset=od_rel_bias.offset + 1 + P,
                      ap=[[1, P], [513, C_H], [1, 2 * P]])
        nc.gpsimd.dma_start(bias_h[:], rel).then_inc(sem("bias_landed"), 16)
        nc.gpsimd.memset(q_pad_c[:], 0.0).then_inc(sem("zeroed"), 1)
        pool.wait_ge(sem("zeroed"), 3)
        pairs_read(pool, ph_v)
        pad_heads(chk, q_c, q_pad_c)

        pairs_read(pool, ph_down1)
        for n, t in enumerate((cin[:, :, 0:CONV_W - 1], stat4[:], q_cur[:])):
            nc.gpsimd.memset(t, 0.0).then_inc(sem("zeroed"), 1)
            pool.wait_ge(sem("zeroed"), 4 + n)
        pool.wait_ge(sem("rope_done"), 18)
        for n in range(IH):
            e = n % 2
            rows = slice(64 * e, 64 * e + 64)
            wait(pool, sem("idx_pad"), n)
            wait(pool, sem("idx_scored"), n - 1)
            nc.gpsimd.tensor_copy(q_cur[rows, e, :], qi[rows, n // 2, :]).then_inc(sem("idx_pad"), 1)
        pool.wait_ge(sem("idx_scored"), IH)
        pool.wait_ge(sem("idx_pad"), IH)
        for i, e in dsa.steps(pool):
            n = dsa.head(i, e)
            wait(pool, sem("at_scores"), n + (dsa.base - 1))
            wait(pool, sem("pad_done"), n + dsa.base)
            nc.gpsimd.tensor_copy(q_cur[:, e % 2, :], q_d[:, n, :]).then_inc(sem("pad_done"), 1)

    @block.scalar
    def _(act):
        rows = sem("rows_landed")
        for name, src in (("mix", g_mix), ("ffn", g_ffn), ("final", g_final.unsqueeze(0)), ("cq", ev_g_cq),
                          ("ckv", ev_g_ckv), ("mix2", mix_norm_g_2), ("ln_g", conv_ln_g_2),
                          ("ln_b", conv_ln_b_2), ("dw_b", conv_dw_b_2), ("ffn2", ffn_norm_g_2),
                          ("final2", final_norm_g_2.unsqueeze(0))):
            at, n = GAINS[name]
            nc.scalar.dma_start(gain_rows[at:at + n, :], src.rearrange("a (r p) -> (a r) p", p=P)).then_inc(rows, 16)
        taps = ffn_dw_w_2[0]
        nc.scalar.dma_start(dw_rows[:, 0, :], taps[0:2].rearrange("w (t p) -> (w t) p", p=P)).then_inc(rows, 16)
        nc.scalar.dma_start(dw_rows[0:2 * FT, 1, :], taps[2].rearrange("(t p) -> t p", p=P)).then_inc(rows, 16)
        nc.scalar.dma_start(dw_rows[2 * FT:, 1, :], ffn_dw_b_2[0].rearrange("(t p) -> t p", p=P)).then_inc(rows, 16)
        nc.scalar.dma_start(conv_rows[:], conv_dw_w_2[0]).then_inc(rows, 16)
        act.preload_act_table_set("natural_log_exp_and_others")
        for j in range(KT):
            act.wait_ge(sem("x_turned"), j + 1)
            nc.scalar.activation(h[:, j, :], ps[:, j, 0:T2], ACT.Copy).then_inc(sem("h_copied"), 1)
        for k in range(AHEAD):
            split_hi(prologue, 0, k)
        act.wait_ge(sem("consts_ready"), 1)
        act.wait_ge(sem("h_copied"), KT)
        norm_act("mix0", h_at(C1), KT, C1, D, (u_h(T1),))

        for i, k in ph_in.steps(act):
            split_hi(ph_in, i, k)
            p = ph_in.pair(k)
            act.wait_ge(unit_done, k + 1)
            src = pair_ap(p, T1)
            if k < 2:
                a = nc.scalar.activation(lat[:, 2 * k:2 * k + 2, :], src, ACT.Copy)
            elif k == 2:
                nc.scalar.activation(lat[:, 4, :], ps[:, 2 * p, 0:T1], ACT.Copy)
                a = nc.scalar.activation(k_rope[:], ps[:, 2 * p + 1, 0:T1], ACT.Copy)
            else:
                j = (k - 3) % 2
                if k < 5:
                    a = nc.scalar.activation(q_b[:, 2 * j:2 * j + 2, :], src, ACT.Copy, scale=HD ** -0.5)
                elif k < 7:
                    a = nc.scalar.activation(k_b[:, 2 * j:2 * j + 2, :], src, ACT.Copy)
                else:
                    a = nc.scalar.activation(v_b[:, :, j * UC:(j + 1) * UC], src, ACT.Copy)
            a.then_inc(pair_read[p], 1)
        pairs_read(act, ph_in)
        cols = slice(0, T1)
        norm_act("cq", lambda kt: lat[:, kt, :], 3, cols, QL, (lambda kt: lat_hi[:, kt, :],))
        act.wait_ge(sem("xl_done"), split_at["cq"] + 3)
        norm_act("ckv", lambda kt: lat[:, 3 + kt, :], 2, cols, KVL, (lambda kt: lat_hi[:, 3 + kt, :],))
        for i, k in ph_lat.steps(act):
            split_hi(ph_lat, i, k)
            p = ph_lat.pair(k)
            act.wait_ge(unit_done, ph_lat.unit(i, k) + 1)
            if k < 2:
                nc.scalar.activation(q_nope[:, 2 * k:2 * k + 2, :], pair_ap(p, T1), ACT.Copy)
                a = nc.scalar.activation(q_rope[:, k, :], ps[:, 2 * p, T1:2 * T1], ACT.Copy)
            elif k == 2:
                a = nc.scalar.activation(k_nope[:], ps[:, 2 * p:2 * p + 2, :].rearrange("p b (t n) -> p (b t) n", t=2),
                                         ACT.Copy)
            else:
                a = nc.scalar.activation(v_a[:], pair_ap(p, 512), ACT.Copy)
            a.then_inc(pair_read[p], 1)
        mla.act((NOPE + ROPE_D) ** -0.5, mla.S)

        def softplus_log(n, e):
            b0 = n + (stk.base + 1)
            bank = ps[:, stk.s_banks[e], 0:stk.width]
            act.wait_ge(sem("at_scores"), b0)
            wait(act, sem("st_sp"), n - 1)
            nc.scalar.activation(stick[:, e % 2, 0, :], bank, ACT.Abs).then_inc(sem("st_abs"), 1)
            act.wait_ge(sem("st_abs"), n + 1)
            nc.scalar.activation(stick[:, e % 2, 1, :], stick[:, e % 2, 0, :], ACT.Exp, scale=-1.0)\
                .then_inc(sem("st_exp"), 1)
            act.wait_ge(sem("st_exp"), n + 1)
            nc.scalar.activation(stick[:, e % 2, 0, :], stick[:, e % 2, 1, :], ACT.Ln, bias=1.0)\
                .then_inc(sem("st_ln"), 1)

        def stick_weights(n, e):
            act.wait_ge(sem("st_t"), n + 1)
            wait(act, sem("at_pt"), n + (stk.base - 1))
            nc.scalar.activation(p1[:, e % 2, 0:stk.width], stick[:, e % 2, 4, :], ACT.Exp).then_inc(sem("at_p"), 1)

        for i, e in stk.steps(act):
            softplus_log(stk.head(i, e), e)
            if (m := stk.head(i, e, 1)) is not None:
                stick_weights(m, (e - 1) % 4)
            if (m := stk.head(i, e, 2)) is not None:
                stk.copies(m, (e - 2) % 4)
        stick_weights(SB_H - 1, 3)
        stk.copies(SB_H - 2, 2)
        stk.copies(SB_H - 1, 3)
        turn_act(0, T1)

        splits_act(ph_out0)
        pairs_read(act, ph_out0)
        norm_act("ffn0", h_at(C1), KT, C1, D, (u_h(T1),))
        ffn_act("ffn0", ph_ffn0)
        splits_act(ph_down0)
        pairs_read(act, ph_down0)
        norm_act("mix1", h_at(C1), KT, C1, D, (u_h(T1),))

        for i, k in ph_qk.steps(act):
            split_hi(ph_qk, i, k)
            p = ph_qk.pair(k)
            act.wait_ge(unit_done, ph_qk.unit(i, k) + 1)
            nc.scalar.activation(paired(qk_c)[:, i * 4 + k], pair_ap(p, T1), ACT.Copy).then_inc(pair_read[p], 1)
        for i, k in ph_v.steps(act):
            split_hi(ph_v, i, k)
            p = ph_v.pair(k)
            act.wait_ge(unit_done, ph_v.unit(i, k) + 1)
            nc.scalar.activation(v_c[:, :, k * UC:(k + 1) * UC], pair_ap(p, UC), ACT.Copy).then_inc(pair_read[p], 1)
        chk.act(1.0, lambda e, b: biased_ap(e, b))
        turn_act(KT, T1)
        splits_act(ph_out1)
        pairs_read(act, ph_out1)
        norm_act("ffn1", h_at(C1), KT, C1, D, (u_h(T1),))
        ffn_act("ffn1", ph_ffn1)
        splits_act(ph_down1)
        pairs_read(act, ph_down1)
        norm_act("final", h_at(C1), KT, C1, D)
        act.wait_ge(sem("un_done"), norm_at["final"][1] + KT)
        norm_act("mix2", h_at(C2), KT, C2, D, (u_h(T2),))

        for i, k in ph_conv.steps(act):
            split_hi(ph_conv, i, k)
            if k % 2 == 0:
                p = ph_conv.pair(k)
                act.wait_ge(unit_done, ph_conv.unit(i, k) + 1)
                wait(act, pair_read[ph_conv.pair(k + 1)], ph_conv.used_before(i, k + 1))
                nc.scalar.activation(sg4[:, k // 2], pair_ap(p, T2), ACT.Sigmoid).then_inc(pair_read[p], 1)
        for i, k in ph_proj.steps(act):
            split_hi(ph_proj, i, k)
            p = ph_proj.pair(k)
            act.wait_ge(unit_done, ph_proj.unit(i, k) + 1)
            if k < 4:
                a = nc.scalar.activation(q_d[:, 2 * k:2 * k + 2, :], pair_ap(p, T2), ACT.Copy)
            elif k == 4:
                a = nc.scalar.activation(k_d[:], pair_ap(p, T2), ACT.Copy)
            elif k == 5:
                nc.scalar.activation(v_d[0:META, 0, :], ps[0:META, 2 * p, UC:2 * UC], ACT.Copy)
                a = nc.scalar.activation(v_d[:, 1:3, :], pair_ap(p, UC), ACT.Copy)
            else:
                a = nc.scalar.activation(qi[:, 2 * (k - 6):2 * (k - 6) + 2, :], pair_ap(p, T2), ACT.Copy)
            a.then_inc(pair_read[p], 1)
        for i, k in ph_idx.steps(act):
            split_hi(ph_idx, i, k)
            p = ph_idx.pair(k)
            act.wait_ge(unit_done, ph_idx.unit(i, k) + 1)
            nc.scalar.activation(ki[:], ps[:, 2 * p, 0:T2], ACT.Copy)
            nc.scalar.activation(wi[:, 1:3, :], ps[:, 2 * p + 1, 0:2 * IH].rearrange("p (b n) -> p b n", b=2), ACT.Copy,
                                 scale=IH ** -0.5).then_inc(pair_read[p], 1)
        for i, k in ph_gate.steps(act):
            split_hi(ph_gate, i, k)
            p = ph_gate.pair(k)
            act.wait_ge(unit_done, ph_gate.unit(i, k) + 1)
            nc.scalar.activation(paired(gates)[:, i * 4 + k], pair_ap(p, T2), ACT.Sigmoid).then_inc(pair_read[p], 1)

        for kt in range(KT):
            act.wait_ge(sem("ln_centred"), kt + 1)
            nc.scalar.activation(cin[:, kt, 0:T2], work[:, kt, :], ACT.Square).then_inc(sem("ln_sq"), 1)
        act.wait_ge(sem("ln_var"), 1)
        nc.scalar.activation(log_ms[:], ps[:, 6, 0:T2], ACT.Ln, scale=1.0 / D, bias=eps[:]).then_inc(sem("ln_log"), 1)
        act.wait_ge(sem("ln_log"), 1)
        nc.scalar.activation(rstd[:], log_ms[:], ACT.Exp, scale=-0.5).then_inc(sem("ln_rstd"), 1)
        for kt in range(KT):
            act.wait_ge(sem("ln_scaled"), kt + 1)
            g, b = GAINS["ln_g"][0] + kt, GAINS["ln_b"][0] + kt
            nc.scalar.activation(work[:, kt, :], work[:, kt, :], ACT.Silu, scale=gains[:, g:g + 1],
                                 bias=gains[:, b:b + 1]).then_inc(sem("ln_silu"), 1)
            act.wait_ge(sem("ln_silu"), kt + 1)
            nc.scalar.activation(u_hi[:, kt, :], work[:, kt, :], ACT.Copy).then_inc(sem("xh_done"), 1)
        splits_act(ph_pw)

        for n in range(IH):
            act.wait_ge(sem("idx_scored"), n + 1)
            wait(act, sem("idx_acc"), n - 1)
            nc.scalar.activation(dots(n % 2), ps[:, n % 4, 0:416], ACT.Relu, scale=ID ** -0.5)\
                .then_inc(sem("idx_relu"), 1)
        dsa.act(DH ** -0.5, dsa.S)
        turn_act(2 * KT, T2)
        splits_act(ph_wo)
        act.wait_ge(sem("wo_added"), 4)
        for kt in range(KT):
            nc.scalar.activation(u_hi[:, kt, :], work[:, kt, :], ACT.Copy).then_inc(sem("xh_done"), 1)
        splits_act(ph_merge)
        pairs_read(act, ph_merge)
        norm_act("ffn2", h_at(CF), KT, CF, D, (u_h(NF),))

        for i, k in ph_ffn2.steps(act):
            split_hi(ph_ffn2, i, k)
            j, s, p = i * 2 + k // 2, (k // 2) % 2, ph_ffn2.pair(k)
            act.wait_ge(unit_done, ph_ffn2.unit(i, k) + 1)
            act.wait_ge(sem("f2_mul"), j + 1)
            for t in range(2):
                tile = j * 2 + (t + (k % 2) * FT)
                dst = (cva if k % 2 == 0 else cvb)[:, s, t, :]
                a = nc.scalar.activation(dst, ps[:, 2 * p + t, 0:T1], ACT.Identity,
                                         scale=ffn_dw[:, 0, bass.ds(tile, 1)], bias=ffn_dw[:, 1, bass.ds(tile + 2 * FT, 1)])
            a.then_inc(sem("f2_tap0"), 1)
            if k % 2:
                first = ph_ffn2.pair(k - 1)
                act.wait_ge(pair_read[first], ph_ffn2.used_before(i, k - 1) + 1)
                nc.scalar.activation(act_g[:, s], cva[:, s], ACT.Silu).then_inc(sem("f2_silu"), 1)
                act.wait_ge(sem("f2_mul"), j + 3)
                nc.scalar.activation(paired(a_hi)[:, j], act_a[:, s], ACT.Copy).then_inc(sem("ffn_hi"), 1)
        splits_act(ph_down2)
        pairs_read(act, ph_down2)
        norm_act("final2", h_at(C1), KT, C1, D)
        act.wait_ge(sem("out_turned"), 1)
        nc.scalar.activation(out_rows[:, 0, :], ps[:, 0:2, :], ACT.Copy).then_inc(sem("out_copied0"), 1)

    @block.tensor
    def _(pe):
        pe.wait_ge(sem("x_landed"), 48)
        for j in range(KT):
            cols = slice(j * P, (j + 1) * P)
            nc.tensor.transpose(ps[:, j, 0:META], meta_rows[:, cols], ident[0:META, 0:META])
            for b in range(2):
                mm = nc.tensor.transpose(ps[:, j, META + b * P:META + (b + 1) * P], x_rows[:, b, cols], ident)
            mm.then_inc(sem("x_turned"), 1)
        pe.wait_ge(sem("rows_landed"), 16 * 15)
        pe.wait_ge(sem("h_copied"), KT)
        nc.tensor.transpose(ps[:, 0, 0:GAIN_ROWS], gain_rows[:], ident[0:GAIN_ROWS, 0:GAIN_ROWS])
        for n in range(2):
            rows = 4 * FT
            nc.tensor.transpose(ps[:, 1 + n, 0:rows], dw_rows[:, n, :], ident[0:rows, 0:rows])
        for j in range(KT):
            mm = nc.tensor.transpose(ps[:, 3, j * CONV_W:(j + 1) * CONV_W], conv_rows[:, j * P:(j + 1) * P],
                                     ident[0:CONV_W, 0:CONV_W])
        mm.then_inc(sem("rows_turned"), 1)
        pe.wait_ge(sem("consts_ready"), 1)
        norm_pe("mix0", KT, T1)
        pe.wait_ge(sem("gains_ready"), 1)
        operands_ready("mix0")
        uh, ul = u_h(T1), u_l(T1)
        for i, k in ph_in.steps(pe):
            if k < 7:
                two_tiles(ph_in, i, k, T1, uh, ul)
            else:
                by_tokens(ph_in, i, k)
        pairs_read(pe, ph_in)
        norm_pe("cq", 3, T1)
        pe.wait_ge(sem("xl_done"), split_at["cq"] + 3)
        norm_pe("ckv", 2, T1)
        operands_ready("ckv", 2)
        lh, ll = (lambda kt: lat_hi[:, kt, :]), (lambda kt: lat_lo[:, kt, :])
        for i, k in ph_lat.steps(pe):
            s, p = begin_unit(ph_lat, i, k)
            if k < 2:
                for t in range(3):
                    dst = ps[:, 2 * p + t % 2, (t // 2) * T1:(t // 2 + 1) * T1]
                    mm = feature_tile(dst, s, 3, 384, t * P, lh, ll)
            elif k == 2:
                for t in range(4):
                    dst = ps[:, 2 * p + t // 2, (t % 2) * T1:(t % 2 + 1) * T1]
                    mm = feature_tile(dst, s, 2, 512, t * P, lh, ll, x0=3)
            else:
                for b in range(2):
                    mm = token_tile(ps[:, 2 * p + b, :], s, 2, 512, slice(0, 512),
                                    lambda kt: lat_hi[:, kt, b * P:(b + 1) * P],
                                    lambda kt: lat_lo[:, kt, b * P:(b + 1) * P], x0=3)
            mm.then_inc(unit_done, 1)
        pairs_read(pe, ph_lat)
        rope_pe(c("rot32"), [q_rope[:, 0, :], q_rope[:, 1, :], k_rope[:]], T1, 0)
        pe.wait_ge(sem("rope_done"), 3)
        mla.pe(mla_scores, head_values(v_a, VD))
        stk.pe(pair_scores(q_pad, k_b, before_b), head_values(v_b, HD))
        pe.wait_ge(sem("at_oev"), MLA_H + SB_H)
        turn_pe(o1, BLOCKS1, T1)
        operands_ready("o0")
        for i, k in ph_out0.steps(pe):
            two_tiles(ph_out0, i, k, T1, uh, ul)
        pairs_read(pe, ph_out0)
        norm_pe("ffn0", KT, T1)
        ffn_pe(ph_ffn0, T1, "ffn0")
        down_pe("ffn0", ph_down0)
        pairs_read(pe, ph_down0)
        norm_pe("mix1", KT, T1)
        operands_ready("mix1")
        for i, k in ph_qk.steps(pe):
            two_tiles(ph_qk, i, k, T1, uh, ul)
        for i, k in ph_v.steps(pe):
            by_tokens(ph_v, i, k)
        pairs_read(pe, ph_v)
        chk.pe(pair_scores(q_pad_c, k_c, chunk_b), head_values(v_c, HD))
        pe.wait_ge(sem("at_oev"), chk.base + C_H)
        turn_pe(o3, BLOCKS1, T1)
        operands_ready("o1")
        for i, k in ph_out1.steps(pe):
            two_tiles(ph_out1, i, k, T1, uh, ul)
        pairs_read(pe, ph_out1)
        norm_pe("ffn1", KT, T1)
        ffn_pe(ph_ffn1, T1, "ffn1")
        down_pe("ffn1", ph_down1)
        pairs_read(pe, ph_down1)
        norm_pe("final", KT, T1)
        norm_pe("mix2", KT, T2)
        operands_ready("mix2")
        uh, ul = u_h(T2), u_l(T2)
        for i, k in ph_conv.steps(pe):
            two_tiles(ph_conv, i, k, T2, uh, ul)
        for i, k in ph_proj.steps(pe):
            if k != 5:
                two_tiles(ph_proj, i, k, T2, uh, ul)
                continue
            s, p = begin_unit(ph_proj, i, k)
            for x0, dst in ((META, ps[:, 2 * p, 0:UC]), (META + P, ps[:, 2 * p + 1, 0:UC]), (0, ps[:, 2 * p, UC:2 * UC])):
                mm = token_tile(dst, s, KT, UC, slice(0, UC), lambda kt: u_hi[:, kt, x0:x0 + P],
                                lambda kt: u_lo[:, kt, x0:x0 + P])
            mm.then_inc(unit_done, 1)
        for i, k in ph_idx.steps(pe):
            s, p = begin_unit(ph_idx, i, k)
            feature_tile(ps[:, 2 * p, 0:T2], s, KT, 2 * ID + IH, 0, uh, ul)
            for b, x0 in enumerate((META, META + P)):
                mm = token_tile(ps[:, 2 * p + 1, b * IH:(b + 1) * IH], s, KT, 2 * ID + IH, slice(2 * ID, 2 * ID + IH),
                                lambda kt: u_hi[:, kt, x0:x0 + P], lambda kt: u_lo[:, kt, x0:x0 + P])
            mm.then_inc(unit_done, 1)
        for i, k in ph_gate.steps(pe):
            two_tiles(ph_gate, i, k, T2, uh, ul)
        pairs_read(pe, ph_gate)

        for kt in range(KT):
            pe.wait_ge(sem("conv_tap"), CONV_W * (kt + 1))
            mm = nc.tensor.matmul(ps[:, 7, 0:T2], ones, work[:, kt, :], start=kt == 0, stop=kt == KT - 1)
        mm.then_inc(sem("ln_sum"), 1)
        for kt in range(KT):
            pe.wait_ge(sem("ln_sq"), kt + 1)
            mm = nc.tensor.matmul(ps[:, 6, 0:T2], ones, cin[:, kt, 0:T2], start=kt == 0, stop=kt == KT - 1)
        mm.then_inc(sem("ln_var"), 1)
        operands_ready("ln")
        for i, k in ph_pw.steps(pe):
            two_tiles(ph_pw, i, k, T2, uh, ul)
        pairs_read(pe, ph_pw)
        rope_pe(c("rot64"), [qi[:, t, :] for t in range(4)] + [ki[:]], T2, 3)
        rope_pe(c("rot128"), [q_d[:, t, :] for t in range(8)] + [k_d[:, t, :] for t in range(2)], T2, 8)
        pe.wait_ge(sem("rope_done"), 18)
        for n in range(IH):
            e = n % 2
            pe.wait_ge(sem("idx_pad"), n + 1)
            wait(pe, sem("idx_relu"), n - 3)
            nc.tensor.matmul(ps[:, n % 4, 0:144], q_cur[:, e, META:META + P], ki[:, 0:144], start=True, stop=True)
            nc.tensor.matmul(ps[:, n % 4, 144:416], q_cur[:, e, META + P:T2], ki[:], start=True, stop=True)\
                .then_inc(sem("idx_scored"), 1)
        pe.wait_ge(sem("pick_ready"), 1)
        pe.wait_ge(sem("idx_relu"), IH)

        def dsa_scores(att, i, e, n):
            pe.wait_ge(sem("pad_done"), n + (att.base + 1))
            for b, (q0, nq, keys) in enumerate(att.blocks):
                end = keys[-1][0] + keys[-1][1]
                nc.tensor.matmul(att.S(e, b), q_cur[:, e % 2, q0:q0 + nq], k_d[:, i, 0:end], start=True, stop=False)
                mask = seen_b[0:META, 0:META] if b == 0 else pick[:, 0:144] if b == 1 else pick[:, 144:416]
                mm = nc.tensor.matmul(att.S(e, b), ident_b[0:nq, 0:nq], mask, start=False, stop=True)
            return mm

        def dsa_values(n, e, b, key):
            kv = (n // 4) if isinstance(n, int) else n // 4
            return v_d[0:BLOCKS2[b][2][key][1], key, kv * DH:(kv + 1) * DH]

        dsa.pe(dsa_scores, dsa_values)
        pe.wait_ge(sem("at_oev"), dsa.base + 8)
        turn_pe(o4, BLOCKS2, T2)
        operands_ready("o2")
        for i, k in ph_wo.steps(pe):
            two_tiles(ph_wo, i, k, T2, uh, ul)
        operands_ready("merge")
        for i, k in ph_merge.steps(pe):
            two_tiles(ph_merge, i, k, T2, uh, ul)
        pairs_read(pe, ph_merge)
        norm_pe("ffn2", KT, NF)
        ffn_pe(ph_ffn2, NF, "ffn2")
        down_pe("ffn2", ph_down2)
        pairs_read(pe, ph_down2)
        norm_pe("final2", KT, T1)
        pe.wait_ge(sem("un_done"), norm_at["final2"][1] + KT)
        for t in range(2):
            for j in range(KT):
                mm = nc.tensor.transpose(ps[:, 2 * t + j // 4, (j % 4) * P:(j % 4 + 1) * P],
                                         work[:, j, t * P:(t + 1) * P], ident)
            mm.then_inc(sem("out_turned"), 1)

    @block.vector
    def _(dve):
        links = [0]

        def link(ins):
            links[0] += 1
            ins.then_inc(sem("vector_link"), 1)
            dve.wait_ge(sem("vector_link"), links[0])

        dve.sem_inc(sem("ffn_lo"), 2)
        dve.sem_inc(sem("f2_mul"), 2)
        dve.wait_ge(sem("x_landed"), 48)
        nc.vector.memset(eps[:], EPS)
        for n, name in enumerate(("ident", "chunk_mask", "before_mask", "seen_mask")):
            a = nc.vector.tensor_copy(masks[:, n, :], c(name))
        a.then_inc(sem("consts_ready"), 1)
        dve.wait_ge(sem("rows_turned"), 1)
        nc.vector.tensor_copy(gains[:], ps[:, 0, 0:GAIN_ROWS])
        nc.vector.tensor_copy(ffn_dw[:], ps[:, 1:3, 0:4 * FT])
        nc.vector.tensor_copy(conv_w[:], ps[:, 3, 0:KT * CONV_W].rearrange("p (k w) -> p k w", w=CONV_W))\
            .then_inc(sem("gains_ready"), 1)
        for k in range(AHEAD):
            split_lo(prologue, 0, k)
        dve.wait_ge(sem("gains_ready"), 1)
        dve.wait_ge(sem("h_copied"), KT)
        norm_dve("mix0", h_at(C1), ("mix", 0), KT, T1, (u_h(T1), u_l(T1)))
        for i, k in ph_in.steps(dve):
            split_lo(ph_in, i, k)
        norm_dve("cq", lambda kt: lat[:, kt, :], ("cq", 0), 3, T1,
                 (lambda kt: lat_hi[:, kt, :], lambda kt: lat_lo[:, kt, :]))
        norm_dve("ckv", lambda kt: lat[:, 3 + kt, :], ("ckv", 0), 2, T1,
                 (lambda kt: lat_hi[:, 3 + kt, :], lambda kt: lat_lo[:, 3 + kt, :]))
        for i, k in ph_lat.steps(dve):
            split_lo(ph_lat, i, k)
        pairs_read(dve, ph_lat)
        rope_dve([q_rope[:, 0, :], q_rope[:, 1, :], k_rope[:]], c("cos32"), c("sin32"), T1, 0, rope_t)
        mla.dve((NOPE + ROPE_D) ** -0.5, mla.S)

        def softplus_sums(n, e):
            z = ps[:, stk.s_banks[e], 0:stk.width]
            st = stick[:, e % 2]
            dve.wait_ge(sem("st_ln"), n + 1)
            wait(dve, sem("st_scan"), n - 1)
            nc.vector.scalar_tensor_tensor(out=st[:, 2, :], in0=z, scalar=0.0, in1=st[:, 0, :], op0=ALU.max, op1=ALU.add)\
                .then_inc(sem("st_sp"), 1)
            dve.wait_ge(sem("st_sp"), n + 1)
            wait(dve, sem("st_t"), n - 1)
            for b, (_, _, keys) in enumerate(BLOCKS1):
                lo, hi = stk.cols[b], stk.cols[b] + sum(m for _, m in keys)
                rev = lambda t: t[:, lo:hi][:, ::-1]
                a = nc.vector.tensor_tensor_scan(rev(st[:, 3, :]), wide_ones[:, 0:hi - lo], rev(st[:, 2, :]), 0.0,
                                                 ALU.mult, ALU.add)
            a.then_inc(sem("st_scan"), 1)
            dve.wait_ge(sem("st_scan"), n + 1)
            wait(dve, sem("at_p"), n + (stk.base - 1))
            nc.vector.tensor_tensor(st[:, 4, :], z, st[:, 3, :], ALU.subtract).then_inc(sem("st_t"), 1)

        def stick_out(n, e):
            dve.wait_ge(sem("at_o"), n + (stk.base + 1))
            for b in range(2):
                a = nc.vector.tensor_copy(stk.o(n, b), stk.O(e, b))
            a.then_inc(sem("at_oev"), 1)

        for i, e in stk.steps(dve):
            softplus_sums(stk.head(i, e), e)
            if (m := stk.head(i, e, 3)) is not None:
                stick_out(m, (e - 3) % 4)
        for m in range(SB_H - 3, SB_H):
            stick_out(m, m % 4)
        turn_dve("o0", T1)
        residual_dve(ph_out0, C1)
        norm_dve("ffn0", h_at(C1), ("ffn", 0), KT, T1, (u_h(T1), u_l(T1)))
        ffn_dve("ffn0", ph_ffn0)
        residual_dve(ph_down0, C1, group=4)
        norm_dve("mix1", h_at(C1), ("mix", KT), KT, T1, (u_h(T1), u_l(T1)))
        for i, k in ph_qk.steps(dve):
            split_lo(ph_qk, i, k)
        for i, k in ph_v.steps(dve):
            split_lo(ph_v, i, k)
        dve.wait_ge(sem("bias_landed"), 16)

        def add_bias(att, n, e):
            wait(dve, sem("at_p"), n + (att.base - 1))
            hb = bias_h[:, n, :]
            nc.vector.scalar_tensor_tensor(out=biased_ap(e, 0)[:, ::-1], in0=att.S(e, 0)[:, ::-1], scalar=HD ** -0.5,
                                           in1=hb[:, 0:P], op0=ALU.mult, op1=ALU.add)
            nc.vector.scalar_tensor_tensor(out=biased_ap(e, 1)[:, ::-1], in0=att.S(e, 1)[:, ::-1], scalar=HD ** -0.5,
                                           in1=hb, op0=ALU.mult, op1=ALU.add).then_inc(sem("biased"), 1)
            dve.wait_ge(sem("biased"), n + 1)

        chk.dve(1.0, lambda e, b: biased_ap(e, b), add_bias)
        turn_dve("o1", T1)
        residual_dve(ph_out1, C1)
        norm_dve("ffn1", h_at(C1), ("ffn", KT), KT, T1, (u_h(T1), u_l(T1)))
        ffn_dve("ffn1", ph_ffn1)
        residual_dve(ph_down1, C1, group=4)
        norm_dve("final", h_at(C1), ("final", 0), KT, T1, into=h_at(C1))
        dve.wait_ge(sem("un_done"), norm_at["final"][1] + KT)
        norm_dve("mix2", h_at(C2), ("mix2", 0), KT, T2, (u_h(T2), u_l(T2)))

        for i, k in ph_conv.steps(dve):
            split_lo(ph_conv, i, k)
            if k % 2:
                p, gate = ph_conv.pair(k), ph_conv.pair(k - 1)
                dve.wait_ge(unit_done, ph_conv.unit(i, k) + 1)
                dve.wait_ge(pair_read[gate], ph_conv.used_before(i, k - 1) + 1)
                nc.vector.tensor_tensor(paired(cin)[:, i * 2 + k // 2, :, CONV_W - 1:], pair_ap(p, T2), sg4[:, k // 2],
                                        ALU.mult).then_inc(pair_read[p], 1)

        def conv_half(tile, half):
            for w in range(16) if half == 0 else range(16, CONV_W):
                src, tap = cin[:, tile, w:w + T2], conv_w[:, tile, w:w + 1]
                if w == 0:
                    a = nc.vector.tensor_scalar(work[:, tile, :], src, tap, gains[:, bass.ds(tile + GAINS["dw_b"][0], 1)],
                                                ALU.mult, ALU.add)
                else:
                    dve.wait_ge(sem("conv_tap"), tile * CONV_W + w)
                    a = nc.vector.scalar_tensor_tensor(out=work[:, tile, :], in0=src, scalar=tap, in1=work[:, tile, :],
                                                       op0=ALU.mult, op1=ALU.add)
                a.then_inc(sem("conv_tap"), 1)

        pairs_read(dve, ph_conv)
        dve.wait_ge(sem("zeroed"), 6)
        for i, k in ph_proj.steps(dve):
            split_lo(ph_proj, i, k)
            conv_half(k // 2, k % 2)
        for i, k in ph_idx.steps(dve):
            split_lo(ph_idx, i, k)
        for i, k in ph_gate.steps(dve):
            split_lo(ph_gate, i, k)
            conv_half(i * 2 + (4 + k // 2), k % 2)

        dve.wait_ge(sem("ln_sum"), 1)
        link(nc.vector.tensor_scalar(log_ms[:], ps[:, 7, 0:T2], 1.0 / D, None, ALU.mult))
        for kt in range(KT):
            nc.vector.tensor_tensor(work[:, kt, :], work[:, kt, :], log_ms[:], ALU.subtract).then_inc(sem("ln_centred"), 1)
        dve.wait_ge(sem("ln_rstd"), 1)
        for kt in range(KT):
            nc.vector.tensor_tensor(work[:, kt, :], work[:, kt, :], rstd[:], ALU.mult).then_inc(sem("ln_scaled"), 1)
        for kt in range(KT):
            dve.wait_ge(sem("xh_done"), split_at["ln"] + kt + 1)
            nc.vector.tensor_tensor(u_lo[:, kt, :], work[:, kt, :], u_hi[:, kt, :].bitcast(F32), ALU.subtract)\
                .then_inc(sem("xl_done"), 1)
        dve.wait_ge(sem("xl_done"), split_at["ln"] + KT)
        for i, k in ph_pw.steps(dve):
            split_lo(ph_pw, i, k)
            p = ph_pw.pair(k)
            dve.wait_ge(unit_done, ph_pw.unit(i, k) + 1)
            nc.vector.tensor_tensor(paired(work)[:, k], pair_ap(p, T2), paired(gates)[:, k], ALU.mult)\
                .then_inc(pair_read[p], 1)
        rope_dve([qi[:, t, :] for t in range(4)] + [ki[:]], c("cos64"), c("sin64"), T2, 3, rope4)
        rope_dve([q_d[:, t, :] for t in range(8)] + [k_d[:, t, :] for t in range(2)], c("cos128"), c("sin128"), T2, 8, rope4)

        spans = ((1, 0, 144), (2, 144, 416))
        for n in range(IH):
            dve.wait_ge(sem("idx_relu"), n + 1)
            wait(dve, sem("idx_acc"), n)
            for b, lo, hi in spans:
                if n == 0:
                    a = nc.vector.tensor_scalar(acc[:, lo:hi], dots(0)[:, lo:hi], wi[:, b, 0:1], None, ALU.mult)
                else:
                    a = nc.vector.scalar_tensor_tensor(out=acc[:, lo:hi], in0=dots(n % 2)[:, lo:hi], scalar=wi[:, b, n:n + 1],
                                                       in1=acc[:, lo:hi], op0=ALU.mult, op1=ALU.add)
            a.then_inc(sem("idx_acc"), 1)
        dve.wait_ge(sem("idx_acc"), IH)
        for lo, hi in ((META, 144), (288, 416)):
            nc.vector.tensor_tensor(acc[:, lo:hi], acc[:, lo:hi], c("seen_mask"), ALU.add)
        nc.vector.memset(acc[:, 0:META], BONUS)
        link(nc.vector.memset(acc[:, 144:144 + META], BONUS))
        rounds = (TOPK - 1) // 8
        for r in range(rounds + 1):
            for b, lo, hi in spans:
                src = acc if r == 0 else left
                a = nc.vector.max(top8[:, b - 1, :], src[:, lo:hi])
            link(a)
            if r < rounds:
                for b, lo, hi in spans:
                    src = acc if r == 0 else left
                    a = nc.vector.match_replace(left[:, lo:hi], top8[:, b - 1, :], src[:, lo:hi], LOWEST)
                link(a)
        last = (TOPK - 1) % 8
        for b, lo, hi in spans:
            thr = top8[:, b - 1, last:last + 1]
            nc.vector.tensor_scalar(above[:, lo:hi], acc[:, lo:hi], thr, None, ALU.is_gt)
            a = nc.vector.tensor_scalar(equal[:, lo:hi], acc[:, lo:hi], thr, None, ALU.is_equal)
        link(a)
        for b, lo, hi in spans:
            nc.vector.reduce_sum(need[:, b - 1:b], above[:, lo:hi], AX)
            a = nc.vector.tensor_tensor_scan(left[:, lo:hi], wide_ones[:, 0:hi - lo], equal[:, lo:hi], 0.0, ALU.mult, ALU.add)
        link(a)
        link(nc.vector.tensor_scalar(need[:], need[:], -1.0, float(TOPK), ALU.mult, ALU.add))
        for b, lo, hi in spans:
            a = nc.vector.scalar_tensor_tensor(out=left[:, lo:hi], in0=left[:, lo:hi], scalar=need[:, b - 1:b],
                                               in1=equal[:, lo:hi], op0=ALU.is_le, op1=ALU.mult)
        link(a)
        link(nc.vector.tensor_tensor(left, left, above, ALU.add))
        link(nc.vector.tensor_scalar(left, left, -NEG, NEG, ALU.mult, ALU.add))
        for lo, hi in ((META, 144), (288, 416)):
            a = nc.vector.tensor_tensor(left[:, lo:hi], left[:, lo:hi], c("seen_mask"), ALU.add)
        link(a)
        nc.vector.tensor_copy(pick[:], left).then_inc(sem("pick_ready"), 1)

        dsa.dve(DH ** -0.5, dsa.S)
        turn_dve("o2", T2)
        for i, k in ph_wo.steps(dve):
            split_lo(ph_wo, i, k)
            p = ph_wo.pair(k)
            dve.wait_ge(unit_done, ph_wo.unit(i, k) + 1)
            wait(dve, sem("wo_added"), k - 1)
            nc.vector.tensor_tensor(sg4[:, k % 2], pair_ap(p, T2), paired(gates)[:, 4 + k], ALU.mult)\
                .then_inc(pair_read[p], 1)
            dve.wait_ge(pair_read[p], ph_wo.used_before(i, k) + 1)
            nc.vector.tensor_tensor(paired(work)[:, k], paired(work)[:, k], sg4[:, k % 2], ALU.add)\
                .then_inc(sem("wo_added"), 1)
        dve.wait_ge(sem("wo_added"), 4)
        for kt in range(KT):
            dve.wait_ge(sem("xh_done"), split_at["merge"] + kt + 1)
            nc.vector.tensor_tensor(u_lo[:, kt, :], work[:, kt, :], u_hi[:, kt, :].bitcast(F32), ALU.subtract)\
                .then_inc(sem("xl_done"), 1)
        residual_dve(ph_merge, C2)
        norm_dve("ffn2", h_at(CF), ("ffn2", 0), KT, NF, (u_h(NF), u_l(NF)))

        for i, k in ph_ffn2.steps(dve):
            split_lo(ph_ffn2, i, k)
            j, s, p = i * 2 + k // 2, (k // 2) % 2, ph_ffn2.pair(k)
            cv = cva if k % 2 == 0 else cvb
            dve.wait_ge(sem("f2_tap0"), ph_ffn2.unit(i, k) - ph_ffn2.u0 + 1)
            for w in (1, 2):
                for t in range(2):
                    tile = j * 2 + (t + (k % 2) * FT)
                    tap = ffn_dw[:, 0, bass.ds(tile + 2 * FT, 1)] if w == 1 else ffn_dw[:, 1, bass.ds(tile, 1)]
                    a = nc.vector.scalar_tensor_tensor(out=cv[:, s, t, :], in0=ps[:, 2 * p + t, w:w + T1], scalar=tap,
                                                       in1=cv[:, s, t, :], op0=ALU.mult, op1=ALU.add)
                if w == 1:
                    a.then_inc(sem("f2_tap1"), 1)
                    dve.wait_ge(sem("f2_tap1"), ph_ffn2.unit(i, k) - ph_ffn2.u0 + 1)
            a.then_inc(pair_read[p], 1)
            if k % 2:
                dve.wait_ge(sem("f2_silu"), j + 1)
                dve.wait_ge(pair_read[p], ph_ffn2.used_before(i, k) + 1)
                dve.wait_ge(sem("ffn_lo"), j + (FFN["ffn2"] + 1))
                nc.vector.tensor_tensor(act_a[:, s], act_g[:, s], cvb[:, s], ALU.mult).then_inc(sem("f2_mul"), 1)
                ffn_lo("ffn2", j, s)
        residual_dve(ph_down2, C1, group=4)
        norm_dve("final2", h_at(C1), ("final2", 0), KT, T1)
        dve.wait_ge(sem("out_turned"), 2)
        nc.vector.tensor_copy(out_rows[:, 1, :], ps[:, 2:4, :]).then_inc(sem("out_copied1"), 1)
    ctx.close()


_INS = ["x", "ev_w_in", "ev_g_cq", "ev_w_uq", "ev_g_ckv", "ev_w_ukv", "ev_w_out", "od_w_qkv", "od_rel_bias",
        "od_w_out", "g_mix", "g_ffn", "w_gate", "w_up", "w_down", "g_final", "meta_tokens_2", "mix_norm_g_2",
        "w_in_2", "conv_ln_g_2", "conv_ln_b_2", "conv_dw_w_2", "conv_dw_b_2", "conv_pw_out_2", "attn_w_o_2",
        "w_merge_out_2", "ffn_norm_g_2", "ffn_up_2", "ffn_dw_w_2", "ffn_dw_b_2", "ffn_down_2", "final_norm_g_2"]


def kernel(**inputs):
    import concourse.bacc as bacc
    from concourse.bass_utils import run_bass_kernel_spmd

    nc = bacc.Bacc("TRN2", target_bir_lowering=False, num_devices=1)
    arrays, args = {}, {}
    for name in _INS:
        a = np.ascontiguousarray(inputs[name])
        arrays[f"in_{name}"] = a
        args[name] = nc.dram_tensor(f"in_{name}", a.shape, mybir.dt.from_np(a.dtype), kind="ExternalInput").ap()
    constants, where = shape_constants()
    arrays["in_constants"] = constants
    args["constants"] = nc.dram_tensor("in_constants", constants.shape, F32, kind="ExternalInput").ap()
    args["out"] = nc.dram_tensor("out_0", (1, SEQ, D), F32, kind="ExternalOutput").ap()
    build(nc, where=where, **args)
    r = run_bass_kernel_spmd(nc, [arrays], core_ids=[0])
    return r.results[0]["out_0"]
```

```python
from contextlib import ExitStack

import numpy as np

import concourse.bass as bass
from concourse import mybir

F32 = mybir.dt.float32
F32R = mybir.dt.float32r
BF16 = mybir.dt.bfloat16
ACT = mybir.ActivationFunctionType
ALU = mybir.AluOpType
AX = mybir.AxisListType.X

P = 128
SEQ, D, META = 256, 1024, 16
T1, T2 = SEQ, SEQ + META
KT = D // P
DFF = 2816
FT = DFF // P
UC = 256
UNIT = KT * UC
RING, AHEAD, RAW = 4, 3, 4
EPS = 1e-6

MLA_H, NOPE, ROPE_D, VD = 8, 64, 32, 64
QL, KVL = 384, 256
SB_H, C_H, HD = 8, 16, 64
DH, KVH, IH, ID = 128, 2, 8, 64
TOPK = min(256, T2 // 4)
CONV_W, CHUNK = 31, 64
NEG, LOWEST, BONUS = -1e30, -3e38, 1e30

DOWN_KT = [(0, 6), (6, 6), (12, 5), (17, 5)]
DOWN_WIDTHS = [n * UC for _ in range(D // UC) for _, n in DOWN_KT]

BLOCKS1 = [(0, P, [(0, P)]), (P, P, [(0, P), (P, P)])]
BLOCKS2 = [
    (0, META, [(0, META)]),
    (META, P, [(0, META), (META, P)]),
    (META + P, P, [(0, META), (META, P), (META + P, P)]),
]

GAINS = {}
for _name, _rows in (("mix", 16), ("ffn", 16), ("final", 8), ("cq", 3), ("ckv", 2), ("mix2", 8),
                     ("ln_g", 8), ("ln_b", 8), ("dw_b", 8), ("ffn2", 8), ("final2", 8)):
    GAINS[_name] = (sum(r for _, r in GAINS.values()), _rows)
GAIN_ROWS = sum(r for _, r in GAINS.values())


def shape_constants():
    def half_rotation(dim):
        r = np.zeros((P, P), np.float32)
        for base in range(0, P, dim):
            for i in range(dim // 2):
                r[base + i, base + dim // 2 + i] = -1.0
                r[base + dim // 2 + i, base + i] = 1.0
        return r.T

    def tables(dim, n):
        half = dim // 2
        inv = np.float32(10000.0) ** (-np.arange(0, dim, 2, dtype=np.float32) / np.float32(dim))
        ang = np.arange(n, dtype=np.float32)[:, None] * inv[None, :].astype(np.float32)
        rows = (np.arange(P) % dim) % half
        return np.cos(ang).T[rows], np.sin(ang).T[rows]

    q, k = np.arange(P)[:, None], np.arange(P)[None, :]
    parts = {
        "ident": np.eye(P), "ones": np.ones((P, T2)), "zeros": np.zeros((P, T1)),
        "rot32": half_rotation(32), "rot128": half_rotation(128), "rot64": half_rotation(64),
        "chunk_mask": np.where(k // CHUNK <= q // CHUNK, 0.0, NEG),
        "before_mask": np.where(k < q, 0.0, NEG),
        "seen_mask": np.where(k <= q, 0.0, LOWEST),
    }
    for name, dim, n in (("32", 32, T1), ("128", 128, T2), ("64", 64, T2)):
        parts["cos" + name], parts["sin" + name] = tables(dim, n)
    where, at = {}, 0
    for name, a in parts.items():
        where[name] = (at, a.shape[1])
        at += a.shape[1]
    return np.concatenate([a.astype(np.float32) for a in parts.values()], axis=1), where


def wait(eng, sem, value):
    if isinstance(value, int) and value <= 0:
        return
    eng.wait_ge(sem, value)


class Phase:

    def __init__(self, plan, units, body, group=1, dmas=None, peel=0, pairs=4, widths=None):
        self.u0, self.units, self.body, self.group = plan["units"], units, body, group
        self.turns, self.rest = divmod(units, body)
        self.peel, self.pairs = peel, pairs
        self.groups = body // group
        self.used = list(plan["used"])
        self.dmas = dmas or [1] * units
        self.widths = widths or [UNIT] * units
        plan["units"] += units
        for n, d in enumerate(self.dmas):
            plan["loads"][(self.u0 + n) % RAW] += 16 * d
        for n in range(units // group):
            plan["used"][n % self.groups % pairs] += 1
        self.used_after = list(plan["used"])
        plan["phases"].append(self)

    def steps(self, eng):
        looped = self.turns - self.peel if self.turns - self.peel > 1 else 0
        if looped:
            with eng.Fori(0, looped) as i:
                for k in range(self.body):
                    yield i, k
        for i in range(looped, self.turns):
            for k in range(self.body):
                yield i, k
        for k in range(self.rest):
            yield self.turns, k

    def unit(self, i, k):
        return i * self.body + (self.u0 + k)

    def pair(self, k):
        return k // self.group % self.groups % self.pairs

    def used_before(self, i, k):
        per_turn = max(1, self.groups // self.pairs)
        return i * per_turn + (self.used[self.pair(k)] + k // self.group % self.groups // self.pairs)


def build(nc, x, ev_w_in, ev_g_cq, ev_w_uq, ev_g_ckv, ev_w_ukv, ev_w_out, od_w_qkv, od_rel_bias,
          od_w_out, g_mix, g_ffn, w_gate, w_up, w_down, g_final, meta_tokens_2, mix_norm_g_2,
          w_in_2, conv_ln_g_2, conv_ln_b_2, conv_dw_w_2, conv_dw_b_2, conv_pw_out_2, attn_w_o_2,
          w_merge_out_2, ffn_norm_g_2, ffn_up_2, ffn_dw_w_2, ffn_dw_b_2, ffn_down_2,
          final_norm_g_2, constants, where, out, debug=None):
    ctx = ExitStack()
    sems = {}

    def sem(name):
        if name not in sems:
            sems[name] = ctx.enter_context(nc.semaphore(name))
        return sems[name]

    def sb(name, shape, dt=F32, scope=None):
        return (scope or ctx).enter_context(nc.sbuf_tensor(name, shape, dt))

    raw = [sb(f"raw{s}", [P, UNIT]) for s in range(RAW)]
    w_hi = [sb(f"w_hi{s}", [P, UNIT], F32R) for s in range(RING)]
    w_lo = [sb(f"w_lo{s}", [P, UNIT], F32R) for s in range(RING)]
    h = sb("h", [P, KT, T2])
    u_hi = sb("u_hi", [P, KT, T2], F32R)
    u_lo = sb("u_lo", [P, KT, T2], F32R)
    work = sb("work", [P, KT, T2])
    const = sb("const", [P, constants.shape[1]])
    masks = sb("masks", [P, 4, P], BF16)
    gains = sb("gains", [P, GAIN_ROWS])
    ffn_dw = sb("ffn_dw", [P, 2, 2 * FT * 2])
    conv_w = sb("conv_w", [P, KT, CONV_W])
    eps = sb("eps", [P, 1])
    log_ms = sb("log_ms", [P, T2])
    rstd = sb("rstd", [P, T2])

    def c(name):
        at, n = where[name]
        return const[:, at:at + n]

    ident, wide_ones = c("ident"), c("ones")
    ones = wide_ones[:, 0:P]
    ident_b, chunk_b, before_b, seen_b = (masks[:, n, :] for n in range(4))

    with ExitStack() as s:
        x_rows = sb("x_rows", [P, 2, D], scope=s)
        meta_rows = sb("meta_rows", [META, D], scope=s)
        gain_rows = sb("gain_rows", [GAIN_ROWS, P], scope=s)
        dw_rows = sb("dw_rows", [2 * 2 * FT, 2, P], scope=s)
        conv_rows = sb("conv_rows", [CONV_W, D], scope=s)
    with ExitStack() as s:
        p1 = sb("p1", [P, 2, 512], scope=s)
        pt1 = sb("pt1", [P, 2, 1024], scope=s)
        stat1 = sb("stat1", [P, 2, 4, 3], scope=s)
        k_rope = sb("k_rope", [P, T1], scope=s)
        with ExitStack() as t:
            q_nope = sb("q_nope", [P, 4, T1], scope=t)
            q_rope = sb("q_rope", [P, 2, T1], scope=t)
            k_nope = sb("k_nope", [P, 4, T1], scope=t)
            v_a = sb("v_a", [P, 2, MLA_H * VD], scope=t)
            lat = sb("lat", [P, 5, T1], scope=t)
        stick = sb("stick", [P, 2, 5, 384], scope=s)
        sb("mla_place", [P, 19 * T1 - 10 * 384], scope=s)
        q_b = sb("q_b", [P, 4, T1], scope=s)
        k_b = sb("k_b", [P, 4, T1], scope=s)
        v_b = sb("v_b", [P, 2, SB_H * HD], scope=s)
        q_pad = sb("q_pad", [P, 4, T1], scope=s)
        q_pad_r = sb("q_pad_r", [P, 4, T1], scope=s)
        rope_t = sb("rope_t", [P, 2, T2], scope=s)
    with ExitStack() as s:
        a_hi = sb("a_hi", [P, FT, T1], F32R, scope=s)
        a_lo = sb("a_lo", [P, FT, T1], F32R, scope=s)
        act_g = sb("act_g", [P, 2, 2, T1], scope=s)
        act_a = sb("act_a", [P, 2, 2, T1], scope=s)
        cva = sb("cva", [P, 2, 2, T1], scope=s)
        cvb = sb("cvb", [P, 2, 2, T1], scope=s)
    with ExitStack() as s:
        p3 = sb("p3", [P, 2, 512], scope=s)
        pt3 = sb("pt3", [P, 2, 1024], scope=s)
        stat3 = sb("stat3", [P, 2, 4, 3], scope=s)
        qk_c = sb("qk_c", [P, 16, T1], scope=s)
        q_c, k_c = qk_c[:, 0:8, :], qk_c[:, 8:16, :]
        v_c = sb("v_c", [P, 2, D], scope=s)
        q_pad_c = sb("q_pad_c", [P, 4, T1], scope=s)
        biased = sb("biased", [P, 2, 512], scope=s)
        bias_h = sb("bias_h", [P, C_H, 2 * P], scope=s)
    with ExitStack() as s:
        with ExitStack() as t:
            p4 = sb("p4", [P, 2, 512], scope=t)
        with ExitStack() as t:
            rope4 = sb("rope4", [P, 2, T2], scope=t)
        sb("p4_place", [P, 2, 512], scope=s)
        stat4 = sb("stat4", [P, 2, 4, 3], scope=s)
        gates = sb("gates", [P, 2 * KT, T2], scope=s)
        q_d = sb("q_d", [P, 8, T2], scope=s)
        k_d = sb("k_d", [P, KVH, T2], scope=s)
        v_d = sb("v_d", [P, 3, KVH * DH], scope=s)
        wi = sb("wi", [P, 3, IH], scope=s)
        q_cur = sb("q_cur", [P, 2, T2], scope=s)
        pick = sb("pick", [P, 416], BF16, scope=s)
        top8 = sb("top8", [P, 2, 8], scope=s)
        need = sb("need", [P, 2], scope=s)
        with ExitStack() as t:
            pt4 = sb("pt4", [P, 2, 1024], scope=t)
        qi = sb("qi", [P, IH * ID // P, T2], scope=s)
        ki = sb("ki", [P, T2], scope=s)
        sg4 = sb("sg4", [P, 2, 2, T2], scope=s)
        cin = sb("cin", [P, KT, CONV_W - 1 + T2], scope=s)
        o_meta = sb("o_meta", [META, D], scope=s)
    with ExitStack() as s:
        out_rows = sb("out_rows", [P, 2, D], scope=s)
    o1 = o3 = work[:].rearrange("p a b -> p (a b)")[:, 0:2 * D].rearrange("p (b d) -> p b d", b=2)
    lat_hi, lat_lo = u_hi[:, 0:5, 0:T1], u_lo[:, 0:5, 0:T1]
    picks = gates[:, KT:2 * KT, :].rearrange("p a b -> p (a b)")
    acc, left, above, equal = (picks[:, n * 416:(n + 1) * 416] for n in range(4))
    sg_flat = sg4[:].rearrange("p a b c -> p (a b c)")

    def dots(n):
        return sg_flat[:, n * 416:(n + 1) * 416]

    def biased_ap(e, b):
        return biased[:, e % 2, chk.cols[b]:chk.cols[b] + (b + 1) * P]

    ps = ctx.enter_context(nc.psum_tensor("ps", [P, 8, 512], F32))

    def paired(t):
        return t.rearrange("p (j t) n -> p j t n", t=2)

    def pw(s, nk, n):
        return s[:, 0:nk * n].rearrange("p (k n) -> p k n", k=nk)

    plan = {"units": 0, "loads": [0] * RAW, "used": [0, 0, 0, 0], "phases": []}
    ph_in = Phase(plan, 9, 9, dmas=[1, 1, 5, 1, 1, 1, 1, 1, 1])
    ph_lat = Phase(plan, 4, 4, dmas=[6, 6, 2, 2], widths=[3 * 384] * 2 + [2 * 512] * 2)
    ph_out0 = Phase(plan, 4, 4, pairs=3)
    ph_ffn0 = Phase(plan, 2 * DFF // UC, 4)
    ph_down0 = Phase(plan, 16, 8, group=4, widths=DOWN_WIDTHS)
    ph_qk = Phase(plan, 8, 4)
    ph_v = Phase(plan, 4, 4)
    ph_out1 = Phase(plan, 4, 4, pairs=3)
    ph_ffn1 = Phase(plan, 2 * DFF // UC, 4)
    ph_down1 = Phase(plan, 16, 8, group=4, widths=DOWN_WIDTHS)
    ph_conv = Phase(plan, 8, 8, pairs=2)
    ph_idx = Phase(plan, 3, 3, dmas=[3, 1, 1], widths=[KT * (2 * ID + IH), UNIT, UNIT], pairs=2)
    ph_proj = Phase(plan, 6, 6, pairs=2)
    ph_gate = Phase(plan, 4, 4, pairs=2)
    ph_gate_b = Phase(plan, 4, 4, pairs=1)
    ph_wo = Phase(plan, 4, 4, pairs=3)
    ph_pw = Phase(plan, 4, 4)
    ph_merge = Phase(plan, 4, 4, pairs=3)
    ph_ffn2 = Phase(plan, 2 * DFF // UC, 4)
    ph_down2 = Phase(plan, 16, 8, group=4, peel=1, widths=DOWN_WIDTHS)
    units = plan["units"]
    landed, widths, count = [], [], [0] * RAW
    for ph in plan["phases"]:
        widths += ph.widths
        for n, d in enumerate(ph.dmas):
            count[(ph.u0 + n) % RAW] += 16 * d
            landed.append(count[(ph.u0 + n) % RAW])

    raw_landed = [sem(f"raw_landed{n}") for n in range(RAW)]
    hi_done, lo_done, unit_done = sem("hi_done"), sem("lo_done"), sem("unit_done")
    pair_read = [sem(f"pair_read{n}") for n in range(4)]

    def pairs_read(eng, ph):
        for n in range(4):
            wait(eng, pair_read[n], ph.used_after[n])

    def split_unit(ph, i, k):
        t = ph.u0 + (i * ph.body if isinstance(i, int) else 0) + k + AHEAD
        if isinstance(i, int):
            return (0, t, widths[t]) if t < units else None
        turns = range(ph.turns - ph.peel)
        return i, t, max(widths[t + j * ph.body] for j in turns)

    def split_hi(ph, i, k):
        if (u := split_unit(ph, i, k)) is None:
            return
        turn, t, n = u
        nc.scalar.wait_ge(raw_landed[t % RAW], turn * (16 * ph.body // RAW) + landed[t])
        wait(nc.scalar, unit_done, turn * ph.body + (t - (RING - 1)))
        nc.scalar.activation(w_hi[t % RING][:, 0:n], raw[t % RAW][:, 0:n], ACT.Copy).then_inc(hi_done, 1)

    def split_lo(ph, i, k):
        if (u := split_unit(ph, i, k)) is None:
            return
        turn, t, n = u
        nc.vector.wait_ge(hi_done, turn * ph.body + (t + 1))
        nc.vector.tensor_tensor(w_lo[t % RING][:, 0:n], raw[t % RAW][:, 0:n], w_hi[t % RING][:, 0:n].bitcast(F32),
                                ALU.subtract).then_inc(lo_done, 1)

    prologue = Phase({"units": -AHEAD, "loads": [0] * RAW, "used": [0] * 4, "phases": []}, AHEAD, AHEAD)

    norm_at, norm_n = {}, [0, 0, 0]
    for name, nk, nsq in (("mix0", KT, KT), ("cq", 3, 3), ("ckv", 2, 2), ("ffn0", KT, 4), ("mix1", KT, 4),
                          ("ffn1", KT, 4), ("final", KT, 4), ("mix2", KT, KT), ("ffn2", KT, 4), ("final2", KT, 4)):
        norm_at[name] = tuple(norm_n)
        norm_n[0] += 1
        norm_n[1] += nk
        norm_n[2] += nsq

    def square(src, kt, n):
        nc.scalar.activation(work[:, kt, 0:n], src, ACT.Square).then_inc(sem("sq_done"), 1)

    def norm_act(name, src, nk, cols, dim, split=None):
        n = cols.stop - cols.start
        for kt in range(nk):
            square(src(kt), kt, n)
        norm_finish_act(name, nk, cols, dim, split)

    def norm_finish_act(name, nk, cols, dim, split=None):
        one, at, _ = norm_at[name]
        n = cols.stop - cols.start
        nc.scalar.wait_ge(sem("ss_done"), one + 1)
        nc.scalar.activation(log_ms[:, 0:n], ps[:, 7, 0:n], ACT.Ln, scale=1.0 / dim,
                             bias=eps[:]).then_inc(sem("ln_done"), 1)
        nc.scalar.wait_ge(sem("ln_done"), one + 1)
        nc.scalar.activation(rstd[:, 0:n], log_ms[:, 0:n], ACT.Exp, scale=-0.5)\
            .then_inc(sem("rstd_done"), 1)
        if split is not None:
            for kt in range(nk):
                nc.scalar.wait_ge(sem("un_done"), at + kt + 1)
                nc.scalar.activation(split[0](kt), work[:, kt, 0:n], ACT.Copy)\
                    .then_inc(sem("xh_done"), 1)

    def norm_pe(name, nk, n):
        at = norm_at[name][2]
        for kt in range(nk):
            nc.tensor.wait_ge(sem("sq_done"), at + kt + 1)
            mm = nc.tensor.matmul(ps[:, 7, 0:n], ones, work[:, kt, 0:n], start=kt == 0,
                                  stop=kt == nk - 1)
        mm.then_inc(sem("ss_done"), 1)

    def square_sum(name, j, n, start=False, stop=False):
        nc.tensor.wait_ge(sem("sq_done"), j + (norm_at[name][2] + 1))
        for t in range(2):
            mm = nc.tensor.matmul(ps[:, 7, 0:n], ones, paired(work)[:, j, t, 0:n], start=start and t == 0,
                                  stop=stop and t == 1)
        if stop:
            mm.then_inc(sem("ss_done"), 1)

    xh_total, xl_total = [0], [0]
    split_at = {}
    for name, nk in (("mix0", KT), ("cq", 3), ("ckv", 2), ("o0", KT), ("ffn0", KT), ("mix1", KT),
                     ("o1", KT), ("ffn1", KT), ("mix2", KT), ("o2", KT), ("ln", KT),
                     ("merge", KT), ("ffn2", KT)):
        split_at[name] = xl_total[0]
        xl_total[0] += nk

    def norm_dve(name, src, gain, nk, n, split=None, into=None):
        one = norm_at[name][0]
        g0 = GAINS[gain[0]][0] + gain[1]

        def lo(kt):
            nc.vector.wait_ge(sem("xh_done"), split_at[name] + kt + 1)
            nc.vector.tensor_tensor(split[1](kt), work[:, kt, 0:n], split[0](kt).bitcast(F32),
                                    ALU.subtract).then_inc(sem("xl_done"), 1)

        nc.vector.wait_ge(sem("rstd_done"), one + 1)
        for kt in range(nk):
            dst = work[:, kt, 0:n] if into is None else into(kt)
            nc.vector.scalar_tensor_tensor(out=dst, in0=src(kt), scalar=gains[:, g0 + kt:g0 + kt + 1],
                                           in1=rstd[:, 0:n], op0=ALU.mult, op1=ALU.mult)\
                .then_inc(sem("un_done"), 1)
            if split is not None and kt >= 1:
                lo(kt - 1)
        if split is not None:
            lo(nk - 1)

    def u_h(n):
        return lambda kt: u_hi[:, kt, 0:n]

    def u_l(n):
        return lambda kt: u_lo[:, kt, 0:n]

    C1, C2, CF = slice(META, T2), slice(0, T2), slice(META - 2, T2)
    NF = T2 - META + 2

    def h_at(cols):
        return lambda kt: h[:, kt, cols]

    def product(out_ap, pairs, start=True, stop=True):
        for n, (a_h, a_l, b_h, b_l) in enumerate(pairs):
            nc.tensor.matmul(out_ap, a_h, b_h, start=start and n == 0, stop=False)
            nc.tensor.matmul(out_ap, a_h, b_l, start=False, stop=False)
            mm = nc.tensor.matmul(out_ap, a_l, b_h, start=False, stop=stop and n == len(pairs) - 1)
        return mm

    def feature_tile(out_ap, s, nk, n, col, xh, xl, x0=0, start=True, stop=True):
        hi, lo = pw(w_hi[s], nk, n), pw(w_lo[s], nk, n)
        return product(out_ap, [(hi[:, kt, col:col + P], lo[:, kt, col:col + P], xh(x0 + kt), xl(x0 + kt))
                                for kt in range(nk)], start, stop)

    def token_tile(out_ap, s, nk, n, cols, xh, xl, x0=0):
        hi, lo = pw(w_hi[s], nk, n), pw(w_lo[s], nk, n)
        return product(out_ap, [(xh(x0 + kt), xl(x0 + kt), hi[:, kt, cols], lo[:, kt, cols])
                                for kt in range(nk)])

    def begin_unit(ph, i, k):
        s = (ph.u0 + k) % RING
        nc.tensor.wait_ge(lo_done, ph.unit(i, k) + 1)
        if k % ph.group == 0:
            wait(nc.tensor, pair_read[ph.pair(k)], ph.used_before(i, k))
        return s, ph.pair(k)

    def by_tokens(ph, i, k):
        s, p = begin_unit(ph, i, k)
        for b in range(2):
            mm = token_tile(ps[:, 2 * p + b, 0:UC], s, KT, UC, slice(0, UC),
                            lambda kt: u_hi[:, kt, b * P:(b + 1) * P], lambda kt: u_lo[:, kt, b * P:(b + 1) * P])
        mm.then_inc(unit_done, 1)

    def two_tiles(ph, i, k, n, xh, xl, ready=None):
        s, p = begin_unit(ph, i, k)
        outs = [ps[:, 2 * p + t, 0:n] for t in range(2)]
        if ready is None:
            for t in range(2):
                mm = feature_tile(outs[t], s, KT, UC, t * P, xh, xl)
        else:
            hi, lo = pw(w_hi[s], KT, UC), pw(w_lo[s], KT, UC)
            for kt in range(KT):
                nc.tensor.wait_ge(sem("xl_done"), split_at[ready] + kt + 1)
                for t in range(2):
                    cols = slice(t * P, (t + 1) * P)
                    mm = product(outs[t], [(hi[:, kt, cols], lo[:, kt, cols], xh(kt), xl(kt))],
                                 kt == 0, kt == KT - 1)
        mm.then_inc(unit_done, 1)

    def down_unit(name, ph, i, k):
        s, p = begin_unit(ph, i, k)
        k0, nk = DOWN_KT[k % 4]
        if k < 4:
            nc.tensor.wait_ge(sem("ffn_lo"), 2 + FFN[name] + (k0 + nk + 1) // 2)
        for t in range(2):
            mm = feature_tile(ps[:, 2 * p + t, 0:T1], s, nk, UC, t * P, lambda kt: a_hi[:, kt, :],
                              lambda kt: a_lo[:, kt, :], x0=k0, start=k % 4 == 0, stop=k % 4 == 3)
        mm.then_inc(unit_done, 1)

    def pair_ap(p, n):
        return ps[:, 2 * p:2 * p + 2, 0:n]

    ATT = {"mla": 0, "stick": MLA_H, "chunk": MLA_H + SB_H, "dsa": MLA_H + SB_H + C_H}

    class Attention:
        def __init__(self, name, heads, blocks, dv, banks, bufs, o, lag=1, act_out=False):
            self.soft = {"mla": 0, "chunk": MLA_H, "dsa": MLA_H + C_H}.get(name)
            self.base, self.turns, self.blocks, self.dv, self.lag = ATT[name], heads // 4, blocks, dv, lag
            self.heads = heads
            self.s_banks, self.pt_banks, self.o_banks = banks
            self.p, self.pt, self.stat = bufs
            self.o, self.act_out = o, act_out
            self.cols, at = [], 0
            for _, _, keys in blocks:
                self.cols.append(at)
                at += sum(n for _, n in keys)
            self.width = at
            self.tcols, small, large = [], 0, 0
            few = any(n < P for _, _, keys in blocks for _, n in keys)
            for _, nq, keys in blocks:
                row = []
                for _, n in keys:
                    if n < P:
                        row.append((0, small))
                        small += nq
                    else:
                        row.append((1 if few else 0, large))
                        large += nq
                self.tcols.append(row)
            self.parts = ([(META, 0, small)] if few else []) + [(P, 1 if few else 0, large)]

        def steps(self, eng):
            looped = self.turns > 2
            for i in range(1 if looped else self.turns):
                for e in range(4):
                    yield i, e
            if looped:
                with eng.Fori(1, self.turns) as i:
                    for e in range(4):
                        yield i, e

        def head(self, i, e, back=0):
            n = i * 4 + (e - back)
            return None if isinstance(n, int) and n < 0 else n

        def S(self, e, b):
            _, nq, keys = self.blocks[b]
            return ps[0:nq, self.s_banks[e % len(self.s_banks)],
                      self.cols[b]:self.cols[b] + sum(n for _, n in keys)]

        def P(self, e, b, key=None):
            _, nq, keys = self.blocks[b]
            at = self.cols[b] + (0 if key is None else sum(n for _, n in keys[:key]))
            n = sum(n for _, n in keys) if key is None else keys[key][1]
            return self.p[0:nq, e % 2, at:at + n]

        def pt_ps(self, e, b, key):
            _, nq, keys = self.blocks[b]
            bank, at = self.tcols[b][key]
            return ps[0:keys[key][1], self.pt_banks[e % len(self.pt_banks)][bank], at:at + nq]

        def PT(self, e, b, key):
            _, nq, keys = self.blocks[b]
            bank, at = self.tcols[b][key]
            return self.pt[0:keys[key][1], e % 2, 512 * bank + at:512 * bank + at + nq]

        def O(self, e, b):
            return ps[0:self.blocks[b][1], self.o_banks[e % 2], b * self.dv:(b + 1) * self.dv]

        def transposes(self, n, e):
            nc.tensor.wait_ge(sem("at_p"), n + (self.base + 1))
            wait(nc.tensor, sem("at_ptc"), n + (self.base + 1 - len(self.pt_banks)))
            for b, (_, nq, keys) in enumerate(self.blocks):
                for key in range(len(keys)):
                    mm = nc.tensor.transpose(self.pt_ps(e, b, key), self.P(e, b, key), ident[0:nq, 0:nq])
            mm.then_inc(sem("at_pt"), 1)

        def values(self, n, e, v):
            nc.tensor.wait_ge(sem("at_ptc"), n + (self.base + 1))
            wait(nc.tensor, sem("at_oev"), n + (self.base - 1))
            for b, (_, nq, keys) in enumerate(self.blocks):
                for key in range(len(keys)):
                    mm = nc.tensor.matmul(self.O(e, b), self.PT(e, b, key), v(n, e, b, key),
                                          start=key == 0, stop=key == len(keys) - 1)
            mm.then_inc(sem("at_o"), 1)

        def pe(self, scores, v, between=None):
            for i, e in self.steps(nc.tensor):
                n = self.head(i, e)
                wait(nc.tensor, sem("at_p"), n + (self.base + 1 - len(self.s_banks)))
                scores(self, i, e, n).then_inc(sem("at_scores"), 1)
                if (m := self.head(i, e, self.lag)) is not None:
                    self.transposes(m, (e - self.lag) % 4)
                if (m := self.head(i, e, self.lag + 1)) is not None:
                    self.values(m, (e - self.lag - 1) % 4, v)
                if between is not None:
                    between(n)
            for m in range(self.heads - self.lag, self.heads):
                self.transposes(m, m % 4)
                self.values(m - 1, (m - 1) % 4, v)
            self.values(self.heads - 1, (self.heads - 1) % 4, v)

        def exps(self, n, e, scale, src):
            nc.scalar.wait_ge(sem("at_neg"), n + (self.soft + 1))
            wait(nc.scalar, sem("at_pt"), n + (self.base - 1))
            if self.act_out:
                wait(nc.scalar, sem("at_rsum"), n + (self.soft - 1))
            else:
                wait(nc.scalar, sem("at_oev"), n + (self.base - 1))
            for b, (_, nq, _) in enumerate(self.blocks):
                st = self.stat[0:nq, e % 2]
                a = nc.scalar.activation(self.P(e, b), src(e, b), ACT.Exp, scale=scale,
                                         bias=st[:, 1, b:b + 1], accum_out=st[:, 2, b:b + 1])
            a.then_inc(sem("at_p"), 1)

        def copies(self, n, e):
            nc.scalar.wait_ge(sem("at_pt"), n + (self.base + 1))
            wait(nc.scalar, sem("at_o"), n + (self.base - 1))
            for rows, bank, width in self.parts:
                a = nc.scalar.activation(self.pt[0:rows, e % 2, 512 * bank:512 * bank + width],
                                         ps[0:rows, self.pt_banks[e % len(self.pt_banks)][bank], 0:width], ACT.Copy)
            a.then_inc(sem("at_ptc"), 1)

        def outputs(self, n, e):
            nc.scalar.wait_ge(sem("at_o"), n + (self.base + 1))
            nc.scalar.wait_ge(sem("at_rsum"), n + (self.soft + 1))
            for b, (_, nq, _) in enumerate(self.blocks):
                a = nc.scalar.activation(self.o(n, b), self.O(e, b), ACT.Copy, scale=self.stat[0:nq, e % 2, 3, b:b + 1])
            a.then_inc(sem("at_oev"), 1)

        def act(self, scale, src, between=None):
            for i, e in self.steps(nc.scalar):
                n = self.head(i, e)
                self.exps(n, e, scale, src)
                if (m := self.head(i, e, 1)) is not None:
                    self.copies(m, (e - 1) % 4)
                if self.act_out and (m := self.head(i, e, 2)) is not None:
                    self.outputs(m, (e - 2) % 4)
                if between is not None:
                    between(n)
            self.copies(self.heads - 1, (self.heads - 1) % 4)
            if self.act_out:
                for m in range(self.heads - 2, self.heads):
                    self.outputs(m, m % 4)

        def maxima(self, n, e, scale, src):
            wait(nc.vector, sem("at_p"), n + (self.base - 1))
            for b, (_, nq, _) in enumerate(self.blocks):
                a = nc.vector.reduce_max(self.stat[0:nq, e % 2, 0, b:b + 1], src(e, b), AX)
            a.then_inc(sem("at_max"), 1)
            nc.vector.wait_ge(sem("at_max"), n + (self.soft + 1))
            nb = len(self.blocks)
            nc.vector.tensor_scalar(self.stat[:, e % 2, 1, 0:nb], self.stat[:, e % 2, 0, 0:nb], -scale,
                                    None, ALU.mult).then_inc(sem("at_neg"), 1)

        def normalise(self, n, e):
            nc.vector.wait_ge(sem("at_p"), n + (self.base + 1))
            nb = len(self.blocks)
            if self.act_out:
                wait(nc.vector, sem("at_oev"), n + (self.base - 1))
            nc.vector.reciprocal(self.stat[:, e % 2, 3, 0:nb], self.stat[:, e % 2, 2, 0:nb])\
                .then_inc(sem("at_rsum"), 1)
            if self.act_out:
                return
            nc.vector.wait_ge(sem("at_o"), n + (self.base + 1))
            nc.vector.wait_ge(sem("at_rsum"), n + (self.soft + 1))
            for b, (_, nq, _) in enumerate(self.blocks):
                a = nc.vector.tensor_scalar(self.o(n, b), self.O(e, b), self.stat[0:nq, e % 2, 3, b:b + 1],
                                            None, ALU.mult)
            a.then_inc(sem("at_oev"), 1)

        def dve(self, scale, src, before=None, between=None):
            for i, e in self.steps(nc.vector):
                n = self.head(i, e)
                nc.vector.wait_ge(sem("at_scores"), n + (self.base + 1))
                if before is not None:
                    before(self, n, e)
                self.maxima(n, e, scale, src)
                if (m := self.head(i, e, 2)) is not None:
                    self.normalise(m, (e - 2) % 4)
                if between is not None:
                    between(n)
            for m in range(self.heads - 2, self.heads):
                self.normalise(m, m % 4)

    def by_head(t, n, d):
        return t.rearrange("p b (n d) -> p b n d", d=d)

    o1v, o3v = by_head(o1, 0, VD), by_head(o3, 0, HD)
    wide = ([0, 1, 2, 3], [[4], [5]], [6, 7])
    mla = Attention("mla", MLA_H, BLOCKS1, VD, wide, (p1, pt1, stat1),
                    lambda n, b: o1v[:, b, n, :])
    stk = Attention("stick", SB_H, BLOCKS1, HD, wide, (p1, pt1, stat1),
                    lambda n, b: o1v[:, b, n + MLA_H, :], lag=2)
    chk = Attention("chunk", C_H, BLOCKS1, HD, wide, (p3, pt3, stat3),
                    lambda n, b: o3v[:, b, n, :])

    def o_dsa(n, b):
        return o_meta[:, n * DH:(n + 1) * DH] if b == 0 else q_d[:, n, (b - 1) * P:b * P]

    dsa = Attention("dsa", 8, BLOCKS2, DH, ([4, 5], [[2, 3]], [6, 7]), (p4, pt4, stat4), o_dsa, act_out=True)

    def pad_heads(att, q, q_dst, extra=None):
        for i, e in att.steps(nc.gpsimd):
            n = att.head(i, e)
            wait(nc.gpsimd, sem("at_scores"), n + (att.base - 3))
            wait(nc.gpsimd, sem("pad_done"), n + att.base)
            rows = slice(64 * (e % 2), 64 * (e % 2) + 64)
            a = nc.gpsimd.tensor_copy(q_dst[rows, e, :], q[rows, i * 2 + e // 2, :])
            if extra is not None:
                a.then_inc(sem("pad_part"), 1)
                nc.gpsimd.wait_ge(sem("pad_part"), n + 1)
                a = extra(i, e)
            a.then_inc(sem("pad_done"), 1)

    def masked_scores(att, e, b, terms, mask):
        out_ap = att.S(e, b)
        for t, (lhs, rhs) in enumerate(terms):
            nc.tensor.matmul(out_ap, lhs, rhs, start=t == 0, stop=False)
        _, nq, keys = att.blocks[b]
        own = sum(n for _, n in keys[:-1])
        return nc.tensor.matmul(out_ap[:, own:own + nq], ident_b[0:nq, 0:nq], mask[0:nq, 0:nq],
                                start=False, stop=True)

    def mla_scores(att, i, e, n):
        nc.tensor.wait_ge(sem("pad_done"), n + (att.base + 1))
        for b, (q0, nq, keys) in enumerate(att.blocks):
            end = keys[-1][0] + keys[-1][1]
            mm = masked_scores(att, e, b, [
                (q_pad[:, e, q0:q0 + nq], k_nope[:, i * 2 + e // 2, 0:end]),
                (q_pad_r[:, e, q0:q0 + nq], k_rope[:, 0:end])], chunk_b)
        return mm

    def pair_scores(q, kk, mask):
        def scores(att, i, e, n):
            nc.tensor.wait_ge(sem("pad_done"), n + (att.base + 1))
            for b, (q0, nq, keys) in enumerate(att.blocks):
                end = keys[-1][0] + keys[-1][1]
                mm = masked_scores(att, e, b, [(q[:, e, q0:q0 + nq], kk[:, i * 2 + e // 2, 0:end])], mask)
            return mm
        return scores

    def head_values(v, d):
        vv = v.rearrange("p b (n d) -> p b n d", d=d)
        return lambda n, e, b, key: vv[:, key, n, :]

    def rope_pe(rot, tiles, n, first, banks):
        for t, x_ap in enumerate(tiles):
            wait(nc.tensor, sem("rope_done"), first + t + 1 - len(banks))
            nc.tensor.matmul(ps[:, banks[(first + t) % len(banks)], 0:n], rot, x_ap, start=True, stop=True)\
                .then_inc(sem("rot_done"), 1)

    def rope_dve(tiles, cos, sin, n, first, tmp, banks):
        def add(t):
            nc.vector.wait_ge(sem("rope_sin"), first + t + 1)
            nc.vector.tensor_tensor(tiles[t], rot(t), tmp[:, (first + t) % 2, 0:n], ALU.add).then_inc(sem("rope_done"), 1)

        def rot(t):
            return ps[:, banks[(first + t) % len(banks)], 0:n]

        for t, x_ap in enumerate(tiles):
            nc.vector.wait_ge(sem("rot_done"), first + t + 1)
            wait(nc.vector, sem("rope_done"), first + t - 1)
            nc.vector.tensor_tensor(tmp[:, (first + t) % 2, 0:n], x_ap, cos, ALU.mult)
            nc.vector.tensor_tensor(rot(t), rot(t), sin, ALU.mult).then_inc(sem("rope_sin"), 1)
            if t:
                add(t - 1)
        add(len(tiles) - 1)

    q_tiles = [q_d[:, t, :] for t in range(8)] + [k_d[:, t, :] for t in range(KVH)]
    idx_tiles = [qi[:, t, :] for t in range(4)] + [ki[:]]
    Q_ROPES = [(0, 4), (4, 8), (8, 10)]

    def turn_groups(n):
        if 2 * n <= 512:
            return [(range(2 * g, 2 * g + 2), ps[:, 4 + g, 0:2 * n]) for g in range(KT // 2)]
        return [(range(j, j + 1), ps[:, j, 0:n]) for j in range(KT)]

    def tiles_ap(t, js, n):
        return t[:, js[0]:js[-1] + 1, 0:n]

    def turn_pe(o, blocks, n):
        for js, bank in turn_groups(n):
            for at, j in enumerate(js):
                for b, (q0, nq, _) in enumerate(blocks):
                    mm = nc.tensor.transpose(bank[:, at * n + q0:at * n + q0 + nq], o(b, j),
                                             ident[0:nq, 0:nq])
            mm.then_inc(sem("turned"), len(js))

    def turn_act(first, n):
        for js, bank in turn_groups(n):
            nc.scalar.wait_ge(sem("turned"), first + js[-1] + 1)
            nc.scalar.activation(tiles_ap(u_hi, js, n), bank.rearrange("p (t n) -> p t n", n=n), ACT.Copy)\
                .then_inc(sem("xh_done"), len(js))

    def turn_dve(name, n):
        for js, bank in turn_groups(n):
            nc.vector.wait_ge(sem("xh_done"), split_at[name] + js[-1] + 1)
            nc.vector.tensor_tensor(tiles_ap(u_lo, js, n), bank.rearrange("p (t n) -> p t n", n=n),
                                    tiles_ap(u_hi, js, n).bitcast(F32), ALU.subtract).then_inc(sem("xl_done"), len(js))

    def operands_ready(name, nk=KT):
        nc.tensor.wait_ge(sem("xl_done"), split_at[name] + nk)

    def residual_dve(ph, cols, group=1):
        n = cols.stop - cols.start
        for i, k in ph.steps(nc.vector):
            last = k == ph.body - 1
            if not last:
                split_lo(ph, i, k)
            if k % group == group - 1:
                p = ph.pair(k)
                j = i * ph.groups + k // group
                nc.vector.wait_ge(unit_done, ph.unit(i, k) + 1)
                hv = h.rearrange("p (j t) n -> p j t n", t=2)[:, j, :, cols]
                nc.vector.tensor_tensor(hv, hv, pair_ap(p, n), ALU.add).then_inc(pair_read[p], 1)
            if last:
                split_lo(ph, i, k)

    def splits_act(ph):
        for i, k in ph.steps(nc.scalar):
            split_hi(ph, i, k)

    def residual_act(ph, cols, group=1):
        n = cols.stop - cols.start
        for i, k in ph.steps(nc.scalar):
            last = k == ph.body - 1
            if not last:
                split_hi(ph, i, k)
            if k % group == group - 1:
                j = i * ph.groups + k // group
                nc.scalar.wait_ge(pair_read[ph.pair(k)], ph.used_before(i, k) + 1)
                nc.scalar.activation(paired(work)[:, j, :, 0:n], paired(h)[:, j, :, cols], ACT.Square)\
                    .then_inc(sem("sq_done"), 1)
            if last:
                split_hi(ph, i, k)

    def residual_pe(ph, n, split, norm, norm_n):
        for i, k in ph.steps(nc.tensor):
            two_tiles(ph, i, k, n, u_h(n), u_l(n), split if k == 0 else None)
            if k:
                square_sum(norm, k - 1, norm_n, start=k == 1)
        square_sum(norm, 3, norm_n, stop=True)

    FFN = {"ffn0": 0, "ffn1": FT // 2, "ffn2": FT}

    def ffn_act(name, ph):
        for i, k in ph.steps(nc.scalar):
            split_hi(ph, i, k)
            j, s, p = i * 2 + k // 2, (k // 2) % 2, ph.pair(k)
            if k % 2 == 0:
                nc.scalar.wait_ge(unit_done, ph.unit(i, k) + 1)
                wait(nc.scalar, pair_read[ph.pair(k + 1)], ph.used_before(i, k + 1))
                nc.scalar.activation(act_g[:, s], pair_ap(p, T1), ACT.Silu).then_inc(pair_read[p], 1)
            else:
                nc.scalar.wait_ge(pair_read[p], ph.used_before(i, k) + 1)
                nc.scalar.activation(paired(a_hi)[:, j], act_a[:, s], ACT.Copy).then_inc(sem("ffn_hi"), 1)

    def ffn_lo(name, j, s):
        nc.vector.wait_ge(sem("ffn_hi"), j + (FFN[name] + 1))
        nc.vector.tensor_tensor(paired(a_lo)[:, j], act_a[:, s], paired(a_hi)[:, j].bitcast(F32), ALU.subtract)\
            .then_inc(sem("ffn_lo"), 1)

    def ffn_dve(name, ph):
        for i, k in ph.steps(nc.vector):
            split_lo(ph, i, k)
            if k % 2 == 0:
                continue
            j, s, p = i * 2 + k // 2, (k // 2) % 2, ph.pair(k)
            nc.vector.wait_ge(unit_done, ph.unit(i, k) + 1)
            gate = ph.pair(k - 1)
            nc.vector.wait_ge(pair_read[gate], ph.used_before(i, k - 1) + 1)
            nc.vector.wait_ge(sem("ffn_lo"), j + (FFN[name] + 1))
            nc.vector.tensor_tensor(act_a[:, s], pair_ap(p, T1), act_g[:, s], ALU.mult)\
                .then_inc(pair_read[p], 1)
            ffn_lo(name, j, s)

    def ffn_pe(ph, n, name):
        for i, k in ph.steps(nc.tensor):
            two_tiles(ph, i, k, n, u_h(n), u_l(n), name if k == 0 else None)

    def down_pe(name, ph, norm):
        wait(nc.tensor, pair_read[3], ph.used_after[3])
        nc.tensor.matmul(ps[:, 7, 0:T1], ones, c("zeros"), start=True, stop=False)
        for i, k in ph.steps(nc.tensor):
            down_unit(name, ph, i, k)
            if k == 5:
                square_sum(norm, i * 2, T1)
        square_sum(norm, 1, T1)
        square_sum(norm, 3, T1, stop=True)

    def column_units(w, per):
        def unit(i, k):
            if isinstance(i, int):
                return w[:, (i * per + k) * UC:(i * per + k + 1) * UC].rearrange("(k p) n -> p k n", p=P)
            whole = w.shape[1] // (per * UC)
            return w[:, 0:whole * per * UC].rearrange("(k p) (i m n) -> p k i m n", p=P, m=per, n=UC)[:, :, i, k, :]
        return unit

    def down_units(w):
        v = w.rearrange("(k p) (i g n) -> p k i g n", p=P, g=2, n=UC)
        return lambda i, g, r: v[:, DOWN_KT[r][0]:DOWN_KT[r][0] + DOWN_KT[r][1], i, g, :]

    def begin_load(ph, i, k):
        wait(nc.sync, lo_done, ph.unit(i, k) - (RAW - 1))
        nc.sync.sem_inc(sem("slot_taken"), 1)
        s = (ph.u0 + k) % RAW
        return raw[s], raw_landed[s]

    def load(ph, i, k, src, nk=KT, n=UC):
        slot, landed_sem = begin_load(ph, i, k)
        nc.sync.dma_start(pw(slot, nk, n), src).then_inc(landed_sem, 16)

    def load_columns(ph, w):
        src = column_units(w, ph.body)
        for i, k in ph.steps(nc.sync):
            load(ph, i, k, src(i, k))

    def load_turns(ph, first, second):
        a, b = column_units(first, ph.body // 2), column_units(second, ph.body // 2)
        for i, k in ph.steps(nc.sync):
            load(ph, i, k, (a if k % 2 == 0 else b)(i, k // 2))

    def load_down(ph, w):
        src = down_units(w)
        for i, k in ph.steps(nc.sync):
            load(ph, i, k, src(i, k // 4, k % 4), nk=DOWN_KT[k % 4][1])

    block = ctx.enter_context(nc.Block())

    @block.sync
    def _(sp):
        nc.sync.dma_start(const[:], constants).then_inc(sem("x_landed"), 16)
        nc.sync.dma_start(x_rows[:], x[0].rearrange("(b p) d -> p b d", p=P)).then_inc(sem("x_landed"), 16)
        nc.sync.dma_start(meta_rows[:], meta_tokens_2).then_inc(sem("x_landed"), 16)
        w = ev_w_in[0]
        rope_col, b_col = QL + KVL, QL + KVL + ROPE_D
        for k in range(9):
            if k < 2:
                load(ph_in, 0, k, column_units(w[:, 0:2 * UC], 9)(0, k))
            elif k == 2:
                slot, landed_sem = begin_load(ph_in, 0, k)
                v, u = pw(slot, KT, UC), w.rearrange("(k p) n -> p k n", p=P)
                nc.sync.dma_start(v[:, :, 0:P], u[:, :, 2 * UC:rope_col]).then_inc(landed_sem, 16)
                for r in range(4):
                    at = P + r * ROPE_D
                    nc.sync.dma_start(v[:, :, at:at + ROPE_D], u[:, :, rope_col:b_col]).then_inc(landed_sem, 16)
            else:
                load(ph_in, 0, k, column_units(w[:, b_col:], 9)(0, k - 3))
        for k in range(2):
            slot, landed_sem = begin_load(ph_lat, 0, k)
            v = pw(slot, 3, 384)
            u = ev_w_uq[0].rearrange("(k p) (g a n) -> p k g a n", p=P, g=2, a=4)
            for kt in range(3):
                nc.sync.dma_start(v[:, kt, 0:256].rearrange("p (a n) -> p a n", a=4),
                                  u[:, kt, k, :, 0:NOPE]).then_inc(landed_sem, 16)
                nc.sync.dma_start(v[:, kt, 256:384].rearrange("p (a n) -> p a n", a=4),
                                  u[:, kt, k, :, NOPE:]).then_inc(landed_sem, 16)
        for k in range(2):
            slot, landed_sem = begin_load(ph_lat, 0, 2 + k)
            v = pw(slot, 2, 512)
            u = ev_w_ukv[0].rearrange("(k p) (a n) -> p k a n", p=P, a=MLA_H)
            for kt in range(2):
                nc.sync.dma_start(v[:, kt, :].rearrange("p (a n) -> p a n", a=MLA_H),
                                  u[:, kt, :, k * NOPE:(k + 1) * NOPE]).then_inc(landed_sem, 16)
        load_columns(ph_out0, ev_w_out[0])
        load_turns(ph_ffn0, w_gate[0], w_up[0])
        load_down(ph_down0, w_down[0])
        load_columns(ph_qk, od_w_qkv[0][:, 0:2 * D])
        load_columns(ph_v, od_w_qkv[0][:, 2 * D:])
        load_columns(ph_out1, od_w_out[0])
        load_turns(ph_ffn1, w_gate[1], w_up[1])
        load_down(ph_down1, w_down[1])
        w = w_in_2[0]
        load_turns(ph_conv, w[:, D:2 * D], w[:, 0:D])
        slot, landed_sem = begin_load(ph_idx, 0, 0)
        v, u, at = pw(slot, KT, 2 * ID + IH), w.rearrange("(k p) n -> p k n", p=P), 2 * D + 8 * UC
        for r in range(2):
            nc.sync.dma_start(v[:, :, r * ID:(r + 1) * ID], u[:, :, at:at + ID]).then_inc(landed_sem, 16)
        nc.sync.dma_start(v[:, :, 2 * ID:], u[:, :, at + ID:at + ID + IH]).then_inc(landed_sem, 16)
        for k in range(2):
            load(ph_idx, 0, 1 + k, u[:, :, at - (2 - k) * UC:at - (1 - k) * UC])
        load_columns(ph_proj, w[:, 2 * D:2 * D + 6 * UC])
        load_columns(ph_gate, w[:, at + ID + IH:at + ID + IH + D])
        load_columns(ph_gate_b, w[:, at + ID + IH + D:])
        load_columns(ph_wo, attn_w_o_2[0])
        load_columns(ph_pw, conv_pw_out_2[0])
        load_columns(ph_merge, w_merge_out_2[0])
        load_turns(ph_ffn2, ffn_up_2[0][:, 0:DFF], ffn_up_2[0][:, DFF:])
        load_down(ph_down2, ffn_down_2[0])
        for t in range(2):
            sp.wait_ge(sem(f"out_copied{t}"), 1)
            nc.sync.dma_start(out[0, t * P:(t + 1) * P, :], out_rows[:, t, :]).then_inc(sem("out_stored"), 16)
        sp.wait_ge(sem("out_stored"), 32)

    @block.gpsimd
    def _(pool):
        pool.wait_ge(sem("gains_ready"), 1)
        nc.gpsimd.memset(q_pad[:], 0.0).then_inc(sem("zeroed"), 1)
        pool.wait_ge(sem("zeroed"), 1)
        nc.gpsimd.memset(q_pad_r[:], 0.0).then_inc(sem("zeroed"), 1)
        pool.wait_ge(sem("zeroed"), 2)
        pairs_read(pool, ph_lat)
        pool.wait_ge(sem("rope_done"), 3)

        def rope_part(i, e):
            rows = slice(32 * e, 32 * e + 32)
            return nc.gpsimd.tensor_copy(q_pad_r[rows, e, :], q_rope[rows, i, :])

        pad_heads(mla, q_nope, q_pad, rope_part)
        pad_heads(stk, q_b, q_pad)

        pairs_read(pool, ph_down0)
        rel = bass.AP(tensor=od_rel_bias.tensor, offset=od_rel_bias.offset + 1 + P,
                      ap=[[1, P], [513, C_H], [1, 2 * P]])
        nc.gpsimd.dma_start(bias_h[:], rel).then_inc(sem("bias_landed"), 16)
        nc.gpsimd.memset(q_pad_c[:], 0.0).then_inc(sem("zeroed"), 1)
        pool.wait_ge(sem("zeroed"), 3)
        pairs_read(pool, ph_v)
        pad_heads(chk, q_c, q_pad_c)

        pairs_read(pool, ph_down1)
        for n, t in enumerate((cin[:, :, 0:CONV_W - 1], stat4[:], q_cur[:])):
            nc.gpsimd.memset(t, 0.0).then_inc(sem("zeroed"), 1)
            pool.wait_ge(sem("zeroed"), 4 + n)
        pool.wait_ge(sem("rope_done"), 8)
        for n in range(IH):
            e = n % 2
            rows = slice(64 * e, 64 * e + 64)
            wait(pool, sem("idx_pad"), n)
            wait(pool, sem("idx_scored"), n - 1)
            nc.gpsimd.tensor_copy(q_cur[rows, e, :], qi[rows, n // 2, :]).then_inc(sem("idx_pad"), 1)
        pool.wait_ge(sem("idx_scored"), IH)
        pool.wait_ge(sem("idx_pad"), IH)
        pool.wait_ge(sem("rope_done"), 18)
        for i, e in dsa.steps(pool):
            n = dsa.head(i, e)
            wait(pool, sem("at_scores"), n + (dsa.base - 1))
            wait(pool, sem("pad_done"), n + dsa.base)
            nc.gpsimd.tensor_copy(q_cur[:, e % 2, :], q_d[:, n, :]).then_inc(sem("pad_done"), 1)

    @block.scalar
    def _(act):
        rows = sem("rows_landed")
        for name, src in (("mix", g_mix), ("ffn", g_ffn), ("final", g_final.unsqueeze(0)), ("cq", ev_g_cq),
                          ("ckv", ev_g_ckv), ("mix2", mix_norm_g_2), ("ln_g", conv_ln_g_2),
                          ("ln_b", conv_ln_b_2), ("dw_b", conv_dw_b_2), ("ffn2", ffn_norm_g_2),
                          ("final2", final_norm_g_2.unsqueeze(0))):
            at, n = GAINS[name]
            nc.scalar.dma_start(gain_rows[at:at + n, :], src.rearrange("a (r p) -> (a r) p", p=P)).then_inc(rows, 16)
        taps = ffn_dw_w_2[0]
        nc.scalar.dma_start(dw_rows[:, 0, :], taps[0:2].rearrange("w (t p) -> (w t) p", p=P)).then_inc(rows, 16)
        nc.scalar.dma_start(dw_rows[0:2 * FT, 1, :], taps[2].rearrange("(t p) -> t p", p=P)).then_inc(rows, 16)
        nc.scalar.dma_start(dw_rows[2 * FT:, 1, :], ffn_dw_b_2[0].rearrange("(t p) -> t p", p=P)).then_inc(rows, 16)
        nc.scalar.dma_start(conv_rows[:], conv_dw_w_2[0]).then_inc(rows, 16)
        act.preload_act_table_set("natural_log_exp_and_others")
        for j in range(KT):
            act.wait_ge(sem("x_turned"), j + 1)
            nc.scalar.activation(h[:, j, :], ps[:, j, 0:T2], ACT.Copy).then_inc(sem("h_copied"), 1)
        for k in range(AHEAD):
            split_hi(prologue, 0, k)
        act.wait_ge(sem("consts_ready"), 1)
        act.wait_ge(sem("h_copied"), KT)
        norm_act("mix0", h_at(C1), KT, C1, D, (u_h(T1),))

        for i, k in ph_in.steps(act):
            split_hi(ph_in, i, k)
            p = ph_in.pair(k)
            act.wait_ge(unit_done, k + 1)
            src = pair_ap(p, T1)
            if k < 2:
                a = nc.scalar.activation(lat[:, 2 * k:2 * k + 2, :], src, ACT.Copy)
            elif k == 2:
                nc.scalar.activation(lat[:, 4, :], ps[:, 2 * p, 0:T1], ACT.Copy)
                a = nc.scalar.activation(k_rope[:], ps[:, 2 * p + 1, 0:T1], ACT.Copy)
            else:
                j = (k - 3) % 2
                if k < 5:
                    a = nc.scalar.activation(q_b[:, 2 * j:2 * j + 2, :], src, ACT.Copy, scale=HD ** -0.5)
                elif k < 7:
                    a = nc.scalar.activation(k_b[:, 2 * j:2 * j + 2, :], src, ACT.Copy)
                else:
                    a = nc.scalar.activation(v_b[:, :, j * UC:(j + 1) * UC], src, ACT.Copy)
            a.then_inc(pair_read[p], 1)
        pairs_read(act, ph_in)
        cols = slice(0, T1)
        norm_act("cq", lambda kt: lat[:, kt, :], 3, cols, QL, (lambda kt: lat_hi[:, kt, :],))
        act.wait_ge(sem("xl_done"), split_at["cq"] + 3)
        norm_act("ckv", lambda kt: lat[:, 3 + kt, :], 2, cols, KVL, (lambda kt: lat_hi[:, 3 + kt, :],))
        for i, k in ph_lat.steps(act):
            split_hi(ph_lat, i, k)
            p = ph_lat.pair(k)
            act.wait_ge(unit_done, ph_lat.unit(i, k) + 1)
            if k < 2:
                nc.scalar.activation(q_nope[:, 2 * k:2 * k + 2, :], pair_ap(p, T1), ACT.Copy)
                a = nc.scalar.activation(q_rope[:, k, :], ps[:, 2 * p, T1:2 * T1], ACT.Copy)
            elif k == 2:
                a = nc.scalar.activation(k_nope[:], ps[:, 2 * p:2 * p + 2, :].rearrange("p b (t n) -> p (b t) n", t=2),
                                         ACT.Copy)
            else:
                a = nc.scalar.activation(v_a[:], pair_ap(p, 512), ACT.Copy)
            a.then_inc(pair_read[p], 1)
        mla.act((NOPE + ROPE_D) ** -0.5, mla.S)

        def softplus_log(n, e):
            b0 = n + (stk.base + 1)
            bank = ps[:, stk.s_banks[e], 0:stk.width]
            act.wait_ge(sem("at_scores"), b0)
            wait(act, sem("st_sp"), n - 1)
            nc.scalar.activation(stick[:, e % 2, 0, :], bank, ACT.Abs).then_inc(sem("st_abs"), 1)
            act.wait_ge(sem("st_abs"), n + 1)
            nc.scalar.activation(stick[:, e % 2, 1, :], stick[:, e % 2, 0, :], ACT.Exp, scale=-1.0)\
                .then_inc(sem("st_exp"), 1)
            act.wait_ge(sem("st_exp"), n + 1)
            nc.scalar.activation(stick[:, e % 2, 0, :], stick[:, e % 2, 1, :], ACT.Ln, bias=1.0)\
                .then_inc(sem("st_ln"), 1)

        def stick_weights(n, e):
            act.wait_ge(sem("st_t"), n + 1)
            wait(act, sem("at_pt"), n + (stk.base - 1))
            nc.scalar.activation(p1[:, e % 2, 0:stk.width], stick[:, e % 2, 4, :], ACT.Exp).then_inc(sem("at_p"), 1)

        for i, e in stk.steps(act):
            softplus_log(stk.head(i, e), e)
            if (m := stk.head(i, e, 1)) is not None:
                stick_weights(m, (e - 1) % 4)
            if (m := stk.head(i, e, 2)) is not None:
                stk.copies(m, (e - 2) % 4)
        stick_weights(SB_H - 1, 3)
        stk.copies(SB_H - 2, 2)
        stk.copies(SB_H - 1, 3)
        turn_act(0, T1)

        residual_act(ph_out0, C1)
        norm_finish_act("ffn0", KT, C1, D, (u_h(T1),))
        ffn_act("ffn0", ph_ffn0)
        act.preload_act_table_set("natural_log_exp_and_others")
        residual_act(ph_down0, C1, group=4)
        norm_finish_act("mix1", KT, C1, D, (u_h(T1),))

        for i, k in ph_qk.steps(act):
            split_hi(ph_qk, i, k)
            p = ph_qk.pair(k)
            act.wait_ge(unit_done, ph_qk.unit(i, k) + 1)
            nc.scalar.activation(paired(qk_c)[:, i * 4 + k], pair_ap(p, T1), ACT.Copy).then_inc(pair_read[p], 1)
        for i, k in ph_v.steps(act):
            split_hi(ph_v, i, k)
            p = ph_v.pair(k)
            act.wait_ge(unit_done, ph_v.unit(i, k) + 1)
            nc.scalar.activation(v_c[:, :, k * UC:(k + 1) * UC], pair_ap(p, UC), ACT.Copy).then_inc(pair_read[p], 1)
        chk.act(1.0, lambda e, b: biased_ap(e, b))
        turn_act(KT, T1)
        residual_act(ph_out1, C1)
        norm_finish_act("ffn1", KT, C1, D, (u_h(T1),))
        ffn_act("ffn1", ph_ffn1)
        act.preload_act_table_set("natural_log_exp_and_others")
        residual_act(ph_down1, C1, group=4)
        norm_finish_act("final", KT, C1, D)
        for kt in range(KT):
            act.wait_ge(sem("un_done"), norm_at["final"][1] + kt + 1)
            square(h[:, kt, :], kt, T2)
        norm_finish_act("mix2", KT, C2, D, (u_h(T2),))

        for i, k in ph_conv.steps(act):
            split_hi(ph_conv, i, k)
            if k % 2 == 0:
                p = ph_conv.pair(k)
                act.wait_ge(unit_done, ph_conv.unit(i, k) + 1)
                wait(act, pair_read[ph_conv.pair(k + 1)], ph_conv.used_before(i, k + 1))
                nc.scalar.activation(sg4[:, (k // 2) % 2], pair_ap(p, T2), ACT.Sigmoid).then_inc(pair_read[p], 1)
        for i, k in ph_idx.steps(act):
            split_hi(ph_idx, i, k)
            p = ph_idx.pair(k)
            act.wait_ge(unit_done, ph_idx.unit(i, k) + 1)
            if k == 0:
                nc.scalar.activation(ki[:], ps[:, 2 * p, 0:T2], ACT.Copy)
                a = nc.scalar.activation(wi[:, 1:3, :], ps[:, 2 * p + 1, 0:2 * IH].rearrange("p (b n) -> p b n", b=2),
                                         ACT.Copy, scale=IH ** -0.5)
            else:
                a = nc.scalar.activation(qi[:, 2 * (k - 1):2 * k, :], pair_ap(p, T2), ACT.Copy)
            a.then_inc(pair_read[p], 1)
        for i, k in ph_proj.steps(act):
            split_hi(ph_proj, i, k)
            p = ph_proj.pair(k)
            act.wait_ge(unit_done, ph_proj.unit(i, k) + 1)
            if k < 4:
                a = nc.scalar.activation(q_d[:, 2 * k:2 * k + 2, :], pair_ap(p, T2), ACT.Copy)
            elif k == 4:
                a = nc.scalar.activation(k_d[:], pair_ap(p, T2), ACT.Copy)
            else:
                nc.scalar.activation(v_d[0:META, 0, :], ps[0:META, 2 * p, UC:2 * UC], ACT.Copy)
                a = nc.scalar.activation(v_d[:, 1:3, :], pair_ap(p, UC), ACT.Copy)
            a.then_inc(pair_read[p], 1)
            if k == 2:
                for n in range(IH):
                    act.wait_ge(sem("idx_scored"), n + 1)
                    wait(act, sem("idx_acc"), n - 1)
                    nc.scalar.activation(dots(n % 2), ps[:, 6 + n % 2, 0:416], ACT.Relu, scale=ID ** -0.5)\
                        .then_inc(sem("idx_relu"), 1)
        for i, k in ph_gate.steps(act):
            split_hi(ph_gate, i, k)
            p = ph_gate.pair(k)
            act.wait_ge(unit_done, ph_gate.unit(i, k) + 1)
            nc.scalar.activation(paired(gates)[:, k], pair_ap(p, T2), ACT.Sigmoid).then_inc(pair_read[p], 1)

        act.preload_act_table_set("natural_log_exp_and_others")

        def gate_b(n):
            if n % 2:
                split_hi(ph_gate_b, 0, n // 2)
            elif n:
                gate_b_out(n // 2 - 1)

        def gate_b_out(g):
            act.wait_ge(unit_done, ph_gate_b.unit(0, g) + 1)
            nc.scalar.activation(paired(gates)[:, 4 + g], pair_ap(0, T2), ACT.Copy).then_inc(pair_read[0], 1)

        dsa.act(DH ** -0.5, dsa.S, gate_b)
        gate_b_out(3)
        turn_act(2 * KT, T2)
        act.wait_ge(pair_read[0], ph_gate_b.used_after[0])
        nc.scalar.activation(gates[:, KT:, :], gates[:, KT:, :], ACT.Sigmoid).then_inc(sem("gates_b"), 1)
        splits_act(ph_wo)

        act.preload_act_table_set("natural_log_exp_and_others")
        for kt in range(KT):
            act.wait_ge(sem("ln_centred"), kt + 1)
            nc.scalar.activation(cin[:, kt, 0:T2], work[:, kt, :], ACT.Square).then_inc(sem("ln_sq"), 1)
        act.wait_ge(sem("ln_var"), 1)
        nc.scalar.activation(log_ms[:], ps[:, 6, 0:T2], ACT.Ln, scale=1.0 / D, bias=eps[:]).then_inc(sem("ln_log"), 1)
        act.wait_ge(sem("ln_log"), 1)
        nc.scalar.activation(rstd[:], log_ms[:], ACT.Exp, scale=-0.5).then_inc(sem("ln_rstd"), 1)
        for kt in range(KT):
            act.wait_ge(sem("ln_scaled"), kt + 1)
            g, b = GAINS["ln_g"][0] + kt, GAINS["ln_b"][0] + kt
            nc.scalar.activation(work[:, kt, :], work[:, kt, :], ACT.Silu, scale=gains[:, g:g + 1],
                                 bias=gains[:, b:b + 1]).then_inc(sem("ln_silu"), 1)
            if kt == 0:
                act.wait_ge(unit_done, ph_wo.unit(0, 3) + 1)
            act.wait_ge(sem("ln_silu"), kt + 1)
            nc.scalar.activation(u_hi[:, kt, :], work[:, kt, :], ACT.Copy).then_inc(sem("xh_done"), 1)
        splits_act(ph_pw)
        act.wait_ge(unit_done, ph_pw.unit(0, 3) + 1)
        for j in range(4):
            act.wait_ge(sem("pw_added"), j + 1)
            nc.scalar.activation(paired(u_hi)[:, j], paired(work)[:, j], ACT.Copy).then_inc(sem("xh_done"), 2)
        residual_act(ph_merge, CF)
        norm_finish_act("ffn2", KT, CF, D, (u_h(NF),))

        for i, k in ph_ffn2.steps(act):
            split_hi(ph_ffn2, i, k)
            j, s, p = i * 2 + k // 2, (k // 2) % 2, ph_ffn2.pair(k)
            act.wait_ge(unit_done, ph_ffn2.unit(i, k) + 1)
            act.wait_ge(sem("f2_mul"), j + 1)
            for t in range(2):
                tile = j * 2 + (t + (k % 2) * FT)
                dst = (cva if k % 2 == 0 else cvb)[:, s, t, :]
                a = nc.scalar.activation(dst, ps[:, 2 * p + t, 0:T1], ACT.Identity,
                                         scale=ffn_dw[:, 0, bass.ds(tile, 1)], bias=ffn_dw[:, 1, bass.ds(tile + 2 * FT, 1)])
            a.then_inc(sem("f2_tap0"), 1)
            if k % 2:
                first = ph_ffn2.pair(k - 1)
                act.wait_ge(pair_read[first], ph_ffn2.used_before(i, k - 1) + 1)
                nc.scalar.activation(act_g[:, s], cva[:, s], ACT.Silu).then_inc(sem("f2_silu"), 1)
                act.wait_ge(sem("f2_mul"), j + 3)
                nc.scalar.activation(paired(a_hi)[:, j], act_a[:, s], ACT.Copy).then_inc(sem("ffn_hi"), 1)
        act.preload_act_table_set("natural_log_exp_and_others")
        residual_act(ph_down2, C1, group=4)
        norm_finish_act("final2", KT, C1, D)
        act.wait_ge(sem("out_turned"), 1)
        nc.scalar.activation(out_rows[:, 0, :], ps[:, 0:2, :], ACT.Copy).then_inc(sem("out_copied0"), 1)

    @block.tensor
    def _(pe):
        pe.wait_ge(sem("x_landed"), 48)
        for j in range(KT):
            cols = slice(j * P, (j + 1) * P)
            nc.tensor.transpose(ps[:, j, 0:META], meta_rows[:, cols], ident[0:META, 0:META])
            for b in range(2):
                mm = nc.tensor.transpose(ps[:, j, META + b * P:META + (b + 1) * P], x_rows[:, b, cols], ident)
            mm.then_inc(sem("x_turned"), 1)
        pe.wait_ge(sem("rows_landed"), 16 * 15)
        pe.wait_ge(sem("h_copied"), KT)
        nc.tensor.transpose(ps[:, 0, 0:GAIN_ROWS], gain_rows[:], ident[0:GAIN_ROWS, 0:GAIN_ROWS])
        for n in range(2):
            rows = 4 * FT
            nc.tensor.transpose(ps[:, 1 + n, 0:rows], dw_rows[:, n, :], ident[0:rows, 0:rows])
        for j in range(KT):
            mm = nc.tensor.transpose(ps[:, 3, j * CONV_W:(j + 1) * CONV_W], conv_rows[:, j * P:(j + 1) * P],
                                     ident[0:CONV_W, 0:CONV_W])
        mm.then_inc(sem("rows_turned"), 1)
        pe.wait_ge(sem("consts_ready"), 1)
        norm_pe("mix0", KT, T1)
        pe.wait_ge(sem("gains_ready"), 1)
        uh, ul = u_h(T1), u_l(T1)
        for i, k in ph_in.steps(pe):
            if k < 7:
                two_tiles(ph_in, i, k, T1, uh, ul, "mix0" if k == 0 else None)
            else:
                by_tokens(ph_in, i, k)
        pairs_read(pe, ph_in)
        norm_pe("cq", 3, T1)
        pe.wait_ge(sem("xl_done"), split_at["cq"] + 3)
        norm_pe("ckv", 2, T1)
        operands_ready("ckv", 2)
        lh, ll = (lambda kt: lat_hi[:, kt, :]), (lambda kt: lat_lo[:, kt, :])
        for i, k in ph_lat.steps(pe):
            s, p = begin_unit(ph_lat, i, k)
            if k < 2:
                for t in range(3):
                    dst = ps[:, 2 * p + t % 2, (t // 2) * T1:(t // 2 + 1) * T1]
                    mm = feature_tile(dst, s, 3, 384, t * P, lh, ll)
            elif k == 2:
                for t in range(4):
                    dst = ps[:, 2 * p + t // 2, (t % 2) * T1:(t % 2 + 1) * T1]
                    mm = feature_tile(dst, s, 2, 512, t * P, lh, ll, x0=3)
            else:
                for b in range(2):
                    mm = token_tile(ps[:, 2 * p + b, :], s, 2, 512, slice(0, 512),
                                    lambda kt: lat_hi[:, kt, b * P:(b + 1) * P],
                                    lambda kt: lat_lo[:, kt, b * P:(b + 1) * P], x0=3)
            mm.then_inc(unit_done, 1)
        pairs_read(pe, ph_lat)
        rope_pe(c("rot32"), [q_rope[:, 0, :], q_rope[:, 1, :], k_rope[:]], T1, 0, [0, 1])
        pe.wait_ge(sem("rope_done"), 3)
        mla.pe(mla_scores, head_values(v_a, VD))
        stk.pe(pair_scores(q_pad, k_b, before_b), head_values(v_b, HD))
        pe.wait_ge(sem("at_oev"), MLA_H + SB_H)
        turn_pe(lambda b, j: o1[:, b, j * P:(j + 1) * P], BLOCKS1, T1)
        residual_pe(ph_out0, T1, "o0", "ffn0", T1)
        ffn_pe(ph_ffn0, T1, "ffn0")
        down_pe("ffn0", ph_down0, "mix1")
        for i, k in ph_qk.steps(pe):
            two_tiles(ph_qk, i, k, T1, uh, ul, "mix1" if k == 0 else None)
        for i, k in ph_v.steps(pe):
            by_tokens(ph_v, i, k)
        pairs_read(pe, ph_v)
        chk.pe(pair_scores(q_pad_c, k_c, chunk_b), head_values(v_c, HD))
        pe.wait_ge(sem("at_oev"), chk.base + C_H)
        turn_pe(lambda b, j: o3[:, b, j * P:(j + 1) * P], BLOCKS1, T1)
        residual_pe(ph_out1, T1, "o1", "ffn1", T1)
        ffn_pe(ph_ffn1, T1, "ffn1")
        down_pe("ffn1", ph_down1, "final")
        pe.wait_ge(sem("rstd_done"), norm_at["final"][0] + 1)
        norm_pe("mix2", KT, T2)
        uh, ul = u_h(T2), u_l(T2)
        for i, k in ph_conv.steps(pe):
            two_tiles(ph_conv, i, k, T2, uh, ul, "mix2" if k == 0 else None)
        for i, k in ph_idx.steps(pe):
            if k:
                two_tiles(ph_idx, i, k, T2, uh, ul)
                continue
            s, p = begin_unit(ph_idx, i, k)
            feature_tile(ps[:, 2 * p, 0:T2], s, KT, 2 * ID + IH, 0, uh, ul)
            for b, x0 in enumerate((META, META + P)):
                mm = token_tile(ps[:, 2 * p + 1, b * IH:(b + 1) * IH], s, KT, 2 * ID + IH, slice(2 * ID, 2 * ID + IH),
                                lambda kt: u_hi[:, kt, x0:x0 + P], lambda kt: u_lo[:, kt, x0:x0 + P])
            mm.then_inc(unit_done, 1)
        for i, k in ph_proj.steps(pe):
            if k < 5:
                two_tiles(ph_proj, i, k, T2, uh, ul)
            else:
                s, p = begin_unit(ph_proj, i, k)
                for x0, dst in ((META, ps[:, 2 * p, 0:UC]), (META + P, ps[:, 2 * p + 1, 0:UC]),
                                (0, ps[:, 2 * p, UC:2 * UC])):
                    mm = token_tile(dst, s, KT, UC, slice(0, UC), lambda kt: u_hi[:, kt, x0:x0 + P],
                                    lambda kt: u_lo[:, kt, x0:x0 + P])
                mm.then_inc(unit_done, 1)
            if k == 0:
                pairs_read(pe, ph_idx)
                pairs_read(pe, ph_conv)
                rope_pe(c("rot64"), idx_tiles, T2, 3, [4, 5, 6, 7])
            if k == 2:
                pe.wait_ge(sem("rope_done"), 8)
                for n in range(IH):
                    e = n % 2
                    pe.wait_ge(sem("idx_pad"), n + 1)
                    wait(pe, sem("idx_relu"), n - 1)
                    nc.tensor.matmul(ps[:, 6 + e, 0:144], q_cur[:, e, META:META + P], ki[:, 0:144], start=True, stop=True)
                    nc.tensor.matmul(ps[:, 6 + e, 144:416], q_cur[:, e, META + P:T2], ki[:], start=True, stop=True)\
                        .then_inc(sem("idx_scored"), 1)
        for i, k in ph_gate.steps(pe):
            two_tiles(ph_gate, i, k, T2, uh, ul)
            if k < len(Q_ROPES):
                pairs_read(pe, ph_proj)
                pe.wait_ge(sem("idx_relu"), IH)
                lo, hi = Q_ROPES[k]
                rope_pe(c("rot128"), q_tiles[lo:hi], T2, 8 + lo, [4, 5, 6, 7])
        pairs_read(pe, ph_gate)
        pe.wait_ge(sem("rope_done"), 18)
        pe.wait_ge(sem("pick_ready"), 1)

        def dsa_scores(att, i, e, n):
            pe.wait_ge(sem("pad_done"), n + (att.base + 1))
            for b, (q0, nq, keys) in enumerate(att.blocks):
                end = keys[-1][0] + keys[-1][1]
                nc.tensor.matmul(att.S(e, b), q_cur[:, e % 2, q0:q0 + nq], k_d[:, i, 0:end], start=True, stop=False)
                mask = seen_b[0:META, 0:META] if b == 0 else pick[:, 0:144] if b == 1 else pick[:, 144:416]
                mm = nc.tensor.matmul(att.S(e, b), ident_b[0:nq, 0:nq], mask, start=False, stop=True)
            return mm

        def dsa_values(n, e, b, key):
            kv = (n // 4) if isinstance(n, int) else n // 4
            return v_d[0:BLOCKS2[b][2][key][1], key, kv * DH:(kv + 1) * DH]

        def gate_b_unit(n):
            if n % 2:
                two_tiles(ph_gate_b, 0, n // 2, T2, uh, ul)

        dsa.pe(dsa_scores, dsa_values, gate_b_unit)
        pe.wait_ge(sem("at_oev"), dsa.base + 8)
        pairs_read(pe, ph_gate_b)
        turn_pe(lambda b, j: o_dsa(j, b), BLOCKS2, T2)
        operands_ready("o2")

        def channel_sums(j):
            pe.wait_ge(sem("conv_tap"), 2 * CONV_W * (j + 1))
            for kt in (2 * j, 2 * j + 1):
                mm = nc.tensor.matmul(ps[:, 7, 0:T2], ones, work[:, kt, :], start=kt == 0, stop=kt == KT - 1)
            if j == KT // 2 - 1:
                mm.then_inc(sem("ln_sum"), 1)

        for i, k in ph_wo.steps(pe):
            two_tiles(ph_wo, i, k, T2, uh, ul)
            channel_sums(k)
        for kt in range(KT):
            pe.wait_ge(sem("ln_sq"), kt + 1)
            mm = nc.tensor.matmul(ps[:, 6, 0:T2], ones, cin[:, kt, 0:T2], start=kt == 0, stop=kt == KT - 1)
        mm.then_inc(sem("ln_var"), 1)
        for i, k in ph_pw.steps(pe):
            two_tiles(ph_pw, i, k, T2, uh, ul, "ln" if k == 0 else None)
        residual_pe(ph_merge, T2, "merge", "ffn2", NF)
        ffn_pe(ph_ffn2, NF, "ffn2")
        down_pe("ffn2", ph_down2, "final2")
        pe.wait_ge(sem("un_done"), norm_at["final2"][1] + KT)
        for t in range(2):
            for j in range(KT):
                mm = nc.tensor.transpose(ps[:, 2 * t + j // 4, (j % 4) * P:(j % 4 + 1) * P],
                                         work[:, j, t * P:(t + 1) * P], ident)
            mm.then_inc(sem("out_turned"), 1)

    @block.vector
    def _(dve):
        links = [0]

        def link(ins):
            links[0] += 1
            ins.then_inc(sem("vector_link"), 1)
            dve.wait_ge(sem("vector_link"), links[0])

        dve.sem_inc(sem("ffn_lo"), 2)
        dve.sem_inc(sem("f2_mul"), 2)
        dve.wait_ge(sem("x_landed"), 48)
        nc.vector.memset(eps[:], EPS)
        for n, name in enumerate(("ident", "chunk_mask", "before_mask", "seen_mask")):
            a = nc.vector.tensor_copy(masks[:, n, :], c(name))
        a.then_inc(sem("consts_ready"), 1)
        dve.wait_ge(sem("rows_turned"), 1)
        nc.vector.tensor_copy(gains[:], ps[:, 0, 0:GAIN_ROWS])
        nc.vector.tensor_copy(ffn_dw[:], ps[:, 1:3, 0:4 * FT])
        nc.vector.tensor_copy(conv_w[:], ps[:, 3, 0:KT * CONV_W].rearrange("p (k w) -> p k w", w=CONV_W))\
            .then_inc(sem("gains_ready"), 1)
        for k in range(AHEAD):
            split_lo(prologue, 0, k)
        dve.wait_ge(sem("gains_ready"), 1)
        dve.wait_ge(sem("h_copied"), KT)
        norm_dve("mix0", h_at(C1), ("mix", 0), KT, T1, (u_h(T1), u_l(T1)))
        for i, k in ph_in.steps(dve):
            split_lo(ph_in, i, k)
        norm_dve("cq", lambda kt: lat[:, kt, :], ("cq", 0), 3, T1,
                 (lambda kt: lat_hi[:, kt, :], lambda kt: lat_lo[:, kt, :]))
        norm_dve("ckv", lambda kt: lat[:, 3 + kt, :], ("ckv", 0), 2, T1,
                 (lambda kt: lat_hi[:, 3 + kt, :], lambda kt: lat_lo[:, 3 + kt, :]))
        for i, k in ph_lat.steps(dve):
            split_lo(ph_lat, i, k)
        pairs_read(dve, ph_lat)
        rope_dve([q_rope[:, 0, :], q_rope[:, 1, :], k_rope[:]], c("cos32"), c("sin32"), T1, 0, rope_t, [0, 1])
        mla.dve((NOPE + ROPE_D) ** -0.5, mla.S)

        def softplus_sums(n, e):
            z = ps[:, stk.s_banks[e], 0:stk.width]
            st = stick[:, e % 2]
            dve.wait_ge(sem("st_ln"), n + 1)
            wait(dve, sem("st_scan"), n - 1)
            nc.vector.scalar_tensor_tensor(out=st[:, 2, :], in0=z, scalar=0.0, in1=st[:, 0, :], op0=ALU.max, op1=ALU.add)\
                .then_inc(sem("st_sp"), 1)
            dve.wait_ge(sem("st_sp"), n + 1)
            wait(dve, sem("st_t"), n - 1)
            for b, (_, _, keys) in enumerate(BLOCKS1):
                lo, hi = stk.cols[b], stk.cols[b] + sum(m for _, m in keys)
                rev = lambda t: t[:, lo:hi][:, ::-1]
                a = nc.vector.tensor_tensor_scan(rev(st[:, 3, :]), wide_ones[:, 0:hi - lo], rev(st[:, 2, :]), 0.0,
                                                 ALU.mult, ALU.add)
            a.then_inc(sem("st_scan"), 1)
            dve.wait_ge(sem("st_scan"), n + 1)
            wait(dve, sem("at_p"), n + (stk.base - 1))
            nc.vector.tensor_tensor(st[:, 4, :], z, st[:, 3, :], ALU.subtract).then_inc(sem("st_t"), 1)

        def stick_out(n, e):
            dve.wait_ge(sem("at_o"), n + (stk.base + 1))
            for b in range(2):
                a = nc.vector.tensor_copy(stk.o(n, b), stk.O(e, b))
            a.then_inc(sem("at_oev"), 1)

        for i, e in stk.steps(dve):
            softplus_sums(stk.head(i, e), e)
            if (m := stk.head(i, e, 3)) is not None:
                stick_out(m, (e - 3) % 4)
        for m in range(SB_H - 3, SB_H):
            stick_out(m, m % 4)
        turn_dve("o0", T1)
        residual_dve(ph_out0, C1)
        norm_dve("ffn0", h_at(C1), ("ffn", 0), KT, T1, (u_h(T1), u_l(T1)))
        ffn_dve("ffn0", ph_ffn0)
        residual_dve(ph_down0, C1, group=4)
        norm_dve("mix1", h_at(C1), ("mix", KT), KT, T1, (u_h(T1), u_l(T1)))
        for i, k in ph_qk.steps(dve):
            split_lo(ph_qk, i, k)
        for i, k in ph_v.steps(dve):
            split_lo(ph_v, i, k)
        dve.wait_ge(sem("bias_landed"), 16)

        def add_bias(att, n, e):
            wait(dve, sem("at_p"), n + (att.base - 1))
            hb = bias_h[:, n, :]
            nc.vector.scalar_tensor_tensor(out=biased_ap(e, 0)[:, ::-1], in0=att.S(e, 0)[:, ::-1], scalar=HD ** -0.5,
                                           in1=hb[:, 0:P], op0=ALU.mult, op1=ALU.add)
            nc.vector.scalar_tensor_tensor(out=biased_ap(e, 1)[:, ::-1], in0=att.S(e, 1)[:, ::-1], scalar=HD ** -0.5,
                                           in1=hb, op0=ALU.mult, op1=ALU.add).then_inc(sem("biased"), 1)
            dve.wait_ge(sem("biased"), n + 1)

        chk.dve(1.0, lambda e, b: biased_ap(e, b), add_bias)
        turn_dve("o1", T1)
        residual_dve(ph_out1, C1)
        norm_dve("ffn1", h_at(C1), ("ffn", KT), KT, T1, (u_h(T1), u_l(T1)))
        ffn_dve("ffn1", ph_ffn1)
        residual_dve(ph_down1, C1, group=4)
        norm_dve("final", h_at(C1), ("final", 0), KT, T1, into=h_at(C1))
        dve.wait_ge(sem("un_done"), norm_at["final"][1] + KT)
        norm_dve("mix2", h_at(C2), ("mix2", 0), KT, T2, (u_h(T2), u_l(T2)))

        conv_steps = [0]

        def conv(steps):
            for _ in range(steps):
                j, w = divmod(conv_steps[0], CONV_W)
                if j == KT // 2:
                    return
                conv_steps[0] += 1
                if w == 0:
                    up = 2 * j + 1
                    dve.wait_ge(pair_read[ph_conv.pair(up)], ph_conv.used_before(0, up) + 1)
                    dve.wait_ge(sem("zeroed"), 6)
                for tile in (2 * j, 2 * j + 1):
                    src, tap = cin[:, tile, w:w + T2], conv_w[:, tile, w:w + 1]
                    done = (j * CONV_W + w) * 2 + tile % 2
                    if w == 0:
                        bias = GAINS["dw_b"][0] + tile
                        a = nc.vector.tensor_scalar(work[:, tile, :], src, tap, gains[:, bias:bias + 1], ALU.mult, ALU.add)
                    else:
                        dve.wait_ge(sem("conv_tap"), done - 1)
                        a = nc.vector.scalar_tensor_tensor(out=work[:, tile, :], in0=src, scalar=tap, in1=work[:, tile, :],
                                                           op0=ALU.mult, op1=ALU.add)
                    a.then_inc(sem("conv_tap"), 1)

        for i, k in ph_conv.steps(dve):
            split_lo(ph_conv, i, k)
            if k == 0:
                dve.wait_ge(sem("xl_done"), split_at["mix2"] + KT)
            if k >= 2:
                conv(4)
            if k % 2:
                p, gate = ph_conv.pair(k), ph_conv.pair(k - 1)
                dve.wait_ge(unit_done, ph_conv.unit(i, k) + 1)
                dve.wait_ge(pair_read[gate], ph_conv.used_before(i, k - 1) + 1)
                nc.vector.tensor_tensor(paired(cin)[:, k // 2, :, CONV_W - 1:], pair_ap(p, T2), sg4[:, (k // 2) % 2],
                                        ALU.mult).then_inc(pair_read[p], 1)
        for i, k in ph_idx.steps(dve):
            split_lo(ph_idx, i, k)
            conv(4)

        spans = ((1, 0, 144), (2, 144, 416))
        rounds = (TOPK - 1) // 8

        def link_conv(ins, steps):
            links[0] += 1
            ins.then_inc(sem("vector_link"), 1)
            conv(steps)
            dve.wait_ge(sem("vector_link"), links[0])

        def top_round(r):
            src = acc if r == 0 else left
            for b, lo, hi in spans:
                a = nc.vector.max(top8[:, b - 1, :], src[:, lo:hi])
            link_conv(a, 1)
            if r < rounds:
                for b, lo, hi in spans:
                    a = nc.vector.match_replace(left[:, lo:hi], top8[:, b - 1, :], src[:, lo:hi], LOWEST)
                link_conv(a, 1)

        for i, k in ph_proj.steps(dve):
            split_lo(ph_proj, i, k)
            if k in (0, 2, 3):
                conv(4)
            elif k == 1:
                rope_dve(idx_tiles, c("cos64"), c("sin64"), T2, 3, rope4, [4, 5, 6, 7])
            if k == 2:
                for n in range(IH):
                    dve.wait_ge(sem("idx_relu"), n + 1)
                    wait(dve, sem("idx_acc"), n)
                    for b, lo, hi in spans:
                        if n == 0:
                            a = nc.vector.tensor_scalar(acc[:, lo:hi], dots(0)[:, lo:hi], wi[:, b, 0:1], None, ALU.mult)
                        else:
                            a = nc.vector.scalar_tensor_tensor(out=acc[:, lo:hi], in0=dots(n % 2)[:, lo:hi],
                                                               scalar=wi[:, b, n:n + 1], in1=acc[:, lo:hi],
                                                               op0=ALU.mult, op1=ALU.add)
                    a.then_inc(sem("idx_acc"), 1)
                dve.wait_ge(sem("idx_acc"), IH)
                for lo, hi in ((META, 144), (288, 416)):
                    nc.vector.tensor_tensor(acc[:, lo:hi], acc[:, lo:hi], c("seen_mask"), ALU.add)
                nc.vector.memset(acc[:, 0:META], BONUS)
                link_conv(nc.vector.memset(acc[:, 144:144 + META], BONUS), 1)
            if k >= 4:
                for r in range(2 * (k - 4), 2 * (k - 4) + 2):
                    top_round(r)
        for i, k in ph_gate.steps(dve):
            split_lo(ph_gate, i, k)
            for r in range(4 + 2 * k, min(6 + 2 * k, rounds + 1)):
                top_round(r)
            if k < len(Q_ROPES):
                lo, hi = Q_ROPES[k]
                rope_dve(q_tiles[lo:hi], c("cos128"), c("sin128"), T2, 8 + lo, rope4, [4, 5, 6, 7])
        last = (TOPK - 1) % 8
        for b, lo, hi in spans:
            thr = top8[:, b - 1, last:last + 1]
            nc.vector.tensor_scalar(above[:, lo:hi], acc[:, lo:hi], thr, None, ALU.is_gt)
            a = nc.vector.tensor_scalar(equal[:, lo:hi], acc[:, lo:hi], thr, None, ALU.is_equal)
        link(a)
        for b, lo, hi in spans:
            nc.vector.reduce_sum(need[:, b - 1:b], above[:, lo:hi], AX)
            a = nc.vector.tensor_tensor_scan(left[:, lo:hi], wide_ones[:, 0:hi - lo], equal[:, lo:hi], 0.0, ALU.mult, ALU.add)
        link(a)
        link(nc.vector.tensor_scalar(need[:], need[:], -1.0, float(TOPK), ALU.mult, ALU.add))
        for b, lo, hi in spans:
            a = nc.vector.scalar_tensor_tensor(out=left[:, lo:hi], in0=left[:, lo:hi], scalar=need[:, b - 1:b],
                                               in1=equal[:, lo:hi], op0=ALU.is_le, op1=ALU.mult)
        link(a)
        link(nc.vector.tensor_tensor(left, left, above, ALU.add))
        link(nc.vector.tensor_scalar(left, left, -NEG, NEG, ALU.mult, ALU.add))
        for lo, hi in ((META, 144), (288, 416)):
            a = nc.vector.tensor_tensor(left[:, lo:hi], left[:, lo:hi], c("seen_mask"), ALU.add)
        link(a)
        nc.vector.tensor_copy(pick[:], left).then_inc(sem("pick_ready"), 1)

        def gate_b(n):
            if n % 2:
                split_lo(ph_gate_b, 0, n // 2)
            conv(4)

        dsa.dve(DH ** -0.5, dsa.S, between=gate_b)
        turn_dve("o2", T2)
        for i, k in ph_wo.steps(dve):
            split_lo(ph_wo, i, k)
            conv(5)
            p = ph_wo.pair(k)
            dve.wait_ge(unit_done, ph_wo.unit(i, k) + 1)
            dve.wait_ge(sem("gates_b"), 1)
            hv = paired(gates)[:, 4 + k]
            nc.vector.tensor_tensor(hv, pair_ap(p, T2), hv, ALU.mult).then_inc(pair_read[p], 1)
        conv(KT // 2 * CONV_W)

        dve.wait_ge(sem("ln_sum"), 1)
        link(nc.vector.tensor_scalar(log_ms[:], ps[:, 7, 0:T2], 1.0 / D, None, ALU.mult))
        for kt in range(KT):
            nc.vector.tensor_tensor(work[:, kt, :], work[:, kt, :], log_ms[:], ALU.subtract).then_inc(sem("ln_centred"), 1)
        dve.wait_ge(sem("ln_rstd"), 1)

        def ln_lo(kt):
            dve.wait_ge(sem("xh_done"), split_at["ln"] + kt + 1)
            nc.vector.tensor_tensor(u_lo[:, kt, :], work[:, kt, :], u_hi[:, kt, :].bitcast(F32), ALU.subtract)\
                .then_inc(sem("xl_done"), 1)

        for kt in range(KT):
            nc.vector.tensor_tensor(work[:, kt, :], work[:, kt, :], rstd[:], ALU.mult).then_inc(sem("ln_scaled"), 1)
            if kt >= 2:
                ln_lo(kt - 2)
        for kt in (KT - 2, KT - 1):
            ln_lo(kt)
        dve.wait_ge(sem("xl_done"), split_at["ln"] + KT)
        for i, k in ph_pw.steps(dve):
            split_lo(ph_pw, i, k)
            p = ph_pw.pair(k)
            dve.wait_ge(unit_done, ph_pw.unit(i, k) + 1)
            nc.vector.tensor_tensor(paired(work)[:, k], pair_ap(p, T2), paired(gates)[:, k], ALU.mult)\
                .then_inc(pair_read[p], 1)
            dve.wait_ge(pair_read[p], ph_pw.used_before(i, k) + 1)
            dve.wait_ge(pair_read[ph_wo.pair(k)], ph_wo.used_before(0, k) + 1)
            nc.vector.tensor_tensor(paired(work)[:, k], paired(work)[:, k], paired(gates)[:, 4 + k], ALU.add)\
                .then_inc(sem("pw_added"), 1)
        for j in range(4):
            dve.wait_ge(sem("xh_done"), split_at["merge"] + 2 * j + 2)
            nc.vector.tensor_tensor(paired(u_lo)[:, j], paired(work)[:, j], paired(u_hi)[:, j].bitcast(F32), ALU.subtract)\
                .then_inc(sem("xl_done"), 2)
        residual_dve(ph_merge, C2)
        norm_dve("ffn2", h_at(CF), ("ffn2", 0), KT, NF, (u_h(NF), u_l(NF)))

        for i, k in ph_ffn2.steps(dve):
            split_lo(ph_ffn2, i, k)
            j, s, p = i * 2 + k // 2, (k // 2) % 2, ph_ffn2.pair(k)
            cv = cva if k % 2 == 0 else cvb
            dve.wait_ge(sem("f2_tap0"), ph_ffn2.unit(i, k) - ph_ffn2.u0 + 1)
            for w in (1, 2):
                for t in range(2):
                    tile = j * 2 + (t + (k % 2) * FT)
                    tap = ffn_dw[:, 0, bass.ds(tile + 2 * FT, 1)] if w == 1 else ffn_dw[:, 1, bass.ds(tile, 1)]
                    a = nc.vector.scalar_tensor_tensor(out=cv[:, s, t, :], in0=ps[:, 2 * p + t, w:w + T1], scalar=tap,
                                                       in1=cv[:, s, t, :], op0=ALU.mult, op1=ALU.add)
                if w == 1:
                    a.then_inc(sem("f2_tap1"), 1)
                    dve.wait_ge(sem("f2_tap1"), ph_ffn2.unit(i, k) - ph_ffn2.u0 + 1)
            a.then_inc(pair_read[p], 1)
            if k % 2:
                dve.wait_ge(sem("f2_silu"), j + 1)
                dve.wait_ge(pair_read[p], ph_ffn2.used_before(i, k) + 1)
                dve.wait_ge(sem("ffn_lo"), j + (FFN["ffn2"] + 1))
                nc.vector.tensor_tensor(act_a[:, s], act_g[:, s], cvb[:, s], ALU.mult).then_inc(sem("f2_mul"), 1)
                ffn_lo("ffn2", j, s)
        residual_dve(ph_down2, C1, group=4)
        norm_dve("final2", h_at(C1), ("final2", 0), KT, T1)
        dve.wait_ge(sem("out_turned"), 2)
        nc.vector.tensor_copy(out_rows[:, 1, :], ps[:, 2:4, :]).then_inc(sem("out_copied1"), 1)
    ctx.close()


_INS = ["x", "ev_w_in", "ev_g_cq", "ev_w_uq", "ev_g_ckv", "ev_w_ukv", "ev_w_out", "od_w_qkv", "od_rel_bias",
        "od_w_out", "g_mix", "g_ffn", "w_gate", "w_up", "w_down", "g_final", "meta_tokens_2", "mix_norm_g_2",
        "w_in_2", "conv_ln_g_2", "conv_ln_b_2", "conv_dw_w_2", "conv_dw_b_2", "conv_pw_out_2", "attn_w_o_2",
        "w_merge_out_2", "ffn_norm_g_2", "ffn_up_2", "ffn_dw_w_2", "ffn_dw_b_2", "ffn_down_2", "final_norm_g_2"]


def kernel(**inputs):
    import concourse.bacc as bacc
    from concourse.bass_utils import run_bass_kernel_spmd

    nc = bacc.Bacc("TRN2", target_bir_lowering=False, num_devices=1)
    arrays, args = {}, {}
    for name in _INS:
        a = np.ascontiguousarray(inputs[name])
        arrays[f"in_{name}"] = a
        args[name] = nc.dram_tensor(f"in_{name}", a.shape, mybir.dt.from_np(a.dtype), kind="ExternalInput").ap()
    constants, where = shape_constants()
    arrays["in_constants"] = constants
    args["constants"] = nc.dram_tensor("in_constants", constants.shape, F32, kind="ExternalInput").ap()
    args["out"] = nc.dram_tensor("out_0", (1, SEQ, D), F32, kind="ExternalOutput").ap()
    build(nc, where=where, **args)
    r = run_bass_kernel_spmd(nc, [arrays], core_ids=[0])
    return r.results[0]["out_0"]
```

```python
from contextlib import ExitStack

import numpy as np

import concourse.bass as bass
from concourse import mybir

F32 = mybir.dt.float32
F32R = mybir.dt.float32r
BF16 = mybir.dt.bfloat16
ACT = mybir.ActivationFunctionType
ALU = mybir.AluOpType
AX = mybir.AxisListType.X

P = 128
SEQ, D, META = 256, 1024, 16
T1, T2 = SEQ, SEQ + META
KT = D // P
DFF = 2816
FT = DFF // P
UC = 256
UNIT = KT * UC
RING, AHEAD, RAW = 4, 2, 4
EPS = 1e-6

MLA_H, NOPE, ROPE_D, VD = 8, 64, 32, 64
QL, KVL = 384, 256
SB_H, C_H, HD = 8, 16, 64
DH, KVH, IH, ID = 128, 2, 8, 64
TOPK = min(256, T2 // 4)
CONV_W, CHUNK = 31, 64
NEG, LOWEST, BONUS = -1e30, -3e38, 1e30

DOWN_KT = [(0, 6), (6, 6), (12, 5), (17, 5)]
DOWN_WIDTHS = [n * UC for _ in range(D // UC) for _, n in DOWN_KT]

BLOCKS1 = [(0, P, [(0, P)]), (P, P, [(0, P), (P, P)])]
BLOCKS2 = [
    (0, META, [(0, META)]),
    (META, P, [(0, META), (META, P)]),
    (META + P, P, [(0, META), (META, P), (META + P, P)]),
]

GAINS = {}
for _name, _rows in (("mix", 16), ("ffn", 16), ("final", 8), ("cq", 3), ("ckv", 2), ("mix2", 8),
                     ("ln_g", 8), ("ln_b", 8), ("dw_b", 8), ("ffn2", 8), ("final2", 8)):
    GAINS[_name] = (sum(r for _, r in GAINS.values()), _rows)
GAIN_ROWS = sum(r for _, r in GAINS.values())


def shape_constants():
    def half_rotation(dim):
        r = np.zeros((P, P), np.float32)
        for base in range(0, P, dim):
            for i in range(dim // 2):
                r[base + i, base + dim // 2 + i] = -1.0
                r[base + dim // 2 + i, base + i] = 1.0
        return r.T

    def tables(dim, n):
        half = dim // 2
        inv = np.float32(10000.0) ** (-np.arange(0, dim, 2, dtype=np.float32) / np.float32(dim))
        ang = np.arange(n, dtype=np.float32)[:, None] * inv[None, :].astype(np.float32)
        rows = (np.arange(P) % dim) % half
        return np.cos(ang).T[rows], np.sin(ang).T[rows]

    q, k = np.arange(P)[:, None], np.arange(P)[None, :]
    parts = {
        "ident": np.eye(P), "ones": np.ones((P, T2)),
        "chunk_mask": np.where(k // CHUNK <= q // CHUNK, 0.0, NEG),
        "before_mask": np.where(k < q, 0.0, NEG),
        "seen_mask": np.where(k <= q, 0.0, LOWEST),
        "rot32": half_rotation(32), "rot128": half_rotation(128), "rot64": half_rotation(64),
    }
    for name, dim, n in (("32", 32, T1), ("128", 128, T2), ("64", 64, T2)):
        parts["cos" + name], parts["sin" + name] = tables(dim, n)
    where, at = {}, 0
    for name, a in parts.items():
        where[name] = (at, a.shape[1])
        at += a.shape[1]
    return np.concatenate([a.astype(np.float32) for a in parts.values()], axis=1), where


def wait(eng, sem, value):
    if isinstance(value, int) and value <= 0:
        return
    eng.wait_ge(sem, value)


class Phase:

    def __init__(self, plan, units, body, group=1, dmas=None, peel=0, pairs=4, widths=None):
        self.u0, self.units, self.body, self.group = plan["units"], units, body, group
        self.turns, self.rest = divmod(units, body)
        self.peel, self.pairs = peel, pairs
        self.groups = body // group
        self.used = list(plan["used"])
        self.dmas = dmas or [1] * units
        self.widths = widths or [UNIT] * units
        plan["units"] += units
        for n, d in enumerate(self.dmas):
            plan["loads"][(self.u0 + n) % RAW] += 16 * d
        for n in range(units // group):
            plan["used"][n % self.groups % pairs] += 1
        self.used_after = list(plan["used"])
        plan["phases"].append(self)

    def steps(self, eng):
        looped = self.turns - self.peel if self.turns - self.peel > 1 else 0
        if looped:
            with eng.Fori(0, looped) as i:
                for k in range(self.body):
                    yield i, k
        for i in range(looped, self.turns):
            for k in range(self.body):
                yield i, k
        for k in range(self.rest):
            yield self.turns, k

    def unit(self, i, k):
        return i * self.body + (self.u0 + k)

    def pair(self, k):
        return k // self.group % self.groups % self.pairs

    def used_before(self, i, k):
        per_turn = max(1, self.groups // self.pairs)
        return i * per_turn + (self.used[self.pair(k)] + k // self.group % self.groups // self.pairs)


def build(nc, x, ev_w_in, ev_g_cq, ev_w_uq, ev_g_ckv, ev_w_ukv, ev_w_out, od_w_qkv, od_rel_bias,
          od_w_out, g_mix, g_ffn, w_gate, w_up, w_down, g_final, meta_tokens_2, mix_norm_g_2,
          w_in_2, conv_ln_g_2, conv_ln_b_2, conv_dw_w_2, conv_dw_b_2, conv_pw_out_2, attn_w_o_2,
          w_merge_out_2, ffn_norm_g_2, ffn_up_2, ffn_dw_w_2, ffn_dw_b_2, ffn_down_2,
          final_norm_g_2, constants, where, out, debug=None):
    ctx = ExitStack()
    sems = {}

    def sem(name):
        if name not in sems:
            sems[name] = ctx.enter_context(nc.semaphore(name))
        return sems[name]

    def sb(name, shape, dt=F32, scope=None):
        return (scope or ctx).enter_context(nc.sbuf_tensor(name, shape, dt))

    raw = [sb(f"raw{s}", [P, UNIT]) for s in range(RAW)]
    w_hi = [sb(f"w_hi{s}", [P, UNIT], F32R) for s in range(RING)]
    w_lo = [sb(f"w_lo{s}", [P, UNIT], F32R) for s in range(RING)]
    h = sb("h", [P, KT, T2])
    u_hi = sb("u_hi", [P, KT, T2], F32R)
    u_lo = sb("u_lo", [P, KT, T2], F32R)
    work = sb("work", [P, KT, T2])
    const = sb("const", [P, constants.shape[1]])
    masks = sb("masks", [P, 4, P], BF16)
    gains = sb("gains", [P, GAIN_ROWS])
    ffn_dw = sb("ffn_dw", [P, 2, 2 * FT * 2])
    conv_w = sb("conv_w", [P, KT, CONV_W])
    eps = sb("eps", [P, 1])
    log_ms = sb("log_ms", [P, T2])
    rstd = sb("rstd", [P, T2])

    def c(name):
        at, n = where[name]
        return const[:, at:at + n]

    ident, wide_ones = c("ident"), c("ones")
    ones = wide_ones[:, 0:P]
    ident_b, chunk_b, before_b, seen_b = (masks[:, n, :] for n in range(4))

    with ExitStack() as s:
        x_rows = sb("x_rows", [P, 2, D], scope=s)
        meta_rows = sb("meta_rows", [META, D], scope=s)
        x_stat = sb("x_stat", [P, 3, 2], scope=s)
        x_diag = sb("x_diag", [P, 2, P], scope=s)
        gain_rows = sb("gain_rows", [GAIN_ROWS, P], scope=s)
        dw_rows = sb("dw_rows", [2 * 2 * FT, 2, P], scope=s)
        conv_rows = sb("conv_rows", [CONV_W, D], scope=s)
    with ExitStack() as s:
        with ExitStack() as t:
            lat_hi = sb("lat_hi", [P, 5, T1], F32R, scope=t)
            lat_lo = sb("lat_lo", [P, 5, T1], F32R, scope=t)
        p1 = sb("p1", [P, 2, 512], scope=s)
        pt1 = sb("pt1", [P, 2, 1024], scope=s)
        stat1 = sb("stat1", [P, 4, 4, 3], scope=s)
        k_rope = sb("k_rope", [P, T1], scope=s)
        with ExitStack() as t:
            q_nope = sb("q_nope", [P, 4, T1], scope=t)
            q_rope = sb("q_rope", [P, 2, T1], scope=t)
            k_nope = sb("k_nope", [P, 4, T1], scope=t)
            v_a = sb("v_a", [P, 2, MLA_H * VD], scope=t)
            lat = sb("lat", [P, 5, T1], scope=t)
        stick = sb("stick", [P, 2, 5, 384], scope=s)
        sb("mla_place", [P, 19 * T1 - 10 * 384], scope=s)
        q_b = sb("q_b", [P, 4, T1], scope=s)
        k_b = sb("k_b", [P, 4, T1], scope=s)
        v_b = sb("v_b", [P, 2, SB_H * HD], scope=s)
        q_pad = sb("q_pad", [P, 4, T1], scope=s)
        q_pad_r = sb("q_pad_r", [P, 4, T1], scope=s)
        rope_t = sb("rope_t", [P, 2, T2], scope=s)
    with ExitStack() as s:
        a_hi = sb("a_hi", [P, FT, T1], F32R, scope=s)
        a_lo = sb("a_lo", [P, FT, T1], F32R, scope=s)
        act_g = sb("act_g", [P, 2, 2, T1], scope=s)
        act_a = sb("act_a", [P, 2, 2, T1], scope=s)
        cva = sb("cva", [P, 2, 2, T1], scope=s)
        cvb = sb("cvb", [P, 2, 2, T1], scope=s)
    with ExitStack() as s:
        p3 = sb("p3", [P, 2, 512], scope=s)
        pt3 = sb("pt3", [P, 2, 1024], scope=s)
        stat3 = sb("stat3", [P, 4, 4, 3], scope=s)
        qk_c = sb("qk_c", [P, 16, T1], scope=s)
        q_c, k_c = qk_c[:, 0:8, :], qk_c[:, 8:16, :]
        v_c = sb("v_c", [P, 2, D], scope=s)
        q_pad_c = sb("q_pad_c", [P, 4, T1], scope=s)
        biased = sb("biased", [P, 2, 512], scope=s)
        bias_h = sb("bias_h", [P, C_H, 2 * P], scope=s)
    with ExitStack() as s:
        with ExitStack() as t:
            p4 = sb("p4", [P, 2, META + (META + P) + T2], scope=t)
        with ExitStack() as t:
            rope4 = sb("rope4", [P, 2, T2], scope=t)
        sb("p4_place", [P, 2, META + (META + P) + T2], scope=s)
        stat4 = sb("stat4", [P, 4, 4, 3], scope=s)
        gates = sb("gates", [P, 2 * KT, T2 - META + 2], scope=s)
        q_d = sb("q_d", [P, 8, T2], scope=s)
        k_d = sb("k_d", [P, KVH, T2], scope=s)
        v_d = sb("v_d", [P, 3, KVH * DH], scope=s)
        wi = sb("wi", [P, 3, IH], scope=s)
        q_cur = sb("q_cur", [P, 2, T2], scope=s)
        pick = sb("pick", [P, 416], BF16, scope=s)
        top8 = sb("top8", [P, 2, 8], scope=s)
        need = sb("need", [P, 2], scope=s)
        with ExitStack() as t:
            pt4 = sb("pt4", [P, 2, 1024], scope=t)
        qi = sb("qi", [P, IH * ID // P, T2], scope=s)
        ki = sb("ki", [P, T2], scope=s)
        sg4 = sb("sg4", [P, 2, 2, T2], scope=s)
        cin = sb("cin", [P, KT, CONV_W - 1 + T2], scope=s)
        o_meta = sb("o_meta", [META, D], scope=s)
    with ExitStack() as s:
        out_rows = sb("out_rows", [P, 2, D], scope=s)
    o1 = o3 = work[:].rearrange("p a b -> p (a b)")[:, 0:2 * D].rearrange("p (b d) -> p b d", b=2)
    picks = gates[:, 12:16, :].rearrange("p a b -> p (a b)")
    acc, left = picks[:, 0:416], picks[:, 416:832]
    sg_flat = sg4[:].rearrange("p a b c -> p (a b c)")

    def dots(n):
        return sg_flat[:, n * 416:(n + 1) * 416]

    above, equal = dots(0), dots(1)

    def biased_ap(e, b):
        return biased[:, e % 2, chk.cols[b]:chk.cols[b] + (b + 1) * P]

    ps = ctx.enter_context(nc.psum_tensor("ps", [P, 8, 512], F32))

    def paired(t):
        return t.rearrange("p (j t) n -> p j t n", t=2)

    def pw(s, nk, n):
        return s[:, 0:nk * n].rearrange("p (k n) -> p k n", k=nk)

    plan = {"units": 0, "loads": [0] * RAW, "used": [0, 0, 0, 0], "phases": []}
    ph_in = Phase(plan, 9, 9, dmas=[1, 1, 5, 1, 1, 1, 1, 1, 1], pairs=3)
    ph_lat = Phase(plan, 4, 4, dmas=[6, 6, 2, 2], widths=[3 * 384] * 2 + [2 * 512] * 2, pairs=2)
    ph_out0 = Phase(plan, 4, 4, pairs=3)
    ph_ffn0 = Phase(plan, 2 * DFF // UC, 4)
    ph_down0 = Phase(plan, 16, 8, group=4, widths=DOWN_WIDTHS)
    ph_qk = Phase(plan, 8, 4)
    ph_v = Phase(plan, 4, 4)
    ph_out1 = Phase(plan, 4, 4, pairs=3)
    ph_ffn1 = Phase(plan, 2 * DFF // UC, 4)
    ph_down1 = Phase(plan, 16, 8, group=4, widths=DOWN_WIDTHS)
    ph_conv = Phase(plan, 8, 8, pairs=2)
    ph_idx = Phase(plan, 3, 3, dmas=[3, 1, 1], widths=[KT * (2 * ID + IH), UNIT, UNIT], pairs=2)
    ph_proj = Phase(plan, 6, 6, pairs=2)
    ph_gate = Phase(plan, 5, 5, pairs=2)
    ph_gate_b = Phase(plan, 3, 3, pairs=1)
    ph_wo = Phase(plan, 4, 4, pairs=3)
    ph_pw = Phase(plan, 4, 4)
    ph_merge = Phase(plan, 4, 4, pairs=3)
    ph_ffn2 = Phase(plan, 2 * DFF // UC, 4)
    ph_down2 = Phase(plan, 16, 8, group=4, peel=1, widths=DOWN_WIDTHS)
    units = plan["units"]
    landed, widths, count = [], [], [0] * RAW
    for ph in plan["phases"]:
        widths += ph.widths
        for n, d in enumerate(ph.dmas):
            count[(ph.u0 + n) % RAW] += 16 * d
            landed.append(count[(ph.u0 + n) % RAW])

    raw_landed = [sem(f"raw_landed{n}") for n in range(RAW)]
    hi_done, lo_done, unit_done = sem("hi_done"), sem("lo_done"), sem("unit_done")
    pair_read = [sem(f"pair_read{n}") for n in range(4)]

    def pairs_read(eng, ph):
        for n in range(4):
            wait(eng, pair_read[n], ph.used_after[n])

    def split_unit(ph, i, k):
        t = ph.u0 + (i * ph.body if isinstance(i, int) else 0) + k + AHEAD
        if isinstance(i, int):
            return (0, t, widths[t]) if t < units else None
        turns = range(ph.turns - ph.peel)
        return i, t, max(widths[t + j * ph.body] for j in turns)

    def split_hi(ph, i, k):
        if (u := split_unit(ph, i, k)) is None:
            return
        turn, t, n = u
        nc.scalar.wait_ge(raw_landed[t % RAW], turn * (16 * ph.body // RAW) + landed[t])
        wait(nc.scalar, unit_done, turn * ph.body + (t - (RING - 1)))
        nc.scalar.activation(w_hi[t % RING][:, 0:n], raw[t % RAW][:, 0:n], ACT.Copy).then_inc(hi_done, 1)

    def split_lo(ph, i, k):
        if (u := split_unit(ph, i, k)) is None:
            return
        turn, t, n = u
        nc.vector.wait_ge(hi_done, turn * ph.body + (t + 1))
        nc.vector.tensor_tensor(w_lo[t % RING][:, 0:n], raw[t % RAW][:, 0:n], w_hi[t % RING][:, 0:n].bitcast(F32),
                                ALU.subtract).then_inc(lo_done, 1)

    prologue = Phase({"units": -AHEAD, "loads": [0] * RAW, "used": [0] * 4, "phases": []}, AHEAD, AHEAD)

    norm_at, norm_n = {}, [0, 0, 0]
    for name, nk, nsq in (("mix0", KT, 0), ("cq", 3, 3), ("ckv", 2, 2), ("ffn0", KT, KT), ("mix1", KT, KT),
                          ("ffn1", KT, KT), ("final", KT, KT), ("mix2", KT, KT), ("ffn2", KT, KT), ("final2", KT, KT)):
        norm_at[name] = tuple(norm_n)
        norm_n[0] += 1
        norm_n[1] += nk
        norm_n[2] += nsq

    def square(src, kt, n):
        nc.scalar.activation(work[:, kt, 0:n], src, ACT.Square).then_inc(sem("sq_done"), 1)

    def norm_finish_act(name, nk, cols, dim, split=None):
        one, at, _ = norm_at[name]
        n = cols.stop - cols.start
        nc.scalar.wait_ge(sem("ss_done"), one + 1)
        nc.scalar.activation(log_ms[:, 0:n], ps[:, 7, 0:n], ACT.Ln, scale=1.0 / dim,
                             bias=eps[:]).then_inc(sem("ln_done"), 1)
        nc.scalar.wait_ge(sem("ln_done"), one + 1)
        nc.scalar.activation(rstd[:, 0:n], log_ms[:, 0:n], ACT.Exp, scale=-0.5)\
            .then_inc(sem("rstd_done"), 1)
        if split is not None:
            norm_round_act(at, nk, n, split[0])

    def norm_round_act(at, nk, n, hi):
        for kt in range(nk):
            nc.scalar.wait_ge(sem("un_done"), at + kt + 1)
            nc.scalar.activation(hi(kt), work[:, kt, 0:n], ACT.Copy).then_inc(sem("xh_done"), 1)

    def norm_pe(name, nk, n):
        at = norm_at[name][2]
        for kt in range(nk):
            nc.tensor.wait_ge(sem("sq_done"), at + kt + 1)
            mm = nc.tensor.matmul(ps[:, 7, 0:n], ones, work[:, kt, 0:n], start=kt == 0,
                                  stop=kt == nk - 1)
        mm.then_inc(sem("ss_done"), 1)

    folds = [n for n in norm_at if n in ("ffn0", "mix1", "ffn1", "final", "ffn2", "final2")]

    def fold_squares(name, n):
        for j in (1, 2):
            nc.gpsimd.wait_ge(sem("sq_done"), norm_at[name][2] + 2 * j + 2)
            wait(nc.gpsimd, sem("sq_folded"), 2 * folds.index(name) + j - 1)
            first = paired(work)[:, 0, :, 0:n]
            nc.gpsimd.tensor_tensor(first, first, paired(work)[:, j, :, 0:n], ALU.add).then_inc(sem("sq_folded"), 1)

    def square_sums(name, n):
        nc.tensor.wait_ge(sem("sq_folded"), 2 * folds.index(name) + 2)
        for j in (0, 3):
            for t in range(2):
                if j:
                    nc.tensor.wait_ge(sem("sq_done"), norm_at[name][2] + KT - 1 + t)
                mm = nc.tensor.matmul(ps[:, 7, 0:n], ones, paired(work)[:, j, t, 0:n], start=j + t == 0,
                                      stop=j > 0 and t == 1)
        mm.then_inc(sem("ss_done"), 1)

    xh_total, xl_total = [0], [0]
    split_at = {}
    for name, nk in (("mix0", KT), ("cq", 3), ("ckv", 2), ("o0", KT), ("ffn0", KT), ("mix1", KT),
                     ("o1", KT), ("ffn1", KT), ("mix2", KT), ("o2", KT), ("ln", KT),
                     ("merge", KT), ("ffn2", KT)):
        split_at[name] = xl_total[0]
        xl_total[0] += nk

    def norm_dve(name, src, gain, nk, n, split=None, into=None, roots=None):
        one = norm_at[name][0]
        g0 = GAINS[gain[0]][0] + gain[1]

        def lo(kt):
            nc.vector.wait_ge(sem("xh_done"), split_at[name] + kt + 1)
            nc.vector.tensor_tensor(split[1](kt), work[:, kt, 0:n], split[0](kt).bitcast(F32),
                                    ALU.subtract).then_inc(sem("xl_done"), 1)

        nc.vector.wait_ge(sem("rstd_done"), one + 1)
        for kt in range(nk):
            dst = work[:, kt, 0:n] if into is None else into(kt)
            nc.vector.scalar_tensor_tensor(out=dst, in0=src(kt), scalar=gains[:, g0 + kt:g0 + kt + 1],
                                           in1=rstd[:, 0:n] if roots is None else roots, op0=ALU.mult,
                                           op1=ALU.mult)\
                .then_inc(sem("un_done"), 1)
            if split is not None and kt >= 1:
                lo(kt - 1)
        if split is not None:
            lo(nk - 1)

    def u_h(n):
        return lambda kt: u_hi[:, kt, 0:n]

    def u_l(n):
        return lambda kt: u_lo[:, kt, 0:n]

    C1, C2, CF = slice(META, T2), slice(0, T2), slice(META - 2, T2)
    NF = CF.stop - CF.start

    def h_at(cols):
        return lambda kt: h[:, kt, cols]

    def product(out_ap, pairs, start=True, stop=True):
        for n, (a_h, a_l, b_h, b_l) in enumerate(pairs):
            nc.tensor.matmul(out_ap, a_h, b_h, start=start and n == 0, stop=False)
            nc.tensor.matmul(out_ap, a_h, b_l, start=False, stop=False)
            mm = nc.tensor.matmul(out_ap, a_l, b_h, start=False, stop=stop and n == len(pairs) - 1)
        return mm

    def feature_tile(out_ap, s, nk, n, col, xh, xl, x0=0, start=True, stop=True):
        hi, lo = pw(w_hi[s], nk, n), pw(w_lo[s], nk, n)
        return product(out_ap, [(hi[:, kt, col:col + P], lo[:, kt, col:col + P], xh(x0 + kt), xl(x0 + kt))
                                for kt in range(nk)], start, stop)

    def token_tile(out_ap, s, nk, n, cols, xh, xl, x0=0):
        hi, lo = pw(w_hi[s], nk, n), pw(w_lo[s], nk, n)
        return product(out_ap, [(xh(x0 + kt), xl(x0 + kt), hi[:, kt, cols], lo[:, kt, cols])
                                for kt in range(nk)])

    def begin_unit(ph, i, k):
        s = (ph.u0 + k) % RING
        nc.tensor.wait_ge(lo_done, ph.unit(i, k) + 1)
        if k % ph.group == 0:
            wait(nc.tensor, pair_read[ph.pair(k)], ph.used_before(i, k))
        return s, ph.pair(k)

    def by_tokens(ph, i, k):
        s, p = begin_unit(ph, i, k)
        for b in range(2):
            mm = token_tile(ps[:, 2 * p + b, 0:UC], s, KT, UC, slice(0, UC),
                            lambda kt: u_hi[:, kt, b * P:(b + 1) * P], lambda kt: u_lo[:, kt, b * P:(b + 1) * P])
        mm.then_inc(unit_done, 1)

    def two_tiles(ph, i, k, n, xh, xl, ready=None):
        s, p = begin_unit(ph, i, k)
        outs = [ps[:, 2 * p + t, 0:n] for t in range(2)]
        if ready is None:
            for t in range(2):
                mm = feature_tile(outs[t], s, KT, UC, t * P, xh, xl)
        else:
            hi, lo = pw(w_hi[s], KT, UC), pw(w_lo[s], KT, UC)
            for kt in range(KT):
                nc.tensor.wait_ge(sem("xl_done"), split_at[ready] + kt + 1)
                for t in range(2):
                    cols = slice(t * P, (t + 1) * P)
                    mm = product(outs[t], [(hi[:, kt, cols], lo[:, kt, cols], xh(kt), xl(kt))],
                                 kt == 0, kt == KT - 1)
        mm.then_inc(unit_done, 1)

    def down_unit(name, ph, i, k):
        s, p = begin_unit(ph, i, k)
        k0, nk = DOWN_KT[k % 4]
        if k < 4:
            nc.tensor.wait_ge(sem("ffn_lo"), 2 + FFN[name] + (k0 + nk + 1) // 2)
        for t in range(2):
            mm = feature_tile(ps[:, 2 * p + t, 0:T1], s, nk, UC, t * P, lambda kt: a_hi[:, kt, :],
                              lambda kt: a_lo[:, kt, :], x0=k0, start=k % 4 == 0, stop=k % 4 == 3)
        mm.then_inc(unit_done, 1)

    def pair_ap(p, n):
        return ps[:, 2 * p:2 * p + 2, 0:n]

    ATT = {"mla": 0, "stick": MLA_H, "chunk": MLA_H + SB_H, "dsa": MLA_H + SB_H + C_H}

    class Attention:
        def __init__(self, name, heads, blocks, dv, banks, bufs, o, lag=1, pe_lag=None, out_lag=None, act_out=False):
            self.soft = {"mla": 0, "chunk": MLA_H, "dsa": MLA_H + C_H}.get(name)
            self.base, self.turns, self.blocks, self.dv, self.lag = ATT[name], heads // 4, blocks, dv, lag
            self.heads = heads
            self.s_banks, self.pt_banks, self.o_banks = banks
            self.p, self.pt, self.stat = bufs
            self.o, self.act_out = o, act_out
            self.pe_lag = pe_lag or lag
            self.out_lag = out_lag or lag + 1
            self.cols, at = [], 0
            for _, _, keys in blocks:
                self.cols.append(at)
                at += sum(n for _, n in keys)
            self.width = at
            self.tcols, small, large = [], 0, 0
            few = any(n < P for _, _, keys in blocks for _, n in keys)
            for _, nq, keys in blocks:
                row = []
                for _, n in keys:
                    if n < P:
                        row.append((0, small))
                        small += nq
                    else:
                        row.append((1 if few else 0, large))
                        large += nq
                self.tcols.append(row)
            self.parts = ([(META, 0, small)] if few else []) + [(P, 1 if few else 0, large)]

        def steps(self, eng):
            looped = self.turns > 2
            for i in range(1 if looped else self.turns):
                for e in range(4):
                    yield i, e
            if looped:
                with eng.Fori(1, self.turns) as i:
                    for e in range(4):
                        yield i, e

        def head(self, i, e, back=0):
            n = i * 4 + (e - back)
            return None if isinstance(n, int) and n < 0 else n

        def S(self, e, b):
            _, nq, keys = self.blocks[b]
            return ps[0:nq, self.s_banks[e % len(self.s_banks)],
                      self.cols[b]:self.cols[b] + sum(n for _, n in keys)]

        def P(self, e, b, key=None):
            _, nq, keys = self.blocks[b]
            at = self.cols[b] + (0 if key is None else sum(n for _, n in keys[:key]))
            n = sum(n for _, n in keys) if key is None else keys[key][1]
            return self.p[0:nq, e % 2, at:at + n]

        def pt_ps(self, e, b, key):
            _, nq, keys = self.blocks[b]
            bank, at = self.tcols[b][key]
            return ps[0:keys[key][1], self.pt_banks[e % len(self.pt_banks)][bank], at:at + nq]

        def PT(self, e, b, key):
            _, nq, keys = self.blocks[b]
            bank, at = self.tcols[b][key]
            return self.pt[0:keys[key][1], e % 2, 512 * bank + at:512 * bank + at + nq]

        def O(self, e, b):
            return ps[0:self.blocks[b][1], self.o_banks[e % 2], b * self.dv:(b + 1) * self.dv]

        def transposes(self, n, e):
            nc.tensor.wait_ge(sem("at_p"), n + (self.base + 1))
            wait(nc.tensor, sem("at_ptc"), n + (self.base + 1 - len(self.pt_banks)))
            for b, (_, nq, keys) in enumerate(self.blocks):
                for key in range(len(keys)):
                    mm = nc.tensor.transpose(self.pt_ps(e, b, key), self.P(e, b, key), ident[0:nq, 0:nq])
            mm.then_inc(sem("at_pt"), 1)

        def values(self, n, e, v):
            nc.tensor.wait_ge(sem("at_ptc"), n + (self.base + 1))
            wait(nc.tensor, sem("at_oev"), n + (self.base - 1))
            for b, (_, nq, keys) in enumerate(self.blocks):
                for key in range(len(keys)):
                    mm = nc.tensor.matmul(self.O(e, b), self.PT(e, b, key), v(n, e, b, key),
                                          start=key == 0, stop=key == len(keys) - 1)
            mm.then_inc(sem("at_o"), 1)

        def pe(self, scores, v, between=None):
            for i, e in self.steps(nc.tensor):
                n = self.head(i, e)
                wait(nc.tensor, sem("at_p"), n + (self.base + 1 - len(self.s_banks)))
                scores(self, i, e, n).then_inc(sem("at_scores"), 1)
                if (m := self.head(i, e, self.pe_lag)) is not None:
                    self.transposes(m, (e - self.pe_lag) % 4)
                if (m := self.head(i, e, self.pe_lag + 1)) is not None:
                    self.values(m, (e - self.pe_lag - 1) % 4, v)
                if between is not None:
                    between(n)
            for m in range(self.heads - self.pe_lag, self.heads):
                self.transposes(m, m % 4)
                self.values(m - 1, (m - 1) % 4, v)
            self.values(self.heads - 1, (self.heads - 1) % 4, v)

        def exps(self, n, e, scale, src):
            nc.scalar.wait_ge(sem("at_neg"), n + (self.soft + 1))
            wait(nc.scalar, sem("at_pt"), n + (self.base - 1))
            if self.act_out:
                wait(nc.scalar, sem("at_rsum"), n + (self.soft - 3))
            else:
                wait(nc.scalar, sem("at_oev"), n + (self.base - 3))
            for b, (_, nq, _) in enumerate(self.blocks):
                st = self.stat[0:nq, e]
                a = nc.scalar.activation(self.P(e, b), src(e, b), ACT.Exp, scale=scale,
                                         bias=st[:, 1, b:b + 1], accum_out=st[:, 2, b:b + 1])
            a.then_inc(sem("at_p"), 1)

        def copies(self, n, e):
            nc.scalar.wait_ge(sem("at_pt"), n + (self.base + 1))
            wait(nc.scalar, sem("at_o"), n + (self.base - 1))
            for rows, bank, width in self.parts:
                a = nc.scalar.activation(self.pt[0:rows, e % 2, 512 * bank:512 * bank + width],
                                         ps[0:rows, self.pt_banks[e % len(self.pt_banks)][bank], 0:width], ACT.Copy)
            a.then_inc(sem("at_ptc"), 1)

        def outputs(self, n, e):
            nc.scalar.wait_ge(sem("at_o"), n + (self.base + 1))
            nc.scalar.wait_ge(sem("at_rsum"), n + (self.soft + 1))
            for b, (_, nq, _) in enumerate(self.blocks):
                a = nc.scalar.activation(self.o(n, b), self.O(e, b), ACT.Copy, scale=self.stat[0:nq, e, 3, b:b + 1])
            a.then_inc(sem("at_oev"), 1)

        def act(self, scale, src, between=None):
            for i, e in self.steps(nc.scalar):
                n = self.head(i, e)
                if (m := self.head(i, e, self.lag)) is not None and self.lag > 1:
                    self.copies(m, (e - self.lag) % 4)
                self.exps(n, e, scale, src)
                if m is not None and self.lag == 1:
                    self.copies(m, (e - self.lag) % 4)
                if self.act_out and (m := self.head(i, e, self.out_lag)) is not None:
                    self.outputs(m, (e - self.out_lag) % 4)
                if between is not None:
                    between(n)
            for m in range(self.heads - self.lag, self.heads):
                self.copies(m, m % 4)
                if self.act_out:
                    self.outputs(m + self.lag - self.out_lag, (m + self.lag - self.out_lag) % 4)
            if self.act_out:
                for m in range(self.heads + self.lag - self.out_lag, self.heads):
                    self.outputs(m, m % 4)

        def maxima(self, n, e, scale, src):
            wait(nc.vector, sem("at_p"), n + (self.base - 3))
            for b, (_, nq, _) in enumerate(self.blocks):
                a = nc.vector.reduce_max(self.stat[0:nq, e, 0, b:b + 1], src(e, b), AX)
            a.then_inc(sem("at_max"), 1)
            nc.vector.wait_ge(sem("at_max"), n + (self.soft + 1))
            nb = len(self.blocks)
            nc.vector.tensor_scalar(self.stat[:, e, 1, 0:nb], self.stat[:, e, 0, 0:nb], -scale,
                                    None, ALU.mult).then_inc(sem("at_neg"), 1)

        def normalise(self, n, e):
            nc.vector.wait_ge(sem("at_p"), n + (self.base + 1))
            nb = len(self.blocks)
            if self.act_out:
                wait(nc.vector, sem("at_oev"), n + (self.base - 3))
            nc.vector.reciprocal(self.stat[:, e, 3, 0:nb], self.stat[:, e, 2, 0:nb])\
                .then_inc(sem("at_rsum"), 1)
            if self.act_out:
                return
            nc.vector.wait_ge(sem("at_o"), n + (self.base + 1))
            nc.vector.wait_ge(sem("at_rsum"), n + (self.soft + 1))
            for b, (_, nq, _) in enumerate(self.blocks):
                a = nc.vector.tensor_scalar(self.o(n, b), self.O(e, b), self.stat[0:nq, e, 3, b:b + 1],
                                            None, ALU.mult)
            a.then_inc(sem("at_oev"), 1)

        def dve(self, scale, src, before=None, between=None):
            for i, e in self.steps(nc.vector):
                n = self.head(i, e)
                nc.vector.wait_ge(sem("at_scores"), n + (self.base + 1))
                if before is not None:
                    before(self, n, e)
                self.maxima(n, e, scale, src)
                if (m := self.head(i, e, self.out_lag)) is not None:
                    self.normalise(m, (e - self.out_lag) % 4)
                if between is not None:
                    between(n)
            for m in range(self.heads - self.out_lag, self.heads):
                self.normalise(m, m % 4)

    def by_head(t, n, d):
        return t.rearrange("p b (n d) -> p b n d", d=d)

    o1v, o3v = by_head(o1, 0, VD), by_head(o3, 0, HD)
    wide = ([0, 1, 2, 3], [[4], [5]], [6, 7])
    mla = Attention("mla", MLA_H, BLOCKS1, VD, wide, (p1, pt1, stat1),
                    lambda n, b: o1v[:, b, n, :], lag=2)
    stk = Attention("stick", SB_H, BLOCKS1, HD, wide, (p1, pt1, stat1),
                    lambda n, b: o1v[:, b, n + MLA_H, :], lag=2, pe_lag=2)
    chk = Attention("chunk", C_H, BLOCKS1, HD, wide, (p3, pt3, stat3),
                    lambda n, b: o3v[:, b, n, :], lag=2, pe_lag=2, out_lag=3, act_out=True)

    def o_dsa(n, b):
        return o_meta[:, n * DH:(n + 1) * DH] if b == 0 else q_d[:, n, (b - 1) * P:b * P]

    dsa = Attention("dsa", 8, BLOCKS2, DH, ([4, 5], [[2, 3]], [6, 7]), (p4, pt4, stat4), o_dsa, act_out=True)

    def pad_heads(att, q, q_dst, extra=None):
        for i, e in att.steps(nc.gpsimd):
            n = att.head(i, e)
            wait(nc.gpsimd, sem("at_scores"), n + (att.base - 3))
            wait(nc.gpsimd, sem("pad_done"), n + att.base)
            rows = slice(64 * (e % 2), 64 * (e % 2) + 64)
            a = nc.gpsimd.tensor_copy(q_dst[rows, e, :], q[rows, i * 2 + e // 2, :])
            if extra is not None:
                a.then_inc(sem("pad_part"), 1)
                nc.gpsimd.wait_ge(sem("pad_part"), n + 1)
                a = extra(i, e)
            a.then_inc(sem("pad_done"), 1)

    def masked_scores(att, e, b, terms, mask):
        out_ap = att.S(e, b)
        for t, (lhs, rhs) in enumerate(terms):
            nc.tensor.matmul(out_ap, lhs, rhs, start=t == 0, stop=False)
        _, nq, keys = att.blocks[b]
        own = sum(n for _, n in keys[:-1])
        return nc.tensor.matmul(out_ap[:, own:own + nq], ident_b[0:nq, 0:nq], mask[0:nq, 0:nq],
                                start=False, stop=True)

    def mla_scores(att, i, e, n):
        nc.tensor.wait_ge(sem("pad_done"), n + (att.base + 1))
        for b, (q0, nq, keys) in enumerate(att.blocks):
            end = keys[-1][0] + keys[-1][1]
            mm = masked_scores(att, e, b, [
                (q_pad[:, e, q0:q0 + nq], k_nope[:, i * 2 + e // 2, 0:end]),
                (q_pad_r[:, e, q0:q0 + nq], k_rope[:, 0:end])], chunk_b)
        return mm

    def pair_scores(q, kk, mask):
        def scores(att, i, e, n):
            nc.tensor.wait_ge(sem("pad_done"), n + (att.base + 1))
            for b, (q0, nq, keys) in enumerate(att.blocks):
                end = keys[-1][0] + keys[-1][1]
                mm = masked_scores(att, e, b, [(q[:, e, q0:q0 + nq], kk[:, i * 2 + e // 2, 0:end])], mask)
            return mm
        return scores

    def head_values(v, d):
        vv = v.rearrange("p b (n d) -> p b n d", d=d)
        return lambda n, e, b, key: vv[:, key, n, :]

    def rope_pe(rot, tiles, n, first, banks):
        for t, x_ap in enumerate(tiles):
            wait(nc.tensor, sem("rope_done"), first + t + 1 - len(banks))
            nc.tensor.matmul(ps[:, banks[(first + t) % len(banks)], 0:n], rot, x_ap, start=True, stop=True)\
                .then_inc(sem("rot_done"), 1)

    def rope_dve(tiles, cos, sin, n, first, tmp, banks):
        def add(t):
            nc.vector.wait_ge(sem("rope_sin"), first + t + 1)
            nc.vector.tensor_tensor(tiles[t], rot(t), tmp[:, (first + t) % 2, 0:n], ALU.add).then_inc(sem("rope_done"), 1)

        def rot(t):
            return ps[:, banks[(first + t) % len(banks)], 0:n]

        for t, x_ap in enumerate(tiles):
            nc.vector.wait_ge(sem("rot_done"), first + t + 1)
            wait(nc.vector, sem("rope_done"), first + t - 1)
            nc.vector.tensor_tensor(tmp[:, (first + t) % 2, 0:n], x_ap, cos, ALU.mult)
            nc.vector.tensor_tensor(rot(t), rot(t), sin, ALU.mult).then_inc(sem("rope_sin"), 1)
            if t:
                add(t - 1)
        add(len(tiles) - 1)

    q_tiles = [q_d[:, t, :] for t in range(8)] + [k_d[:, t, :] for t in range(KVH)]
    idx_tiles = [qi[:, t, :] for t in range(4)] + [ki[:]]
    rope_tiles = [k_rope[:], q_rope[:, 0, :], q_rope[:, 1, :]]
    Q_ROPES = [(0, 4), (4, 8), (8, 10)]

    def turn_groups(n):
        if 2 * n <= 512:
            return [(range(2 * g, 2 * g + 2), ps[:, 4 + g, 0:2 * n]) for g in range(KT // 2)]
        return [(range(j, j + 1), ps[:, j, 0:n]) for j in range(KT)]

    def tiles_ap(t, js, n):
        return t[:, js[0]:js[-1] + 1, 0:n]

    def turn_pe(o, blocks, n):
        for js, bank in turn_groups(n):
            for at, j in enumerate(js):
                for b, (q0, nq, _) in enumerate(blocks):
                    mm = nc.tensor.transpose(bank[:, at * n + q0:at * n + q0 + nq], o(b, j),
                                             ident[0:nq, 0:nq])
            mm.then_inc(sem("turned"), len(js))

    def turn_act(first, n, skip=0):
        for js, bank in turn_groups(n):
            nc.scalar.wait_ge(sem("turned"), first + js[-1] + 1)
            nc.scalar.activation(tiles_ap(u_hi, js, n - skip), bank.rearrange("p (t n) -> p t n", n=n)[:, :, skip:],
                                 ACT.Copy).then_inc(sem("xh_done"), len(js))

    def turn_dve(name, n, skip=0):
        for js, bank in turn_groups(n):
            nc.vector.wait_ge(sem("xh_done"), split_at[name] + js[-1] + 1)
            nc.vector.tensor_tensor(tiles_ap(u_lo, js, n - skip), bank.rearrange("p (t n) -> p t n", n=n)[:, :, skip:],
                                    tiles_ap(u_hi, js, n - skip).bitcast(F32), ALU.subtract)\
                .then_inc(sem("xl_done"), len(js))

    def operands_ready(name, nk=KT):
        nc.tensor.wait_ge(sem("xl_done"), split_at[name] + nk)

    def residual_dve(ph, cols, group=1):
        n = cols.stop - cols.start
        for i, k in ph.steps(nc.vector):
            split_lo(ph, i, k)
            if k % group == group - 1:
                p = ph.pair(k)
                j = i * ph.groups + k // group
                nc.vector.wait_ge(unit_done, ph.unit(i, k) + 1)
                for t in range(2):
                    hv = paired(h)[:, j, t, cols]
                    nc.vector.tensor_tensor(hv, hv, ps[:, 2 * p + t, 0:n], ALU.add)\
                        .then_inc(pair_read[p] if t else sem("half_added"), 1)

    def splits_act(ph):
        for i, k in ph.steps(nc.scalar):
            split_hi(ph, i, k)

    def residual_act(ph, cols, group=1):
        n = cols.stop - cols.start
        for i, k in ph.steps(nc.scalar):
            split_hi(ph, i, k)
            if k % group == group - 1:
                j = i * ph.groups + k // group
                before = 4 * [ph_out0, ph_down0, ph_out1, ph_down1, ph_merge, ph_down2].index(ph)
                for t in range(2):
                    if t:
                        nc.scalar.wait_ge(pair_read[ph.pair(k)], ph.used_before(i, k) + 1)
                    else:
                        nc.scalar.wait_ge(sem("half_added"), j + (before + 1))
                    nc.scalar.activation(paired(work)[:, j, t, 0:n], paired(h)[:, j, t, cols], ACT.Square)\
                        .then_inc(sem("sq_done"), 1)

    def residual_pe(ph, n, split, norm, norm_n):
        for i, k in ph.steps(nc.tensor):
            two_tiles(ph, i, k, n, u_h(n), u_l(n), split if k == 0 else None)
        square_sums(norm, norm_n)

    FFN = {"ffn0": 0, "ffn1": FT // 2, "ffn2": FT}

    def ffn_act(name, ph):
        nc.scalar.preload_act_table_set("silu_and_others")
        for i, k in ph.steps(nc.scalar):
            split_hi(ph, i, k)
            j, s, p = i * 2 + k // 2, (k // 2) % 2, ph.pair(k)
            if k % 2 == 0:
                nc.scalar.wait_ge(unit_done, ph.unit(i, k) + 1)
                wait(nc.scalar, pair_read[ph.pair(k + 1)], ph.used_before(i, k + 1))
                nc.scalar.activation(act_g[:, s], pair_ap(p, T1), ACT.Silu).then_inc(pair_read[p], 1)
            else:
                nc.scalar.wait_ge(pair_read[p], ph.used_before(i, k) + 1)
                nc.scalar.activation(paired(a_hi)[:, j], act_a[:, s], ACT.Copy).then_inc(sem("ffn_hi"), 1)

    def ffn_lo(name, j, s):
        nc.vector.wait_ge(sem("ffn_hi"), j + (FFN[name] + 1))
        nc.vector.tensor_tensor(paired(a_lo)[:, j], act_a[:, s], paired(a_hi)[:, j].bitcast(F32), ALU.subtract)\
            .then_inc(sem("ffn_lo"), 1)

    def ffn_dve(name, ph):
        for i, k in ph.steps(nc.vector):
            split_lo(ph, i, k)
            if k % 2 == 0:
                continue
            j, s, p = i * 2 + k // 2, (k // 2) % 2, ph.pair(k)
            nc.vector.wait_ge(unit_done, ph.unit(i, k) + 1)
            gate = ph.pair(k - 1)
            nc.vector.wait_ge(pair_read[gate], ph.used_before(i, k - 1) + 1)
            nc.vector.wait_ge(sem("ffn_lo"), j + (FFN[name] + 1))
            nc.vector.tensor_tensor(act_a[:, s], pair_ap(p, T1), act_g[:, s], ALU.mult)\
                .then_inc(pair_read[p], 1)
            ffn_lo(name, j, s)

    def ffn_pe(ph, n, name):
        for i, k in ph.steps(nc.tensor):
            two_tiles(ph, i, k, n, u_h(n), u_l(n), name if k == 0 else None)

    def down_pe(name, ph, norm):
        wait(nc.tensor, pair_read[3], ph.used_after[3])
        for i, k in ph.steps(nc.tensor):
            down_unit(name, ph, i, k)
        square_sums(norm, T1)

    def column_units(w, per):
        def unit(i, k):
            if isinstance(i, int):
                return w[:, (i * per + k) * UC:(i * per + k + 1) * UC].rearrange("(k p) n -> p k n", p=P)
            whole = w.shape[1] // (per * UC)
            return w[:, 0:whole * per * UC].rearrange("(k p) (i m n) -> p k i m n", p=P, m=per, n=UC)[:, :, i, k, :]
        return unit

    def down_units(w):
        v = w.rearrange("(k p) (i g n) -> p k i g n", p=P, g=2, n=UC)
        return lambda i, g, r: v[:, DOWN_KT[r][0]:DOWN_KT[r][0] + DOWN_KT[r][1], i, g, :]

    def begin_load(ph, i, k):
        wait(nc.sync, lo_done, ph.unit(i, k) - (RAW - 1))
        nc.sync.sem_inc(sem("slot_taken"), 1)
        s = (ph.u0 + k) % RAW
        return raw[s], raw_landed[s]

    def load(ph, i, k, src, nk=KT, n=UC):
        slot, landed_sem = begin_load(ph, i, k)
        nc.sync.dma_start(pw(slot, nk, n), src).then_inc(landed_sem, 16)

    def load_columns(ph, w):
        src = column_units(w, ph.body)
        for i, k in ph.steps(nc.sync):
            load(ph, i, k, src(i, k))

    def load_turns(ph, first, second):
        a, b = column_units(first, ph.body // 2), column_units(second, ph.body // 2)
        for i, k in ph.steps(nc.sync):
            load(ph, i, k, (a if k % 2 == 0 else b)(i, k // 2))

    def load_down(ph, w):
        src = down_units(w)
        for i, k in ph.steps(nc.sync):
            load(ph, i, k, src(i, k // 4, k % 4), nk=DOWN_KT[k % 4][1])

    block = ctx.enter_context(nc.Block())

    @block.sync
    def _(sp):
        def load_rows():
            rows = sem("rows_landed")
            for name, src in (("mix", g_mix), ("ffn", g_ffn), ("final", g_final.unsqueeze(0)), ("cq", ev_g_cq),
                              ("ckv", ev_g_ckv), ("mix2", mix_norm_g_2), ("ln_g", conv_ln_g_2),
                              ("ln_b", conv_ln_b_2), ("dw_b", conv_dw_b_2), ("ffn2", ffn_norm_g_2),
                              ("final2", final_norm_g_2.unsqueeze(0))):
                at, n = GAINS[name]
                nc.sync.dma_start(gain_rows[at:at + n, :], src.rearrange("a (r p) -> (a r) p", p=P)).then_inc(rows, 16)
            taps = ffn_dw_w_2[0]
            nc.sync.dma_start(dw_rows[:, 0, :], taps[0:2].rearrange("w (t p) -> (w t) p", p=P)).then_inc(rows, 16)
            nc.sync.dma_start(dw_rows[0:2 * FT, 1, :], taps[2].rearrange("(t p) -> t p", p=P)).then_inc(rows, 16)
            nc.sync.dma_start(dw_rows[2 * FT:, 1, :], ffn_dw_b_2[0].rearrange("(t p) -> t p", p=P)).then_inc(rows, 16)
            nc.sync.dma_start(conv_rows[:], conv_dw_w_2[0]).then_inc(rows, 16)

        early = where["rot32"][0]
        nc.sync.dma_start(x_rows[:], x[0].rearrange("(b p) d -> p b d", p=P)).then_inc(sem("x_landed"), 16)
        nc.sync.dma_start(const[:, 0:early], constants[:, 0:early]).then_inc(sem("x_landed"), 16)
        nc.sync.dma_start(meta_rows[:], meta_tokens_2).then_inc(sem("x_landed"), 16)
        w = ev_w_in[0]
        rope_col, b_col = QL + KVL, QL + KVL + ROPE_D
        for k in range(9):
            if k < 2:
                load(ph_in, 0, k, column_units(w[:, 0:2 * UC], 9)(0, k))
                if k == 0:
                    load_rows()
            elif k == 2:
                slot, landed_sem = begin_load(ph_in, 0, k)
                v, u = pw(slot, KT, UC), w.rearrange("(k p) n -> p k n", p=P)
                nc.sync.dma_start(v[:, :, 0:P], u[:, :, 2 * UC:rope_col]).then_inc(landed_sem, 16)
                for r in range(4):
                    at = P + r * ROPE_D
                    nc.sync.dma_start(v[:, :, at:at + ROPE_D], u[:, :, rope_col:b_col]).then_inc(landed_sem, 16)
            else:
                load(ph_in, 0, k, column_units(w[:, b_col:], 9)(0, k - 3))
                if k == 4:
                    nc.sync.dma_start(const[:, early:], constants[:, early:]).then_inc(sem("tables_landed"), 16)
        for k in range(2):
            slot, landed_sem = begin_load(ph_lat, 0, k)
            v = pw(slot, 3, 384)
            u = ev_w_uq[0].rearrange("(k p) (g a n) -> p k g a n", p=P, g=2, a=4)
            for kt in range(3):
                nc.sync.dma_start(v[:, kt, 0:256].rearrange("p (a n) -> p a n", a=4),
                                  u[:, kt, k, :, 0:NOPE]).then_inc(landed_sem, 16)
                nc.sync.dma_start(v[:, kt, 256:384].rearrange("p (a n) -> p a n", a=4),
                                  u[:, kt, k, :, NOPE:]).then_inc(landed_sem, 16)
        for k in range(2):
            slot, landed_sem = begin_load(ph_lat, 0, 2 + k)
            v = pw(slot, 2, 512)
            u = ev_w_ukv[0].rearrange("(k p) (a n) -> p k a n", p=P, a=MLA_H)
            for kt in range(2):
                nc.sync.dma_start(v[:, kt, :].rearrange("p (a n) -> p a n", a=MLA_H),
                                  u[:, kt, :, k * NOPE:(k + 1) * NOPE]).then_inc(landed_sem, 16)
        load_columns(ph_out0, ev_w_out[0])
        load_turns(ph_ffn0, w_gate[0], w_up[0])
        load_down(ph_down0, w_down[0])
        load_columns(ph_qk, od_w_qkv[0][:, 0:2 * D])
        load_columns(ph_v, od_w_qkv[0][:, 2 * D:])
        load_columns(ph_out1, od_w_out[0])
        load_turns(ph_ffn1, w_gate[1], w_up[1])
        load_down(ph_down1, w_down[1])
        w = w_in_2[0]
        load_turns(ph_conv, w[:, D:2 * D], w[:, 0:D])
        slot, landed_sem = begin_load(ph_idx, 0, 0)
        v, u, at = pw(slot, KT, 2 * ID + IH), w.rearrange("(k p) n -> p k n", p=P), 2 * D + 8 * UC
        for r in range(2):
            nc.sync.dma_start(v[:, :, r * ID:(r + 1) * ID], u[:, :, at:at + ID]).then_inc(landed_sem, 16)
        nc.sync.dma_start(v[:, :, 2 * ID:], u[:, :, at + ID:at + ID + IH]).then_inc(landed_sem, 16)
        for k in range(2):
            load(ph_idx, 0, 1 + k, u[:, :, at - (2 - k) * UC:at - (1 - k) * UC])
        load_columns(ph_proj, w[:, 2 * D:2 * D + 6 * UC])
        gate_col = at + ID + IH
        load_columns(ph_gate, w[:, gate_col:gate_col + ph_gate.units * UC])
        load_columns(ph_gate_b, w[:, gate_col + ph_gate.units * UC:])
        load_columns(ph_wo, attn_w_o_2[0])
        load_columns(ph_pw, conv_pw_out_2[0])
        load_columns(ph_merge, w_merge_out_2[0])
        load_turns(ph_ffn2, ffn_up_2[0][:, 0:DFF], ffn_up_2[0][:, DFF:])
        load_down(ph_down2, ffn_down_2[0])
        for half in range(2):
            for t in range(2):
                cols = slice(half * 512, (half + 1) * 512)
                sp.wait_ge(sem(f"out_copied{t}"), half + 1)
                nc.sync.dma_start(out[0, t * P:(t + 1) * P, cols], out_rows[:, t, cols]).then_inc(sem("out_stored"), 16)
        sp.wait_ge(sem("out_stored"), 64)

    @block.gpsimd
    def _(pool):
        pool.wait_ge(sem("gains_ready"), 1)
        nc.gpsimd.memset(q_pad[:], 0.0).then_inc(sem("zeroed"), 1)
        pool.wait_ge(sem("zeroed"), 1)
        nc.gpsimd.memset(q_pad_r[:], 0.0).then_inc(sem("zeroed"), 1)
        pool.wait_ge(sem("zeroed"), 2)
        for k in range(2):
            pool.wait_ge(pair_read[ph_lat.pair(k)], ph_lat.used_before(0, k) + 1)

        def rope_part(i, e):
            if isinstance(i, int) and i == e == 0:
                pool.wait_ge(sem("rope_done"), 3)
            rows = slice(32 * e, 32 * e + 32)
            return nc.gpsimd.tensor_copy(q_pad_r[rows, e, :], q_rope[rows, i, :])

        pad_heads(mla, q_nope, q_pad, rope_part)
        pad_heads(stk, q_b, q_pad)
        fold_squares("ffn0", T1)
        fold_squares("mix1", T1)

        pairs_read(pool, ph_down0)
        rel = bass.AP(tensor=od_rel_bias.tensor, offset=od_rel_bias.offset + 1 + P,
                      ap=[[1, P], [513, C_H], [1, 2 * P]])
        nc.gpsimd.dma_start(bias_h[:], rel).then_inc(sem("bias_landed"), 16)
        nc.gpsimd.memset(q_pad_c[:], 0.0).then_inc(sem("zeroed"), 1)
        pool.wait_ge(sem("zeroed"), 3)
        pairs_read(pool, ph_v)
        pad_heads(chk, q_c, q_pad_c)
        fold_squares("ffn1", T1)
        fold_squares("final", T1)

        pairs_read(pool, ph_down1)
        for n, t in enumerate((cin[:, :, 0:CONV_W - 1], stat4[:], q_cur[:])):
            nc.gpsimd.memset(t, 0.0).then_inc(sem("zeroed"), 1)
            pool.wait_ge(sem("zeroed"), 4 + n)
        pool.wait_ge(sem("rope_done"), 8)
        for n in range(IH):
            e = n % 2
            rows = slice(64 * e, 64 * e + 64)
            wait(pool, sem("idx_pad"), n)
            wait(pool, sem("idx_scored"), n - 1)
            nc.gpsimd.tensor_copy(q_cur[rows, e, :], qi[rows, n // 2, :]).then_inc(sem("idx_pad"), 1)
        pool.wait_ge(sem("idx_scored"), IH)
        pool.wait_ge(sem("idx_pad"), IH)
        pool.wait_ge(sem("rope_done"), 18)
        for i, e in dsa.steps(pool):
            n = dsa.head(i, e)
            wait(pool, sem("at_scores"), n + (dsa.base - 1))
            wait(pool, sem("pad_done"), n + dsa.base)
            nc.gpsimd.tensor_copy(q_cur[:, e % 2, :], q_d[:, n, :]).then_inc(sem("pad_done"), 1)
        fold_squares("ffn2", NF)
        fold_squares("final2", T1)

    @block.scalar
    def _(act):
        act.preload_act_table_set("natural_log_exp_and_others")
        act.wait_ge(sem("x_landed"), 48)
        for b in range(2):
            a = nc.scalar.activation(work[:].rearrange("p a b -> p (a b)")[:, b * D:(b + 1) * D], x_rows[:, b, :],
                                     ACT.Square, accum_out=x_stat[:, 0, b:b + 1])
        a.then_inc(sem("x_squared"), 1)
        act.wait_ge(sem("x_squared"), 1)
        act.wait_ge(sem("eps_ready"), 1)
        nc.scalar.activation(x_stat[:, 1, :], x_stat[:, 0, :], ACT.Ln, scale=1.0 / D, bias=eps[:]).then_inc(sem("ln_done"), 1)
        act.wait_ge(sem("ln_done"), 1)
        nc.scalar.activation(x_stat[:, 2, :], x_stat[:, 1, :], ACT.Exp, scale=-0.5).then_inc(sem("rstd_done"), 1)
        split_hi(prologue, 0, 0)
        norm_round_act(0, KT, T1, u_h(T1))
        split_hi(prologue, 0, 1)

        for i, k in ph_in.steps(act):
            split_hi(ph_in, i, k)
            p = ph_in.pair(k)
            act.wait_ge(unit_done, k + 1)
            src = pair_ap(p, T1)
            if k < 2:
                a = nc.scalar.activation(lat[:, 2 * k:2 * k + 2, :], src, ACT.Copy)
            elif k == 2:
                nc.scalar.activation(lat[:, 4, :], ps[:, 2 * p, 0:T1], ACT.Copy)
                a = nc.scalar.activation(k_rope[:], ps[:, 2 * p + 1, 0:T1], ACT.Copy)
            else:
                j = (k - 3) % 2
                if k < 5:
                    a = nc.scalar.activation(q_b[:, 2 * j:2 * j + 2, :], src, ACT.Copy, scale=HD ** -0.5)
                elif k < 7:
                    a = nc.scalar.activation(k_b[:, 2 * j:2 * j + 2, :], src, ACT.Copy)
                else:
                    a = nc.scalar.activation(v_b[:, :, j * UC:(j + 1) * UC], src, ACT.Copy)
            a.then_inc(pair_read[p], 1)
            cols = slice(0, T1)
            if k == 2:
                act.wait_ge(pair_read[0], 1)
                act.wait_ge(pair_read[1], 1)
                act.wait_ge(pair_read[2], 1)
                for kt in range(3):
                    square(lat[:, kt, :], kt, T1)
            elif k == 3:
                norm_finish_act("cq", 3, cols, QL, (lambda kt: lat_hi[:, kt, :],))
                act.wait_ge(sem("xl_done"), split_at["cq"] + 3)
                for kt in range(2):
                    square(lat[:, 3 + kt, :], kt, T1)
            elif k == 4:
                norm_finish_act("ckv", 2, cols, KVL, (lambda kt: lat_hi[:, 3 + kt, :],))
        for i, k in ph_lat.steps(act):
            split_hi(ph_lat, i, k)
            p = ph_lat.pair(k)
            act.wait_ge(unit_done, ph_lat.unit(i, k) + 1)
            if k < 2:
                nc.scalar.activation(q_nope[:, 2 * k:2 * k + 2, :], pair_ap(p, T1), ACT.Copy)
                a = nc.scalar.activation(q_rope[:, k, :], ps[:, 2 * p, T1:2 * T1], ACT.Copy)
            elif k == 2:
                a = nc.scalar.activation(k_nope[:], ps[:, 2 * p:2 * p + 2, :].rearrange("p b (t n) -> p (b t) n", t=2),
                                         ACT.Copy)
            else:
                a = nc.scalar.activation(v_a[:], pair_ap(p, 512), ACT.Copy)
            a.then_inc(pair_read[p], 1)
        mla.act((NOPE + ROPE_D) ** -0.5, mla.S)

        def softplus_log(n, e):
            b0 = n + (stk.base + 1)
            bank = ps[:, stk.s_banks[e], 0:stk.width]
            act.wait_ge(sem("at_scores"), b0)
            wait(act, sem("st_sp"), n - 1)
            nc.scalar.activation(stick[:, e % 2, 0, :], bank, ACT.Abs).then_inc(sem("st_abs"), 1)
            act.wait_ge(sem("st_abs"), n + 1)
            nc.scalar.activation(stick[:, e % 2, 1, :], stick[:, e % 2, 0, :], ACT.Exp, scale=-1.0)\
                .then_inc(sem("st_exp"), 1)
            act.wait_ge(sem("st_exp"), n + 1)
            nc.scalar.activation(stick[:, e % 2, 0, :], stick[:, e % 2, 1, :], ACT.Ln, bias=1.0)\
                .then_inc(sem("st_ln"), 1)

        def stick_weights(n, e):
            act.wait_ge(sem("st_t"), n + 1)
            wait(act, sem("at_pt"), n + (stk.base - 1))
            nc.scalar.activation(p1[:, e % 2, 0:stk.width], stick[:, e % 2, 4, :], ACT.Exp).then_inc(sem("at_p"), 1)

        for i, e in stk.steps(act):
            softplus_log(stk.head(i, e), e)
            if (m := stk.head(i, e, 1)) is not None:
                stick_weights(m, (e - 1) % 4)
            if (m := stk.head(i, e, 2)) is not None:
                stk.copies(m, (e - 2) % 4)
        stick_weights(SB_H - 1, 3)
        stk.copies(SB_H - 2, 2)
        stk.copies(SB_H - 1, 3)
        turn_act(0, T1)

        residual_act(ph_out0, C1)
        norm_finish_act("ffn0", KT, C1, D, (u_h(T1),))
        ffn_act("ffn0", ph_ffn0)
        act.preload_act_table_set("natural_log_exp_and_others")
        residual_act(ph_down0, C1, group=4)
        norm_finish_act("mix1", KT, C1, D, (u_h(T1),))

        for i, k in ph_qk.steps(act):
            split_hi(ph_qk, i, k)
            p = ph_qk.pair(k)
            act.wait_ge(unit_done, ph_qk.unit(i, k) + 1)
            nc.scalar.activation(paired(qk_c)[:, i * 4 + k], pair_ap(p, T1), ACT.Copy).then_inc(pair_read[p], 1)
        for i, k in ph_v.steps(act):
            split_hi(ph_v, i, k)
            p = ph_v.pair(k)
            act.wait_ge(unit_done, ph_v.unit(i, k) + 1)
            nc.scalar.activation(v_c[:, :, k * UC:(k + 1) * UC], pair_ap(p, UC), ACT.Copy).then_inc(pair_read[p], 1)
        chk.act(1.0, lambda e, b: biased_ap(e, b))
        turn_act(KT, T1)
        residual_act(ph_out1, C1)
        norm_finish_act("ffn1", KT, C1, D, (u_h(T1),))
        ffn_act("ffn1", ph_ffn1)
        act.preload_act_table_set("natural_log_exp_and_others")
        residual_act(ph_down1, C1, group=4)
        norm_finish_act("final", KT, C1, D)
        for kt in range(KT):
            act.wait_ge(sem("un_done"), norm_at["final"][1] + kt + 1)
            square(h[:, kt, :], kt, T2)
        norm_finish_act("mix2", KT, C2, D, (u_h(T2),))

        def first_tap(j):
            up = 2 * j + 1
            act.wait_ge(pair_read[ph_conv.pair(up)], ph_conv.used_before(0, up) + 1)
            act.wait_ge(sem("zeroed"), 6)
            act.wait_ge(sem("xl_done"), split_at["mix2"] + KT)
            for tile in (2 * j, 2 * j + 1):
                bias = GAINS["dw_b"][0] + tile
                a = nc.scalar.activation(work[:, tile, 0:NF], cin[:, tile, CF], ACT.Identity, scale=conv_w[:, tile, 0:1],
                                         bias=gains[:, bias:bias + 1])
            a.then_inc(sem("first_tap"), 1)

        for i, k in ph_conv.steps(act):
            split_hi(ph_conv, i, k)
            if k and k % 2 == 0:
                first_tap(k // 2 - 1)
            if k % 2 == 0:
                p = ph_conv.pair(k)
                act.wait_ge(unit_done, ph_conv.unit(i, k) + 1)
                wait(act, pair_read[ph_conv.pair(k + 1)], ph_conv.used_before(i, k + 1))
                nc.scalar.activation(sg4[:, (k // 2) % 2], pair_ap(p, T2), ACT.Sigmoid).then_inc(pair_read[p], 1)
        for i, k in ph_idx.steps(act):
            split_hi(ph_idx, i, k)
            if k == 0:
                first_tap(KT // 2 - 1)
            p = ph_idx.pair(k)
            act.wait_ge(unit_done, ph_idx.unit(i, k) + 1)
            if k == 0:
                nc.scalar.activation(ki[:], ps[:, 2 * p, 0:T2], ACT.Copy)
                a = nc.scalar.activation(wi[:, 1:3, :], ps[:, 2 * p + 1, 0:2 * IH].rearrange("p (b n) -> p b n", b=2),
                                         ACT.Copy, scale=IH ** -0.5)
            else:
                a = nc.scalar.activation(qi[:, 2 * (k - 1):2 * k, :], pair_ap(p, T2), ACT.Copy)
            a.then_inc(pair_read[p], 1)
        for i, k in ph_proj.steps(act):
            split_hi(ph_proj, i, k)
            p = ph_proj.pair(k)
            act.wait_ge(unit_done, ph_proj.unit(i, k) + 1)
            if k < 4:
                a = nc.scalar.activation(q_d[:, 2 * k:2 * k + 2, :], pair_ap(p, T2), ACT.Copy)
            elif k == 4:
                a = nc.scalar.activation(k_d[:], pair_ap(p, T2), ACT.Copy)
            else:
                nc.scalar.activation(v_d[0:META, 0, :], ps[0:META, 2 * p, UC:2 * UC], ACT.Copy)
                a = nc.scalar.activation(v_d[:, 1:3, :], pair_ap(p, UC), ACT.Copy)
            a.then_inc(pair_read[p], 1)
            if k == 2:
                for n in range(IH):
                    act.wait_ge(sem("idx_scored"), n + 1)
                    wait(act, sem("idx_acc"), n - 1)
                    nc.scalar.activation(dots(n % 2), ps[:, 6 + n % 2, 0:416], ACT.Relu, scale=ID ** -0.5)\
                        .then_inc(sem("idx_relu"), 1)
        for i, k in ph_gate.steps(act):
            split_hi(ph_gate, i, k)
            p = ph_gate.pair(k)
            act.wait_ge(unit_done, ph_gate.unit(i, k) + 1)
            nc.scalar.activation(paired(gates)[:, k], pair_ap(p, NF), ACT.Sigmoid).then_inc(pair_read[p], 1)

        act.preload_act_table_set("natural_log_exp_and_others")

        def gate_b(n):
            if n % 2 and n // 2 < ph_gate_b.units:
                split_hi(ph_gate_b, 0, n // 2)
            elif n and n % 2 == 0:
                gate_b_out(n // 2 - 1)

        def gate_b_out(g):
            act.wait_ge(unit_done, ph_gate_b.unit(0, g) + 1)
            nc.scalar.activation(paired(gates)[:, ph_gate.units + g], pair_ap(0, NF), ACT.Copy).then_inc(pair_read[0], 1)

        dsa.act(DH ** -0.5, dsa.S, gate_b)
        turn_act(2 * KT, T2, CF.start)
        act.wait_ge(pair_read[0], ph_gate_b.used_after[0])
        raw_gates = gates[:, 2 * ph_gate.units:, :]
        nc.scalar.activation(raw_gates, raw_gates, ACT.Sigmoid).then_inc(sem("gates_b"), 1)
        act.preload_act_table_set("natural_log_exp_and_others")
        for i, k in ph_wo.steps(act):
            split_hi(ph_wo, i, k)
            if k == 1:
                for kt in range(KT):
                    act.wait_ge(sem("ln_centred"), kt + 1)
                    nc.scalar.activation(cin[:, kt, 0:NF], work[:, kt, 0:NF], ACT.Square).then_inc(sem("ln_sq"), 1)
        act.wait_ge(sem("ln_var"), 1)
        nc.scalar.activation(log_ms[:, 0:NF], ps[:, 6, 0:NF], ACT.Ln, scale=1.0 / D, bias=eps[:]).then_inc(sem("ln_log"), 1)
        act.wait_ge(sem("ln_log"), 1)
        nc.scalar.activation(rstd[:, 0:NF], log_ms[:, 0:NF], ACT.Exp, scale=-0.5).then_inc(sem("ln_rstd"), 1)
        for kt in range(KT):
            act.wait_ge(sem("ln_scaled"), kt + 1)
            g, b = GAINS["ln_g"][0] + kt, GAINS["ln_b"][0] + kt
            nc.scalar.activation(work[:, kt, 0:NF], work[:, kt, 0:NF], ACT.Silu, scale=gains[:, g:g + 1],
                                 bias=gains[:, b:b + 1]).then_inc(sem("ln_silu"), 1)
        act.wait_ge(unit_done, ph_wo.unit(0, 3) + 1)
        for kt in range(KT):
            act.wait_ge(sem("ln_silu"), kt + 1)
            nc.scalar.activation(u_hi[:, kt, 0:NF], work[:, kt, 0:NF], ACT.Copy).then_inc(sem("xh_done"), 1)
        splits_act(ph_pw)
        act.wait_ge(unit_done, ph_pw.unit(0, 3) + 1)
        for j in range(4):
            act.wait_ge(sem("pw_added"), j + 1)
            nc.scalar.activation(paired(u_hi)[:, j, :, 0:NF], paired(work)[:, j, :, 0:NF], ACT.Copy).then_inc(sem("xh_done"), 2)
        residual_act(ph_merge, CF)
        norm_finish_act("ffn2", KT, CF, D, (u_h(NF),))

        act.preload_act_table_set("silu_and_others")

        def f2_hi(j, s):
            act.wait_ge(sem("f2_mul"), j + 3)
            nc.scalar.activation(paired(a_hi)[:, j], act_a[:, s], ACT.Copy).then_inc(sem("ffn_hi"), 1)

        for i, k in ph_ffn2.steps(act):
            split_hi(ph_ffn2, i, k)
            if k == 2:
                f2_hi(i * 2, 0)
            j, s, p = i * 2 + k // 2, (k // 2) % 2, ph_ffn2.pair(k)
            act.wait_ge(unit_done, ph_ffn2.unit(i, k) + 1)
            act.wait_ge(sem("f2_mul"), j + 1)
            for t in range(2):
                tile = j * 2 + (t + (k % 2) * FT)
                dst = (cva if k % 2 == 0 else cvb)[:, s, t, :]
                a = nc.scalar.activation(dst, ps[:, 2 * p + t, 0:T1], ACT.Identity,
                                         scale=ffn_dw[:, 0, bass.ds(tile, 1)], bias=ffn_dw[:, 1, bass.ds(tile + 2 * FT, 1)])
            a.then_inc(sem("f2_tap0"), 1)
            if k % 2:
                first = ph_ffn2.pair(k - 1)
                act.wait_ge(pair_read[first], ph_ffn2.used_before(i, k - 1) + 1)
                nc.scalar.activation(act_g[:, s], cva[:, s], ACT.Silu).then_inc(sem("f2_silu"), 1)
                if k == 3 or isinstance(i, int) and i == ph_ffn2.turns:
                    f2_hi(j, s)
        act.preload_act_table_set("natural_log_exp_and_others")
        residual_act(ph_down2, C1, group=4)
        norm_finish_act("final2", KT, C1, D)
        for half in range(2):
            act.wait_ge(sem("out_turned"), half + 1)
            nc.scalar.activation(out_rows[:, 0, half * 512:(half + 1) * 512], ps[:, half, :], ACT.Copy)\
                .then_inc(sem("out_copied0"), 1)

    @block.tensor
    def _(pe):
        pe.wait_ge(sem("x_landed"), 48)
        for j in range(KT):
            cols = slice(j * P, (j + 1) * P)
            nc.tensor.transpose(ps[:, j, 0:META], meta_rows[:, cols], ident[0:META, 0:META])
            for b in range(2):
                mm = nc.tensor.transpose(ps[:, j, META + b * P:META + (b + 1) * P], x_rows[:, b, cols], ident)
            mm.then_inc(sem("x_turned"), 1)
        pe.wait_ge(sem("rows_landed"), 16 * 15)
        pe.wait_ge(sem("h_copied"), KT)
        nc.tensor.transpose(ps[:, 0, 0:GAIN_ROWS], gain_rows[:], ident[0:GAIN_ROWS, 0:GAIN_ROWS])
        for n in range(2):
            rows = 4 * FT
            nc.tensor.transpose(ps[:, 1 + n, 0:rows], dw_rows[:, n, :], ident[0:rows, 0:rows])
        for j in range(KT):
            mm = nc.tensor.transpose(ps[:, 3, j * CONV_W:(j + 1) * CONV_W], conv_rows[:, j * P:(j + 1) * P],
                                     ident[0:CONV_W, 0:CONV_W])
        mm.then_inc(sem("rows_turned"), 1)
        pe.wait_ge(sem("diag_ready"), 1)
        for b in range(2):
            mm = nc.tensor.matmul(ps[:, 7, b * P:(b + 1) * P], ones, x_diag[:, b, :], start=True, stop=True)
        mm.then_inc(sem("ss_done"), 1)
        pe.wait_ge(sem("gains_ready"), 1)
        uh, ul = u_h(T1), u_l(T1)
        for i, k in ph_in.steps(pe):
            if k < 7:
                two_tiles(ph_in, i, k, T1, uh, ul, "mix0" if k == 0 else None)
            else:
                by_tokens(ph_in, i, k)
            if k == 3:
                norm_pe("cq", 3, T1)
            elif k == 4:
                pe.wait_ge(sem("ln_done"), norm_at["cq"][0] + 1)
                norm_pe("ckv", 2, T1)
        operands_ready("ckv", 2)
        lh, ll = (lambda kt: lat_hi[:, kt, :]), (lambda kt: lat_lo[:, kt, :])
        for i, k in ph_lat.steps(pe):
            s, p = begin_unit(ph_lat, i, k)
            if k < 2:
                for t in range(3):
                    dst = ps[:, 2 * p + t % 2, (t // 2) * T1:(t // 2 + 1) * T1]
                    mm = feature_tile(dst, s, 3, 384, t * P, lh, ll)
            elif k == 2:
                for t in range(4):
                    dst = ps[:, 2 * p + t // 2, (t % 2) * T1:(t % 2 + 1) * T1]
                    mm = feature_tile(dst, s, 2, 512, t * P, lh, ll, x0=3)
            else:
                for b in range(2):
                    mm = token_tile(ps[:, 2 * p + b, :], s, 2, 512, slice(0, 512),
                                    lambda kt: lat_hi[:, kt, b * P:(b + 1) * P],
                                    lambda kt: lat_lo[:, kt, b * P:(b + 1) * P], x0=3)
            mm.then_inc(unit_done, 1)
            if k in (1, 2):
                wait(pe, pair_read[ph_lat.pair(k - 1)], ph_lat.used_before(0, k - 1) + 1)
            if k == 1:
                pe.wait_ge(sem("tables_landed"), 16)
                pairs_read(pe, ph_in)
                rope_pe(c("rot32"), rope_tiles[0:2], T1, 0, [4, 5])
            elif k == 2:
                rope_pe(c("rot32"), rope_tiles[2:], T1, 2, [4, 5])
        pairs_read(pe, ph_lat)
        pe.wait_ge(sem("consts_ready"), 1)
        pe.wait_ge(sem("rope_done"), 3)
        mla.pe(mla_scores, head_values(v_a, VD))
        stk.pe(pair_scores(q_pad, k_b, before_b), head_values(v_b, HD))
        pe.wait_ge(sem("at_oev"), MLA_H + SB_H)
        turn_pe(lambda b, j: o1[:, b, j * P:(j + 1) * P], BLOCKS1, T1)
        residual_pe(ph_out0, T1, "o0", "ffn0", T1)
        ffn_pe(ph_ffn0, T1, "ffn0")
        down_pe("ffn0", ph_down0, "mix1")
        for i, k in ph_qk.steps(pe):
            two_tiles(ph_qk, i, k, T1, uh, ul, "mix1" if k == 0 else None)
        for i, k in ph_v.steps(pe):
            by_tokens(ph_v, i, k)
        pairs_read(pe, ph_v)
        chk.pe(pair_scores(q_pad_c, k_c, chunk_b), head_values(v_c, HD))
        pe.wait_ge(sem("at_oev"), chk.base + C_H)
        turn_pe(lambda b, j: o3[:, b, j * P:(j + 1) * P], BLOCKS1, T1)
        residual_pe(ph_out1, T1, "o1", "ffn1", T1)
        ffn_pe(ph_ffn1, T1, "ffn1")
        down_pe("ffn1", ph_down1, "final")
        pe.wait_ge(sem("rstd_done"), norm_at["final"][0] + 1)
        norm_pe("mix2", KT, T2)
        uh, ul = u_h(T2), u_l(T2)
        for i, k in ph_conv.steps(pe):
            two_tiles(ph_conv, i, k, T2, uh, ul, "mix2" if k == 0 else None)
        for i, k in ph_idx.steps(pe):
            if k:
                two_tiles(ph_idx, i, k, T2, uh, ul)
                continue
            s, p = begin_unit(ph_idx, i, k)
            feature_tile(ps[:, 2 * p, 0:T2], s, KT, 2 * ID + IH, 0, uh, ul)
            for b, x0 in enumerate((META, META + P)):
                mm = token_tile(ps[:, 2 * p + 1, b * IH:(b + 1) * IH], s, KT, 2 * ID + IH, slice(2 * ID, 2 * ID + IH),
                                lambda kt: u_hi[:, kt, x0:x0 + P], lambda kt: u_lo[:, kt, x0:x0 + P])
            mm.then_inc(unit_done, 1)
        for i, k in ph_proj.steps(pe):
            if k < 5:
                two_tiles(ph_proj, i, k, T2, uh, ul)
            else:
                s, p = begin_unit(ph_proj, i, k)
                for x0, dst in ((META, ps[:, 2 * p, 0:UC]), (META + P, ps[:, 2 * p + 1, 0:UC]),
                                (0, ps[:, 2 * p, UC:2 * UC])):
                    mm = token_tile(dst, s, KT, UC, slice(0, UC), lambda kt: u_hi[:, kt, x0:x0 + P],
                                    lambda kt: u_lo[:, kt, x0:x0 + P])
                mm.then_inc(unit_done, 1)
            if k == 0:
                pairs_read(pe, ph_idx)
                pairs_read(pe, ph_conv)
                rope_pe(c("rot64"), idx_tiles, T2, 3, [4, 5, 6, 7])
            if k == 2:
                pe.wait_ge(sem("rope_done"), 8)
                for n in range(IH):
                    e = n % 2
                    pe.wait_ge(sem("idx_pad"), n + 1)
                    wait(pe, sem("idx_relu"), n - 1)
                    nc.tensor.matmul(ps[:, 6 + e, 0:144], q_cur[:, e, META:META + P], ki[:, 0:144], start=True, stop=True)
                    nc.tensor.matmul(ps[:, 6 + e, 144:416], q_cur[:, e, META + P:T2], ki[:], start=True, stop=True)\
                        .then_inc(sem("idx_scored"), 1)
        uh_f, ul_f = (lambda kt: u_hi[:, kt, CF]), (lambda kt: u_lo[:, kt, CF])
        for i, k in ph_gate.steps(pe):
            two_tiles(ph_gate, i, k, NF, uh_f, ul_f)
            if k < len(Q_ROPES):
                pairs_read(pe, ph_proj)
                pe.wait_ge(sem("idx_relu"), IH)
                lo, hi = Q_ROPES[k]
                rope_pe(c("rot128"), q_tiles[lo:hi], T2, 8 + lo, [4, 5, 6, 7])
        pairs_read(pe, ph_gate)
        pe.wait_ge(sem("rope_done"), 18)
        pe.wait_ge(sem("pick_ready"), 1)

        def dsa_scores(att, i, e, n):
            pe.wait_ge(sem("pad_done"), n + (att.base + 1))
            for b, (q0, nq, keys) in enumerate(att.blocks):
                end = keys[-1][0] + keys[-1][1]
                nc.tensor.matmul(att.S(e, b), q_cur[:, e % 2, q0:q0 + nq], k_d[:, i, 0:end], start=True, stop=False)
                mask = seen_b[0:META, 0:META] if b == 0 else pick[:, 0:144] if b == 1 else pick[:, 144:416]
                mm = nc.tensor.matmul(att.S(e, b), ident_b[0:nq, 0:nq], mask, start=False, stop=True)
            return mm

        def dsa_values(n, e, b, key):
            kv = (n // 4) if isinstance(n, int) else n // 4
            return v_d[0:BLOCKS2[b][2][key][1], key, kv * DH:(kv + 1) * DH]

        def gate_b_unit(n):
            if n % 2 and n // 2 < ph_gate_b.units:
                two_tiles(ph_gate_b, 0, n // 2, NF, uh_f, ul_f)

        dsa.pe(dsa_scores, dsa_values, gate_b_unit)
        pe.wait_ge(sem("at_oev"), dsa.base + 8)
        pairs_read(pe, ph_gate_b)
        turn_pe(lambda b, j: o_dsa(j, b), BLOCKS2, T2)
        operands_ready("o2")

        def channel_sums(j):
            pe.wait_ge(sem("conv_tap"), 2 * (CONV_W - 1) * (j + 1))
            for kt in (2 * j, 2 * j + 1):
                mm = nc.tensor.matmul(ps[:, 7, 0:NF], ones, work[:, kt, 0:NF], start=kt == 0, stop=kt == KT - 1)
            if j == KT // 2 - 1:
                mm.then_inc(sem("ln_sum"), 1)

        for i, k in ph_wo.steps(pe):
            two_tiles(ph_wo, i, k, NF, u_h(NF), u_l(NF))
            if k == 0:
                for j in range(KT // 2):
                    channel_sums(j)
            elif k == 2:
                for kt in range(KT):
                    pe.wait_ge(sem("ln_sq"), kt + 1)
                    mm = nc.tensor.matmul(ps[:, 6, 0:NF], ones, cin[:, kt, 0:NF], start=kt == 0, stop=kt == KT - 1)
                mm.then_inc(sem("ln_var"), 1)
        for i, k in ph_pw.steps(pe):
            two_tiles(ph_pw, i, k, NF, u_h(NF), u_l(NF), "ln" if k == 0 else None)
        residual_pe(ph_merge, NF, "merge", "ffn2", NF)
        ffn_pe(ph_ffn2, NF, "ffn2")
        down_pe("ffn2", ph_down2, "final2")
        pairs_read(pe, ph_down2)
        for j in range(KT):
            pe.wait_ge(sem("un_done"), norm_at["final2"][1] + j + 1)
            for t in range(2):
                mm = nc.tensor.transpose(ps[:, 2 * t + j // 4, (j % 4) * P:(j % 4 + 1) * P],
                                         work[:, j, t * P:(t + 1) * P], ident)
            if j % 4 == 3:
                mm.then_inc(sem("out_turned"), 1)

    @block.vector
    def _(dve):
        links = [0]

        def link(ins):
            links[0] += 1
            ins.then_inc(sem("vector_link"), 1)
            dve.wait_ge(sem("vector_link"), links[0])

        dve.sem_inc(sem("ffn_lo"), 2)
        dve.sem_inc(sem("f2_mul"), 2)
        dve.wait_ge(sem("x_landed"), 48)
        nc.vector.memset(eps[:], EPS).then_inc(sem("eps_ready"), 1)
        for j in range(KT):
            dve.wait_ge(sem("x_turned"), j + 1)
            nc.vector.tensor_copy(h[:, j, :], ps[:, j, 0:T2]).then_inc(sem("h_copied"), 1)
        dve.wait_ge(sem("rstd_done"), 1)
        for b in range(2):
            a = nc.vector.tensor_scalar(x_diag[:, b, :], ident, x_stat[:, 2, b:b + 1], None, ALU.mult)
        a.then_inc(sem("diag_ready"), 1)
        split_lo(prologue, 0, 0)
        dve.wait_ge(sem("rows_turned"), 1)
        nc.vector.tensor_copy(gains[:], ps[:, 0, 0:GAIN_ROWS])
        nc.vector.tensor_copy(ffn_dw[:], ps[:, 1:3, 0:4 * FT])
        nc.vector.tensor_copy(conv_w[:], ps[:, 3, 0:KT * CONV_W].rearrange("p (k w) -> p k w", w=CONV_W))\
            .then_inc(sem("gains_ready"), 1)
        dve.wait_ge(sem("gains_ready"), 1)
        dve.wait_ge(sem("h_copied"), KT)
        dve.wait_ge(sem("ss_done"), 1)
        norm_dve("mix0", h_at(C1), ("mix", 0), KT, T1, (u_h(T1), u_l(T1)), roots=ps[:, 7, 0:T1])
        for n, name in enumerate(("ident", "chunk_mask", "before_mask", "seen_mask")):
            a = nc.vector.tensor_copy(masks[:, n, :], c(name))
        a.then_inc(sem("consts_ready"), 1)
        split_lo(prologue, 0, 1)
        for i, k in ph_in.steps(dve):
            split_lo(ph_in, i, k)
            if k == 3:
                norm_dve("cq", lambda kt: lat[:, kt, :], ("cq", 0), 3, T1,
                         (lambda kt: lat_hi[:, kt, :], lambda kt: lat_lo[:, kt, :]))
            elif k == 4:
                norm_dve("ckv", lambda kt: lat[:, 3 + kt, :], ("ckv", 0), 2, T1,
                         (lambda kt: lat_hi[:, 3 + kt, :], lambda kt: lat_lo[:, 3 + kt, :]))
        for i, k in ph_lat.steps(dve):
            split_lo(ph_lat, i, k)
            if k == 1:
                dve.wait_ge(sem("tables_landed"), 16)
                rope_dve(rope_tiles[0:2], c("cos32"), c("sin32"), T1, 0, rope_t, [4, 5])
            elif k == 2:
                rope_dve(rope_tiles[2:], c("cos32"), c("sin32"), T1, 2, rope_t, [4, 5])
        mla.dve((NOPE + ROPE_D) ** -0.5, mla.S)

        def softplus_sums(n, e):
            z = ps[:, stk.s_banks[e], 0:stk.width]
            st = stick[:, e % 2]
            dve.wait_ge(sem("st_ln"), n + 1)
            wait(dve, sem("st_scan"), n - 1)
            nc.vector.scalar_tensor_tensor(out=st[:, 2, :], in0=z, scalar=0.0, in1=st[:, 0, :], op0=ALU.max, op1=ALU.add)\
                .then_inc(sem("st_sp"), 1)
            dve.wait_ge(sem("st_sp"), n + 1)
            wait(dve, sem("st_t"), n - 1)
            for b, (_, _, keys) in enumerate(BLOCKS1):
                lo, hi = stk.cols[b], stk.cols[b] + sum(m for _, m in keys)
                rev = lambda t: t[:, lo:hi][:, ::-1]
                a = nc.vector.tensor_tensor_scan(rev(st[:, 3, :]), wide_ones[:, 0:hi - lo], rev(st[:, 2, :]), 0.0,
                                                 ALU.mult, ALU.add)
            a.then_inc(sem("st_scan"), 1)
            dve.wait_ge(sem("st_scan"), n + 1)
            wait(dve, sem("at_p"), n + (stk.base - 1))
            nc.vector.tensor_tensor(st[:, 4, :], z, st[:, 3, :], ALU.subtract).then_inc(sem("st_t"), 1)

        def stick_out(n, e):
            dve.wait_ge(sem("at_o"), n + (stk.base + 1))
            for b in range(2):
                a = nc.vector.tensor_copy(stk.o(n, b), stk.O(e, b))
            a.then_inc(sem("at_oev"), 1)

        for i, e in stk.steps(dve):
            softplus_sums(stk.head(i, e), e)
            if (m := stk.head(i, e, 3)) is not None:
                stick_out(m, (e - 3) % 4)
        for m in range(SB_H - 3, SB_H):
            stick_out(m, m % 4)
        turn_dve("o0", T1)
        residual_dve(ph_out0, C1)
        norm_dve("ffn0", h_at(C1), ("ffn", 0), KT, T1, (u_h(T1), u_l(T1)))
        ffn_dve("ffn0", ph_ffn0)
        residual_dve(ph_down0, C1, group=4)
        norm_dve("mix1", h_at(C1), ("mix", KT), KT, T1, (u_h(T1), u_l(T1)))
        for i, k in ph_qk.steps(dve):
            split_lo(ph_qk, i, k)
        for i, k in ph_v.steps(dve):
            split_lo(ph_v, i, k)
        dve.wait_ge(sem("bias_landed"), 16)

        def add_bias(att, n, e):
            wait(dve, sem("at_p"), n + (att.base - 1))
            hb = bias_h[:, n, :]
            nc.vector.scalar_tensor_tensor(out=biased_ap(e, 0)[:, ::-1], in0=att.S(e, 0)[:, ::-1], scalar=HD ** -0.5,
                                           in1=hb[:, 0:P], op0=ALU.mult, op1=ALU.add)
            nc.vector.scalar_tensor_tensor(out=biased_ap(e, 1)[:, ::-1], in0=att.S(e, 1)[:, ::-1], scalar=HD ** -0.5,
                                           in1=hb, op0=ALU.mult, op1=ALU.add).then_inc(sem("biased"), 1)
            dve.wait_ge(sem("biased"), n + 1)

        chk.dve(1.0, lambda e, b: biased_ap(e, b), add_bias)
        turn_dve("o1", T1)
        residual_dve(ph_out1, C1)
        norm_dve("ffn1", h_at(C1), ("ffn", KT), KT, T1, (u_h(T1), u_l(T1)))
        ffn_dve("ffn1", ph_ffn1)
        residual_dve(ph_down1, C1, group=4)
        norm_dve("final", h_at(C1), ("final", 0), KT, T1, into=h_at(C1))
        dve.wait_ge(sem("un_done"), norm_at["final"][1] + KT)
        norm_dve("mix2", h_at(C2), ("mix2", 0), KT, T2, (u_h(T2), u_l(T2)))

        conv_steps = [0]

        def conv(steps):
            for _ in range(steps):
                j, w = divmod(conv_steps[0], CONV_W - 1)
                if j == KT // 2:
                    return
                conv_steps[0] += 1
                w += 1
                if w == 1:
                    dve.wait_ge(sem("first_tap"), j + 1)
                for tile in (2 * j, 2 * j + 1):
                    src, tap = cin[:, tile, w + CF.start:w + CF.stop], conv_w[:, tile, w:w + 1]
                    if w > 1:
                        dve.wait_ge(sem("conv_tap"), (j * (CONV_W - 1) + w - 1) * 2 + tile % 2 - 1)
                    nc.vector.scalar_tensor_tensor(out=work[:, tile, 0:NF], in0=src, scalar=tap, in1=work[:, tile, 0:NF],
                                                   op0=ALU.mult, op1=ALU.add).then_inc(sem("conv_tap"), 1)

        for i, k in ph_conv.steps(dve):
            split_lo(ph_conv, i, k)
            if k >= 2:
                conv(5 if k in (4, 6) else 4)
            if k % 2:
                p, gate = ph_conv.pair(k), ph_conv.pair(k - 1)
                dve.wait_ge(unit_done, ph_conv.unit(i, k) + 1)
                dve.wait_ge(pair_read[gate], ph_conv.used_before(i, k - 1) + 1)
                nc.vector.tensor_tensor(paired(cin)[:, k // 2, :, CONV_W - 1:], pair_ap(p, T2), sg4[:, (k // 2) % 2],
                                        ALU.mult).then_inc(pair_read[p], 1)
        for i, k in ph_idx.steps(dve):
            split_lo(ph_idx, i, k)
            conv(4)

        spans = ((1, 0, 144), (2, 144, 416))
        rounds = (TOPK - 1) // 8

        def link_conv(ins, steps):
            links[0] += 1
            ins.then_inc(sem("vector_link"), 1)
            conv(steps)
            dve.wait_ge(sem("vector_link"), links[0])

        def top_round(r):
            src = acc if r == 0 else left
            for b, lo, hi in spans:
                a = nc.vector.max(top8[:, b - 1, :], src[:, lo:hi])
            link_conv(a, r % 2)
            if r < rounds:
                for b, lo, hi in spans:
                    a = nc.vector.match_replace(left[:, lo:hi], top8[:, b - 1, :], src[:, lo:hi], LOWEST)
                link_conv(a, 1)

        for i, k in ph_proj.steps(dve):
            split_lo(ph_proj, i, k)
            if k < 4:
                conv(6 if k == 1 else 4)
            if k == 0:
                rope_dve(idx_tiles, c("cos64"), c("sin64"), T2, 3, rope4, [4, 5, 6, 7])
            if k == 2:
                for n in range(IH):
                    dve.wait_ge(sem("idx_relu"), n + 1)
                    wait(dve, sem("idx_acc"), n)
                    for b, lo, hi in spans:
                        if n == 0:
                            a = nc.vector.tensor_scalar(acc[:, lo:hi], dots(0)[:, lo:hi], wi[:, b, 0:1], None, ALU.mult)
                        else:
                            a = nc.vector.scalar_tensor_tensor(out=acc[:, lo:hi], in0=dots(n % 2)[:, lo:hi],
                                                               scalar=wi[:, b, n:n + 1], in1=acc[:, lo:hi],
                                                               op0=ALU.mult, op1=ALU.add)
                    a.then_inc(sem("idx_acc"), 1)
                dve.wait_ge(sem("idx_acc"), IH)
                for lo, hi in ((META, 144), (288, 416)):
                    nc.vector.tensor_tensor(acc[:, lo:hi], acc[:, lo:hi], c("seen_mask"), ALU.add)
                nc.vector.memset(acc[:, 0:META], BONUS)
                link_conv(nc.vector.memset(acc[:, 144:144 + META], BONUS), 1)
            if k >= 4:
                for r in range(2 * (k - 4), 2 * (k - 4) + 2):
                    top_round(r)
        for i, k in ph_gate.steps(dve):
            split_lo(ph_gate, i, k)
            for r in range(4 + 2 * k, min(6 + 2 * k, rounds + 1)):
                top_round(r)
            if k < len(Q_ROPES):
                lo, hi = Q_ROPES[k]
                rope_dve(q_tiles[lo:hi], c("cos128"), c("sin128"), T2, 8 + lo, rope4, [4, 5, 6, 7])
        last = (TOPK - 1) % 8
        for b, lo, hi in spans:
            thr = top8[:, b - 1, last:last + 1]
            nc.vector.tensor_scalar(above[:, lo:hi], acc[:, lo:hi], thr, None, ALU.is_gt)
            a = nc.vector.tensor_scalar(equal[:, lo:hi], acc[:, lo:hi], thr, None, ALU.is_equal)
        link(a)
        for b, lo, hi in spans:
            nc.vector.reduce_sum(need[:, b - 1:b], above[:, lo:hi], AX)
            a = nc.vector.tensor_tensor_scan(left[:, lo:hi], wide_ones[:, 0:hi - lo], equal[:, lo:hi], 0.0, ALU.mult, ALU.add)
        link(a)
        link(nc.vector.tensor_scalar(need[:], need[:], -1.0, float(TOPK), ALU.mult, ALU.add))
        for b, lo, hi in spans:
            a = nc.vector.scalar_tensor_tensor(out=left[:, lo:hi], in0=left[:, lo:hi], scalar=need[:, b - 1:b],
                                               in1=equal[:, lo:hi], op0=ALU.is_le, op1=ALU.mult)
        link(a)
        link(nc.vector.tensor_tensor(left, left, above, ALU.add))
        link(nc.vector.tensor_scalar(left, left, -NEG, NEG, ALU.mult, ALU.add))
        for lo, hi in ((META, 144), (288, 416)):
            a = nc.vector.tensor_tensor(left[:, lo:hi], left[:, lo:hi], c("seen_mask"), ALU.add)
        link(a)
        nc.vector.tensor_copy(pick[:], left).then_inc(sem("pick_ready"), 1)

        def gate_b(n):
            if n % 2 and n // 2 < ph_gate_b.units:
                conv(6)
                split_lo(ph_gate_b, 0, n // 2)
            else:
                conv(4)

        dsa.dve(DH ** -0.5, dsa.S, between=gate_b)
        turn_dve("o2", T2, CF.start)
        conv(KT // 2 * CONV_W)
        for i, k in ph_wo.steps(dve):
            split_lo(ph_wo, i, k)
            if k == 3:
                dve.wait_ge(sem("ln_rstd"), 1)
                for kt in range(KT):
                    nc.vector.tensor_tensor(work[:, kt, 0:NF], work[:, kt, 0:NF], rstd[:, 0:NF], ALU.mult).then_inc(sem("ln_scaled"), 1)
            p = ph_wo.pair(k)
            dve.wait_ge(unit_done, ph_wo.unit(i, k) + 1)
            dve.wait_ge(sem("gates_b"), 1)
            hv = paired(gates)[:, 4 + k]
            nc.vector.tensor_tensor(hv, pair_ap(p, NF), hv, ALU.mult).then_inc(pair_read[p], 1)
            if k == 0:
                dve.wait_ge(sem("ln_sum"), 1)
                link(nc.vector.tensor_scalar(log_ms[:, 0:NF], ps[:, 7, 0:NF], 1.0 / D, None, ALU.mult))
                for kt in range(KT):
                    nc.vector.tensor_tensor(work[:, kt, 0:NF], work[:, kt, 0:NF], log_ms[:, 0:NF], ALU.subtract)\
                        .then_inc(sem("ln_centred"), 1)

        def ln_lo(kt):
            dve.wait_ge(sem("xh_done"), split_at["ln"] + kt + 1)
            nc.vector.tensor_tensor(u_lo[:, kt, 0:NF], work[:, kt, 0:NF], u_hi[:, kt, 0:NF].bitcast(F32), ALU.subtract)\
                .then_inc(sem("xl_done"), 1)

        for kt in range(KT):
            ln_lo(kt)
        dve.wait_ge(sem("xl_done"), split_at["ln"] + KT)
        for i, k in ph_pw.steps(dve):
            split_lo(ph_pw, i, k)
            p = ph_pw.pair(k)
            dve.wait_ge(unit_done, ph_pw.unit(i, k) + 1)
            nc.vector.tensor_tensor(paired(work)[:, k, :, 0:NF], pair_ap(p, NF), paired(gates)[:, k], ALU.mult)\
                .then_inc(pair_read[p], 1)
            dve.wait_ge(pair_read[p], ph_pw.used_before(i, k) + 1)
            dve.wait_ge(pair_read[ph_wo.pair(k)], ph_wo.used_before(0, k) + 1)
            nc.vector.tensor_tensor(paired(work)[:, k, :, 0:NF], paired(work)[:, k, :, 0:NF], paired(gates)[:, 4 + k], ALU.add)\
                .then_inc(sem("pw_added"), 1)
        for j in range(4):
            dve.wait_ge(sem("xh_done"), split_at["merge"] + 2 * j + 2)
            nc.vector.tensor_tensor(paired(u_lo)[:, j, :, 0:NF], paired(work)[:, j, :, 0:NF], paired(u_hi)[:, j, :, 0:NF].bitcast(F32), ALU.subtract)\
                .then_inc(sem("xl_done"), 2)
        residual_dve(ph_merge, CF)
        norm_dve("ffn2", h_at(CF), ("ffn2", 0), KT, NF, (u_h(NF), u_l(NF)))

        for i, k in ph_ffn2.steps(dve):
            split_lo(ph_ffn2, i, k)
            if k == 2:
                ffn_lo("ffn2", i * 2, 0)
            j, s, p = i * 2 + k // 2, (k // 2) % 2, ph_ffn2.pair(k)
            cv = cva if k % 2 == 0 else cvb
            dve.wait_ge(sem("f2_tap0"), ph_ffn2.unit(i, k) - ph_ffn2.u0 + 1)
            for w in (1, 2):
                for t in range(2):
                    tile = j * 2 + (t + (k % 2) * FT)
                    tap = ffn_dw[:, 0, bass.ds(tile + 2 * FT, 1)] if w == 1 else ffn_dw[:, 1, bass.ds(tile, 1)]
                    a = nc.vector.scalar_tensor_tensor(out=cv[:, s, t, :], in0=ps[:, 2 * p + t, w:w + T1], scalar=tap,
                                                       in1=cv[:, s, t, :], op0=ALU.mult, op1=ALU.add)
                if w == 1:
                    a.then_inc(sem("f2_tap1"), 1)
                    dve.wait_ge(sem("f2_tap1"), ph_ffn2.unit(i, k) - ph_ffn2.u0 + 1)
            a.then_inc(pair_read[p], 1)
            if k % 2:
                dve.wait_ge(sem("f2_silu"), j + 1)
                dve.wait_ge(pair_read[p], ph_ffn2.used_before(i, k) + 1)
                dve.wait_ge(sem("ffn_lo"), j + (FFN["ffn2"] + 1))
                nc.vector.tensor_tensor(act_a[:, s], act_g[:, s], cvb[:, s], ALU.mult).then_inc(sem("f2_mul"), 1)
                if k == 3 or isinstance(i, int) and i == ph_ffn2.turns:
                    ffn_lo("ffn2", j, s)
        residual_dve(ph_down2, C1, group=4)
        norm_dve("final2", h_at(C1), ("final2", 0), KT, T1)
        for half in range(2):
            dve.wait_ge(sem("out_turned"), half + 1)
            nc.vector.tensor_copy(out_rows[:, 1, half * 512:(half + 1) * 512], ps[:, 2 + half, :])\
                .then_inc(sem("out_copied1"), 1)
    ctx.close()


_INS = ["x", "ev_w_in", "ev_g_cq", "ev_w_uq", "ev_g_ckv", "ev_w_ukv", "ev_w_out", "od_w_qkv", "od_rel_bias",
        "od_w_out", "g_mix", "g_ffn", "w_gate", "w_up", "w_down", "g_final", "meta_tokens_2", "mix_norm_g_2",
        "w_in_2", "conv_ln_g_2", "conv_ln_b_2", "conv_dw_w_2", "conv_dw_b_2", "conv_pw_out_2", "attn_w_o_2",
        "w_merge_out_2", "ffn_norm_g_2", "ffn_up_2", "ffn_dw_w_2", "ffn_dw_b_2", "ffn_down_2", "final_norm_g_2"]


def kernel(**inputs):
    import concourse.bacc as bacc
    from concourse.bass_utils import run_bass_kernel_spmd

    nc = bacc.Bacc("TRN2", target_bir_lowering=False, num_devices=1)
    arrays, args = {}, {}
    for name in _INS:
        a = np.ascontiguousarray(inputs[name])
        arrays[f"in_{name}"] = a
        args[name] = nc.dram_tensor(f"in_{name}", a.shape, mybir.dt.from_np(a.dtype), kind="ExternalInput").ap()
    constants, where = shape_constants()
    arrays["in_constants"] = constants
    args["constants"] = nc.dram_tensor("in_constants", constants.shape, F32, kind="ExternalInput").ap()
    args["out"] = nc.dram_tensor("out_0", (1, SEQ, D), F32, kind="ExternalOutput").ap()
    build(nc, where=where, **args)
    r = run_bass_kernel_spmd(nc, [arrays], core_ids=[0])
    return r.results[0]["out_0"]
```
